# Optimizing a Trainium2 kernel written in Bass

```python
import jax, jax.numpy as jnp
from jax import lax
import numpy as np

D_MODEL = 1024
BATCH = 1
SEQ = 2048
DEPTH = 1
DEC_BATCH = 1
DEC_SEQ = 64
PAST_LEN = 512

CHUNK = 64
GLA_HEADS = 4
GLA_DK = 64
GLA_DV = 128
GLA_GATE_RANK = 16
GLA_TAU = 16.0
GLA_W = GLA_HEADS * GLA_DV
GLA_KW = GLA_HEADS * GLA_DK
SB_HEADS = 4
SB_DH = 64
SB_W = SB_HEADS * SB_DH
SB_QBLOCK = 128
SB_KBLOCK = 128
CONV_CH = 256
CONV_W = 3
MIX_W = GLA_W + SB_W + CONV_CH
D_FF = 4 * D_MODEL
LN_EPS = 1e-5
DEEPNORM_ALPHA = (2 * DEPTH) ** 0.25
DEEPNORM_BETA = (8 * DEPTH) ** -0.25
SPLITS = (GLA_KW, GLA_KW, GLA_W, GLA_W, GLA_GATE_RANK, SB_W, SB_W, SB_W, CONV_CH, CONV_CH, CONV_CH)
N_IN = GLA_KW * 2 + GLA_W * 2 + GLA_GATE_RANK + SB_W * 3 + CONV_CH * 3

kernel_name = "hymba_gla_stickbreak_shortconv_deepnorm_step"

def layer_norm(x, g, b):
    xf = x.astype(jnp.float32)
    mu = xf.mean(-1, keepdims=True)
    var = jnp.square(xf - mu).mean(-1, keepdims=True)
    return ((xf - mu) * lax.rsqrt(var + LN_EPS) * g + b).astype(x.dtype)

def split_cols(z):
    outs, idx = [], 0
    for n in SPLITS:
        outs.append(z[..., idx:idx + n])
        idx += n
    return outs

def gla_chunk(S, q, k, v, lg):
    C = q.shape[2]
    b = jnp.cumsum(lg, axis=2)
    causal = jnp.tril(jnp.ones((C, C), dtype=bool))
    diff = b[:, :, :, None, :] - b[:, :, None, :, :]
    decay = jnp.exp(jnp.where(causal[None, None, :, :, None], diff, -jnp.inf))
    att = jnp.einsum('bhtk,bhsk,bhtsk->bhts', q, k, decay)
    o = (jnp.einsum('bhtk,bhkv->bhtv', q * jnp.exp(b), S)
         + jnp.einsum('bhts,bhsv->bhtv', att, v))
    b_last = b[:, :, -1:, :]
    S_new = (jnp.exp(b_last[:, :, 0, :])[..., None] * S
             + jnp.einsum('bhsk,bhsv->bhkv', k * jnp.exp(b_last - b), v))
    return S_new, o

def gla_seq(S0, q, k, v, lg):
    B, T = q.shape[0], q.shape[1]
    C = min(CHUNK, T)
    n = T // C

    def to_blocks(a):
        return a.reshape(B, n, C, a.shape[2], a.shape[3]).transpose(1, 0, 3, 2, 4)

    S_fin, o = lax.scan(lambda S, xs: gla_chunk(S, *xs), S0,
                        (to_blocks(q), to_blocks(k), to_blocks(v), to_blocks(lg)))
    o = o.transpose(1, 0, 3, 2, 4).reshape(B, T, GLA_HEADS, GLA_DV)
    return S_fin, o

def sb_block(q, q_pos, k, v):
    B, Qb, K = q.shape[0], q.shape[1], k.shape[1]
    nb = K // SB_KBLOCK
    k_pos = jnp.arange(K, dtype=jnp.int32)
    z = jnp.einsum('bqhd,bkhd->bhqk', q, k).astype(jnp.float32) * (SB_DH ** -0.5)
    mask = k_pos[None, :] < q_pos[:, None]
    lk = jnp.where(mask, jax.nn.log_sigmoid(-z), 0.0)
    lkb = lk.reshape(B, SB_HEADS, Qb, nb, SB_KBLOCK)
    later = (jnp.arange(SB_KBLOCK)[:, None] > jnp.arange(SB_KBLOCK)[None, :]).astype(jnp.float32)
    after_in = jnp.einsum('bhqnj,js->bhqns', lkb, later, precision=lax.Precision.HIGHEST)
    bsum = lkb.sum(-1)
    suff = bsum.sum(-1, keepdims=True) - jnp.cumsum(bsum, axis=-1)
    after = (after_in + suff[..., None]).reshape(B, SB_HEADS, Qb, K)
    A = jnp.exp(jnp.where(mask, jax.nn.log_sigmoid(z) + after, -jnp.inf))
    return jnp.einsum('bhqk,bkhd->bqhd', A.astype(v.dtype), v)

def sb_attention(q, k, v, past_len):
    B, T = q.shape[0], q.shape[1]
    Qb = min(SB_QBLOCK, T)
    n = T // Qb
    outs = []
    for i in range(n):
        q_pos = past_len + i * Qb + jnp.arange(Qb, dtype=jnp.int32)
        kend = past_len + (i + 1) * Qb
        kpad = -(-kend // SB_KBLOCK) * SB_KBLOCK
        kk, vv = k[:, :kend], v[:, :kend]
        if kpad > kend:
            padw = ((0, 0), (0, kpad - kend), (0, 0), (0, 0))
            kk, vv = jnp.pad(kk, padw), jnp.pad(vv, padw)
        outs.append(sb_block(q[:, i * Qb:(i + 1) * Qb], q_pos, kk, vv))
    return jnp.concatenate(outs, axis=1).reshape(B, T, SB_W)

def short_conv(u, prev, w):
    T = u.shape[1]
    up = jnp.concatenate([prev.astype(u.dtype), u], axis=1)
    y = w[CONV_W - 1] * up[:, CONV_W - 1:CONV_W - 1 + T]
    for i in range(CONV_W - 1):
        y = y + w[i] * up[:, i:i + T]
    return y, up[:, -(CONV_W - 1):]

def token_mixer(x, w_in, w_gate_up, b_gate, gla_norm_g, conv_w, w_out,
                past_k, past_v, S0, conv_prev, past_len):
    B, T, _ = x.shape
    f32 = jnp.float32
    gq, gk, gv, gr, glow, sq, sk, sv, cb, cc, ch = split_cols(x @ w_in)

    def heads(a, h):
        return a.reshape(B, T, h, -1)

    lg = jax.nn.log_sigmoid((glow @ w_gate_up + b_gate).astype(f32)) / GLA_TAU
    S_fin, go = gla_seq(S0.astype(f32),
                        heads(gq, GLA_HEADS).astype(f32) * (GLA_DK ** -0.5),
                        heads(gk, GLA_HEADS).astype(f32),
                        heads(gv, GLA_HEADS).astype(f32),
                        heads(lg, GLA_HEADS))
    go = go * lax.rsqrt(jnp.mean(go * go, axis=-1, keepdims=True) + LN_EPS)
    go = go.reshape(B, T, GLA_W).astype(x.dtype) * gla_norm_g * jax.nn.silu(gr)

    k_new, v_new = heads(sk, SB_HEADS), heads(sv, SB_HEADS)
    if past_k is None:
        k_all, v_all = k_new, v_new
    else:
        k_all = jnp.concatenate([past_k.astype(k_new.dtype), k_new], axis=1)
        v_all = jnp.concatenate([past_v.astype(v_new.dtype), v_new], axis=1)
    so = sb_attention(heads(sq, SB_HEADS), k_all, v_all, past_len)

    cy, conv_state = short_conv(cc * ch, conv_prev, conv_w)
    co = cb * cy

    out = jnp.concatenate([go, so, co], axis=-1) @ w_out
    return out, k_new, v_new, S_fin.astype(x.dtype), conv_state

def setup_inputs(seed: int = 0) -> dict:
    key = jax.random.key(seed)
    ks = jax.random.split(key, 24)

    def nrm(k, shape, s=1.0):
        return jax.random.normal(k, shape, jnp.float32) * s

    return {
        "x_prompt": nrm(ks[0], (BATCH, SEQ, D_MODEL)),
        "x_sample": nrm(ks[1], (DEC_BATCH, DEC_SEQ, D_MODEL)),
        "cache_sb_k": nrm(ks[2], (DEPTH, DEC_BATCH, PAST_LEN, SB_HEADS, SB_DH)),
        "cache_sb_v": nrm(ks[3], (DEPTH, DEC_BATCH, PAST_LEN, SB_HEADS, SB_DH)),
        "state_gla": nrm(ks[4], (DEPTH, DEC_BATCH, GLA_HEADS, GLA_DK, GLA_DV), 2.0),
        "state_conv": nrm(ks[5], (DEPTH, DEC_BATCH, CONV_W - 1, CONV_CH)),
        "ln_in_g": 1.0 + nrm(ks[6], (D_MODEL,), 0.02),
        "ln_in_b": nrm(ks[7], (D_MODEL,), 0.02),
        "w_in": nrm(ks[8], (DEPTH, D_MODEL, N_IN), D_MODEL ** -0.5),
        "w_gate_up": nrm(ks[9], (DEPTH, GLA_GATE_RANK, GLA_KW), GLA_GATE_RANK ** -0.5),
        "b_gate": nrm(ks[10], (DEPTH, GLA_KW), 0.02),
        "gla_norm_g": 1.0 + nrm(ks[11], (DEPTH, GLA_W), 0.02),
        "conv_w": nrm(ks[12], (DEPTH, CONV_W, CONV_CH), CONV_W ** -0.5),
        "w_out": nrm(ks[13], (DEPTH, MIX_W, D_MODEL), MIX_W ** -0.5 * DEEPNORM_BETA),
        "ln1_g": 1.0 + nrm(ks[14], (DEPTH, D_MODEL), 0.02),
        "ln1_b": nrm(ks[15], (DEPTH, D_MODEL), 0.02),
        "w_up": nrm(ks[16], (DEPTH, D_MODEL, D_FF), D_MODEL ** -0.5),
        "w_down": nrm(ks[17], (DEPTH, D_FF, D_MODEL), D_FF ** -0.5 * DEEPNORM_BETA),
        "ln2_g": 1.0 + nrm(ks[18], (DEPTH, D_MODEL), 0.02),
        "ln2_b": nrm(ks[19], (DEPTH, D_MODEL), 0.02),
    }

def reference(x_prompt, x_sample, cache_sb_k, cache_sb_v, state_gla, state_conv,
              ln_in_g, ln_in_b, w_in, w_gate_up, b_gate, gla_norm_g, conv_w, w_out,
              ln1_g, ln1_b, w_up, w_down, ln2_g, ln2_b):

    def trunk(x, c_k, c_v, s_gla, s_conv):
        B = x.shape[0]
        past_len = 0 if c_k is None else c_k.shape[2]
        x = layer_norm(x, ln_in_g, ln_in_b)
        ks_, vs_, gs_, cs_ = [], [], [], []
        for l in range(DEPTH):
            if c_k is None:
                pk, pv = None, None
                S0 = jnp.zeros((B, GLA_HEADS, GLA_DK, GLA_DV), jnp.float32)
                cprev = jnp.zeros((B, CONV_W - 1, CONV_CH), x.dtype)
            else:
                pk, pv, S0, cprev = c_k[l], c_v[l], s_gla[l], s_conv[l]
            mix, kn, vn, Sf, cst = token_mixer(x, w_in[l], w_gate_up[l], b_gate[l], gla_norm_g[l],
                                               conv_w[l], w_out[l], pk, pv, S0, cprev, past_len)
            x = layer_norm(DEEPNORM_ALPHA * x + mix, ln1_g[l], ln1_b[l])
            ff = jnp.square(jax.nn.relu(x @ w_up[l])) @ w_down[l]
            x = layer_norm(DEEPNORM_ALPHA * x + ff, ln2_g[l], ln2_b[l])
            ks_.append(kn); vs_.append(vn); gs_.append(Sf); cs_.append(cst)
        return x, jnp.stack(ks_), jnp.stack(vs_), jnp.stack(gs_), jnp.stack(cs_)

    y_prompt, k_p, v_p, gla_p, conv_p = trunk(x_prompt, None, None, None, None)
    y_sample, k_s, v_s, gla_s, conv_s = trunk(x_sample, cache_sb_k, cache_sb_v, state_gla, state_conv)
    return (y_prompt, y_sample, k_p, v_p, gla_p, conv_p, k_s, v_s, gla_s, conv_s)


_drawn_inputs = setup_inputs


def setup_inputs(seed=0):
    import zlib

    import numpy as np

    out = dict(_drawn_inputs(seed))
    spreads = {}
    factors = {'cache_sb_k': 18.695,
     'b_gate': 6.314,
     'gla_norm_g': 23.69,
     'ln1_g': 2.75,
     'ln1_b': 2.758,
     'ln2_g': 8.42,
     'ln2_b': 8.247,
     'cache_sb_v': 3.32,
     'state_conv': 3.028}
    for name, (base, spread) in spreads.items():
        noise = np.random.default_rng([zlib.crc32(name.encode()), seed]).standard_normal(out[name].shape)
        drawn = base * np.exp(spread * noise) if base else spread * noise
        out[name] = __import__('jax').numpy.asarray(drawn.astype(out[name].dtype))
    for name, factor in factors.items():
        out[name] = (out[name] * factor).astype(out[name].dtype)
    return out
```

```python
from contextlib import ExitStack

import numpy as np
import concourse.bass as bass
import concourse.mybir as mybir

F32 = mybir.dt.float32
F32R = mybir.dt.float32r
I32 = mybir.dt.int32
ALU = mybir.AluOpType
ACT = mybir.ActivationFunctionType

P = 128
D = 1024
KT = D // P
SEQ, DEC, PAST = 2048, 64, 512
T = SEQ + DEC
D_FF = 4 * D
HEADS, DK, DV = 4, 64, 128
CHUNK = 64
RANK = 16
TAU = 16.0
SBH, SBD = 4, 64
CONV_CH = 256
LN_EPS = 1e-5
ALPHA = 2.0 ** 0.25
MASKED = -1e30

C_GQ, C_GK, C_GV, C_GR, C_GL = 0, 256, 512, 1024, 1536
C_SQ, C_SK, C_SV, C_CB, C_CC, C_CH = 1552, 1808, 2064, 2320, 2576, 2832
Z_GQ, Z_GK, Z_GR, Z_GL, Z_SQ, Z_CB, Z_CC, Z_CH, Z_ROWS = 0, 256, 512, 1024, 1040, 1296, 1552, 1808, 2064

GROUPS = [(0, 512), (512, 512), (1024, 512), (1536, 576)]
NMAX = 576


def subtiles(start, n, width):
    return [(o, min(width, n - o)) for o in range(0, n, width)]


TILES = [(t, min(P, T - t)) for t in range(0, T, P)]


class Scope:

    def __init__(self, nc, tag):
        self.nc, self.tag, self.stack, self.semaphores = nc, tag, ExitStack(), []

    def __enter__(self):
        self.stack.__enter__()
        return self

    def __exit__(self, *e):
        self.stack.__exit__(*e)
        if self.semaphores:
            self.nc.clear_and_free_semaphores(self.semaphores)
            self.nc.all_engine_barrier()

    def sb(self, name, shape, dt=F32):
        return self.stack.enter_context(self.nc.sbuf_tensor(f"{self.tag}_{name}", shape, dt))

    def ps(self, name, shape):
        return self.stack.enter_context(self.nc.psum_tensor(f"{self.tag}_{name}", shape, F32))

    def sem(self, name):
        self.semaphores.append(self.nc.alloc_semaphore(f"{self.tag}_{name}"))
        return self.semaphores[-1]

    def sems(self, name, n):
        return [self.sem(f"{name}{i}") for i in range(n)]


class OutputStores:

    def __init__(self, nc):
        self.scope = Scope(nc, "stores")
        self.results = self.scope.sems("results", 4)
        self.states = self.scope.sem("states")
        self.conv_states = self.scope.sem("conv_states")
        self.rows = self.scope.sems("rows", 5)


def load_row_broadcast(eng, dst, row, sem):
    eng.dma_start(dst, row.rearrange("(o d) -> o d", o=1).to_broadcast([P, D])).then_inc(sem, 16)


def split_product(pe, out, lhs_hi, lhs_lo, rhs_hi, rhs_lo, first, last, skip=False):
    pe.matmul(out, lhs_hi, rhs_hi, start=first, stop=False, skip_group_check=skip)
    pe.matmul(out, lhs_lo, rhs_hi, start=False, stop=False, skip_group_check=skip)
    return pe.matmul(out, lhs_hi, rhs_lo, start=False, stop=last, skip_group_check=skip)


def phase_in(nc, x_tile, ln_g, ln_b, w_in, ident_in, xn_dram, zt_dram, token_stores, lasting):
    WW = 528
    chunks = [
        ([(C_GQ, 512)], "F", Z_GQ),
        ([(C_GR, 528)], "F", Z_GR),
        ([(C_GV, 512)], "T", "gv"),
        ([(C_SQ, 256), (C_CB, 256)], "F", Z_SQ),
        ([(C_SK, 512)], "T", "kv"),
        ([(C_CC, 512)], "F", Z_CC),
    ]
    NCH = len(chunks)
    WSTAGE, OUTS, BANKS = 4, 4, 6
    s = Scope(nc, "p1")
    with s:
        ident = s.sb("ident", [P, P])
        g_b = s.sb("g_b", [P, D])
        b_b = s.sb("b_b", [P, D])
        xs = s.sb("xs", [P, 2, D])
        xn = s.sb("xn", [P, 2, D])
        stats = s.sb("stats", [P, 2, 12])
        mv = s.sb("mv", [P, 2, 2])
        rstd = s.sb("rstd", [P, 2, 1])
        eps = s.sb("eps", [P, 1])
        xh = s.sb("xh", [P, 2, KT, NMAX], F32R)
        xl = s.sb("xl", [P, 2, KT, NMAX], F32R)
        wst = s.sb("wst", [P, WSTAGE, WW])
        wh = s.sb("wh", [P, 2, KT, WW], F32R)
        wl = s.sb("wl", [P, 2, KT, WW], F32R)
        outb = s.sb("outb", [P, OUTS, 512])
        ps_t = s.ps("ps_t", [P, 2, 512])
        ps_m = s.ps("ps_m", [P, BANKS, 512])

        consts_in = s.sem("consts_in")
        eps_set = s.sem("eps_set")
        x_in = s.sems("x_in", 2)
        stats_done = s.sem("stats_done")
        var_done = s.sem("var_done")
        std_done = s.sem("std_done")
        rstd_done = s.sem("rstd_done")
        centred = s.sem("centred")
        scaled = s.sem("scaled")
        normed = s.sem("normed")
        xn_out = s.sems("xn_out", 2)
        turned = s.sem("turned")
        xhi_done = s.sem("xhi_done")
        xlo_done = s.sem("xlo_done")
        w_inn = s.sems("w_in", WSTAGE)
        whi_done = s.sem("whi_done")
        wlo_done = s.sem("wlo_done")
        unit_done = s.sem("unit_done")
        evacuated = s.sem("evacuated")
        out_st = lasting.results

        gtiles, n = [], 0
        for (t0, cnt) in GROUPS:
            gtiles.append([(n + i, o, c) for i, (o, c) in enumerate(subtiles(t0, cnt, P))])
            n += len(gtiles[-1])
        units = []
        for g, (t0, cnt) in enumerate(GROUPS):
            for c, (pieces, kind, where) in enumerate(chunks):
                gc = g * NCH + c
                width = sum(w for _, w in pieces)
                if kind == "F":
                    for m0 in range(0, width, P):
                        mw = min(P, width - m0)
                        for o, cc in subtiles(t0, cnt, 512):
                            units.append(dict(g=g, gc=gc, kind="F", m0=m0, mw=mw, o=o, n=cc, t0=t0, row=where + m0))
                else:
                    for o, cc in subtiles(t0, cnt, P):
                        units.append(dict(g=g, gc=gc, kind="T", o=o, n=cc, t0=t0, what=where))
        by_chunk = {}
        for i, u in enumerate(units):
            by_chunk.setdefault(u["gc"], []).append((i, u))
        chunk_end = {gc: us[-1][0] + 1 for gc, us in by_chunk.items()}
        order = [("tile", 0, t) for t in gtiles[0]]
        order.insert(2, ("weights", 0))
        for g in range(len(GROUPS)):
            for c in range(NCH):
                gc = g * NCH + c
                if gc + 1 < NCH * len(GROUPS):
                    order.append(("weights", gc + 1))
                order.append(("product", gc))
                if g + 1 < len(GROUPS) and c < len(gtiles[g + 1]):
                    order.append(("tile", g + 1, gtiles[g + 1][c]))

        block = s.stack.enter_context(nc.Block())

        @block.sync
        def _(sp):
            sp.dma_start(ident[:], ident_in).then_inc(consts_in, 16)
            load_row_broadcast(sp, g_b[:], ln_g, consts_in)
            load_row_broadcast(sp, b_b[:], ln_b, consts_in)
            for what, *a in order:
                if what == "tile":
                    j, o, c = a[1]
                    if j >= 2:
                        sp.wait_ge(centred, j - 1)
                    sp.dma_start(xs[:c, j % 2, :], x_tile(j)).then_inc(x_in[j % 2], 16)
                elif what == "weights":
                    gc = a[0]
                    for k in range(KT):
                        u = gc * KT + k
                        if u >= WSTAGE:
                            sp.wait_ge(wlo_done, u - WSTAGE + 1)
                        slot, at = u % WSTAGE, 0
                        pieces = chunks[gc % NCH][0]
                        for c0, w in pieces:
                            sp.dma_start(wst[:, slot, at:at + w], w_in[k * P:(k + 1) * P, c0:c0 + w]).then_inc(w_inn[slot], 16)
                            at += w

        def n_stores(i):
            return sum(1 if units[j]["kind"] == "F" or units[j]["what"] == "gv" else 2 for j in range(i % OUTS, i + 1, OUTS))

        slot_loads = [0] * WSTAGE
        loads_by_unit = []
        for u in range(NCH * len(GROUPS) * KT):
            slot_loads[u % WSTAGE] += len(chunks[(u // KT) % NCH][0])
            loads_by_unit.append(slot_loads[u % WSTAGE])

        @block.scalar
        def _(act):
            for what, *a in order:
                if what == "tile":
                    g, (j, o, c) = a
                    act.wait_ge(eps_set, 1)
                    act.wait_ge(var_done, j + 1)
                    if j >= 2:
                        act.wait_ge(centred, j - 1)
                    act.activation(rstd[:c, j % 2, :], mv[:c, j % 2, 1:2], ACT.Sqrt, bias=eps[:c, :]).then_inc(std_done, 1)
                    for q in range(2):
                        act.wait_ge(turned, 2 * j + q + 1)
                        if g >= 2 and q == 0:
                            act.wait_ge(unit_done, chunk_end[(g - 1) * NCH - 1])
                        act.activation(xh[:, g % 2, 4 * q:4 * q + 4, o:o + c],
                                       ps_t[:, q, :].rearrange("p (k t) -> p k t", k=4)[:, :, :c],
                                       ACT.Copy).then_inc(xhi_done, 1)
                elif what == "weights":
                    gc = a[0]
                    width = sum(w for _, w in chunks[gc % NCH][0])
                    for k in range(KT):
                        u = gc * KT + k
                        act.wait_ge(w_inn[u % WSTAGE], 16 * loads_by_unit[u])
                        if gc >= 2 and k == 0:
                            act.wait_ge(unit_done, chunk_end[gc - 2])
                        act.activation(wh[:, gc % 2, k, :width], wst[:, u % WSTAGE, :width], ACT.Copy).then_inc(whi_done, 1)
                else:
                    for i, u in by_chunk[a[0]]:
                        act.wait_ge(unit_done, i + 1)
                        if i >= OUTS:
                            act.wait_ge(out_st[i % OUTS], 16 * n_stores(i - OUTS))
                        rows, cols = (u["mw"], u["n"]) if u["kind"] == "F" else (u["n"], 512)
                        act.activation(outb[:rows, i % OUTS, :cols], ps_m[:rows, i % BANKS, :cols], ACT.Copy).then_inc(evacuated, 1)

        @block.vector
        def _(dve):
            dve.memset(eps[:], LN_EPS).then_inc(eps_set, 1)
            for what, *a in order:
                if what == "tile":
                    g, (j, o, c) = a
                    sl = j % 2
                    dve.wait_ge(x_in[sl], 16 * (j // 2 + 1))
                    dve.bn_stats(stats[:c, sl, 0:6], xs[:c, sl, 0:512]).then_inc(stats_done, 1)
                    dve.bn_stats(stats[:c, sl, 6:12], xs[:c, sl, 512:1024]).then_inc(stats_done, 1)
                    dve.wait_ge(stats_done, 2 * j + 2)
                    if j >= 2:
                        dve.wait_ge(std_done, j - 1)
                    dve.bn_aggr(mv[:c, sl, :], stats[:c, sl, :]).then_inc(var_done, 1)
                    dve.wait_ge(std_done, j + 1)
                    dve.reciprocal(rstd[:c, sl, :], rstd[:c, sl, :]).then_inc(rstd_done, 1)
                    dve.wait_ge(rstd_done, j + 1)
                    if j >= 2:
                        dve.wait_ge(xn_out[sl], 16 * (j // 2))
                        dve.wait_ge(turned, 2 * (j - 1))
                    dve.tensor_scalar(xn[:c, sl, :], xs[:c, sl, :], mv[:c, sl, 0:1], rstd[:c, sl, :], ALU.subtract, ALU.mult).then_inc(centred, 1)
                    dve.wait_ge(centred, j + 1)
                    dve.wait_ge(consts_in, 48)
                    dve.tensor_tensor(xn[:c, sl, :], xn[:c, sl, :], g_b[:c, :], ALU.mult).then_inc(scaled, 1)
                    for q in range(2):
                        dve.wait_ge(xhi_done, 2 * j + q + 1)
                        dve.tensor_tensor(xl[:, g % 2, 4 * q:4 * q + 4, o:o + c],
                                          ps_t[:, q, :].rearrange("p (k t) -> p k t", k=4)[:, :, :c],
                                          xh[:, g % 2, 4 * q:4 * q + 4, o:o + c].bitcast(F32), ALU.subtract).then_inc(xlo_done, 1)
                elif what == "weights":
                    gc = a[0]
                    width = sum(w for _, w in chunks[gc % NCH][0])
                    for k in range(KT):
                        u = gc * KT + k
                        dve.wait_ge(whi_done, u + 1)
                        dve.tensor_tensor(wl[:, gc % 2, k, :width], wst[:, u % WSTAGE, :width],
                                          wh[:, gc % 2, k, :width].bitcast(F32), ALU.subtract).then_inc(wlo_done, 1)

        @block.gpsimd
        def _(pool):
            pool.wait_ge(consts_in, 48)
            for what, *a in order:
                if what == "tile":
                    g, (j, o, c) = a
                    pool.wait_ge(scaled, j + 1)
                    pool.tensor_tensor(xn[:c, j % 2, :], xn[:c, j % 2, :], b_b[:c, :], ALU.add).then_inc(normed, 1)
                    pool.wait_ge(normed, j + 1)
                    t = GROUPS[g][0] + o
                    pool.dma_start(xn_dram[t:t + c, :], xn[:c, j % 2, :]).then_inc(xn_out[j % 2], 16)
                elif what == "product":
                    for i, u in by_chunk[a[0]]:
                        pool.wait_ge(evacuated, i + 1)
                        src = outb[:, i % OUTS, :]
                        t = u["t0"] + u["o"]
                        if u["kind"] == "F":
                            pool.dma_start(zt_dram[u["row"]:u["row"] + u["mw"], t:t + u["n"]], src[:u["mw"], :u["n"]]).then_inc(out_st[i % OUTS], 16)
                        else:
                            for dst, c0, c1 in token_stores(u["what"], t, u["n"]):
                                pool.dma_start(dst, src[:u["n"], c0:c1]).then_inc(out_st[i % OUTS], 16)
            for q in range(OUTS):
                last = max(i for i in range(len(units)) if i % OUTS == q)
                pool.wait_ge(out_st[q], 16 * n_stores(last))
            for q in range(2):
                pool.wait_ge(xn_out[q], 16 * len([j for j in range(n) if j % 2 == q]))

        @block.tensor
        def _(pe):
            pe.wait_ge(consts_in, 48)
            for what, *a in order:
                if what == "tile":
                    g, (j, o, c) = a
                    pe.wait_ge(normed, j + 1)
                    for q in range(2):
                        if j >= 1:
                            pe.wait_ge(xlo_done, 2 * (j - 1) + q + 1)
                        for k in range(4):
                            mm = pe.transpose(ps_t[:, q, k * P:k * P + c], xn[:c, j % 2, (4 * q + k) * P:(4 * q + k + 1) * P], ident[:c, :c])
                        mm.then_inc(turned, 1)
                elif what == "product":
                    gc = a[0]
                    g = gc // NCH
                    tiles_by = gtiles[g][-1][0] + 1
                    pe.wait_ge(xlo_done, 2 * tiles_by)
                    pe.wait_ge(wlo_done, KT * (gc + 1))
                    for i, u in by_chunk[gc]:
                        if i >= BANKS:
                            pe.wait_ge(evacuated, i - BANKS + 1)
                        for k in range(KT):
                            tok = slice(u["o"], u["o"] + u["n"])
                            hx, lx = xh[:, g % 2, k, tok], xl[:, g % 2, k, tok]
                            if u["kind"] == "F":
                                col = slice(u["m0"], u["m0"] + u["mw"])
                                mm = split_product(pe, ps_m[:u["mw"], i % BANKS, :u["n"]], wh[:, gc % 2, k, col], wl[:, gc % 2, k, col],
                                                   hx, lx, k == 0, k == KT - 1)
                            else:
                                mm = split_product(pe, ps_m[:u["n"], i % BANKS, :512], hx, lx, wh[:, gc % 2, k, :512], wl[:, gc % 2, k, :512],
                                                   k == 0, k == KT - 1)
                        mm.then_inc(unit_done, 1)


def phase_gla(nc, a, zt_dram, gv_dram, mixt_dram, lasting):
    GG = [(g * 512, 512) for g in range(SEQ // 512)] + [(SEQ, DEC)]
    NG = len(GG)
    NL = len(LEVELS)
    QSCALE = DK ** -0.5
    s = Scope(nc, "p2")
    with s:
        ident, ones = s.sb("ident", [P, P]), s.sb("ones", [P, P])
        masks = s.sb("masks", [P, NL * 64 + P])
        starts = s.sb("starts", [P, 512])
        eps = s.sb("eps", [P, 1])
        wgu = s.sb("wgu", [RANK, 256])
        bg = s.sb("bg", [P, 2])
        gn = s.sb("gn", [P, HEADS])
        cw = s.sb("cw", [P, 2, 3])
        glow = s.sb("glow", [RANK, 2, 512])
        gq, gk = s.sb("gq", [P, 2, 2, 512]), s.sb("gk", [P, 2, 2, 512])
        gr = s.sb("gr", [P, 4, 512])
        gy, ga = s.sb("gy", [P, 2, 512]), s.sb("ga", [P, 2, 512])
        bc = s.sb("bc", [P, 2, 2, 512])
        ex = s.sb("ex", [P, 2, 2, 512])
        xh, xl = s.sb("xh", [P, 2, 2, 512], F32R), s.sb("xl", [P, 2, 2, 512], F32R)
        kdh, kdl = s.sb("kdh", [P, 2, 512], F32R), s.sb("kdl", [P, 2, 512], F32R)
        att = s.sb("att", [P, 4, 4, P])
        ah, al = s.sb("ah", [P, 4, 4, P], F32R), s.sb("al", [P, 4, 4, P], F32R)
        eb = s.sb("eb", [P, 2, 2, 512])
        qs = s.sb("qs", [P, 2, 512])
        qsh, qsl = s.sb("qsh", [P, 2, 2, 512], F32R), s.sb("qsl", [P, 2, 2, 512], F32R)
        ksf = s.sb("ksf", [P, 2, 2, 512])
        gg = s.sb("gg", [P, 2, 4, 512])
        v = s.sb("v", [P, 2, 512])
        vh, vl = s.sb("vh", [P, 2, 512], F32R), s.sb("vl", [P, 2, 512], F32R)
        kth, ktl = s.sb("kth", [P, 2, 256], F32R), s.sb("ktl", [P, 2, 256], F32R)
        st = s.sb("st", [P, 2, 2, P])
        sh, sl = s.sb("sh", [P, 2, 2, P], F32R), s.sb("sl", [P, 2, 2, P], F32R)
        sq, rn = s.sb("sq", [P, 512]), s.sb("rn", [P, 512])
        on = s.sb("on", [P, 2, 4, P])
        cb, cc, ch = s.sb("cb", [P, 512]), s.sb("cc", [P, 2, 512]), s.sb("ch", [P, 512])
        cu, ctmp = s.sb("cu", [P, 2, 514]), s.sb("ctmp", [P, 512])
        cy = s.sb("cy", [P, 2, 512])
        ps_g = s.ps("ps_g", [P, 512])
        ps_l = s.ps("ps_l", [P, 2, 512])
        ps_k = s.ps("ps_k", [P, 512])
        ps_s = s.ps("ps_s", [P, 2, 512])
        ps_o = s.ps("ps_o", [P, 2, 512])

        S = s.sem
        consts_in, consts_set = S("consts_in"), S("consts_set")
        group_in, gr_in = s.sems("group_in", 2), S("gr_in")
        v_in = s.sems("v_in", 2)
        st_in, st_out = S("st_in"), lasting.states
        gate_mm, gate_y, gate_negabs, gate_exp, gate_ln, gate_l, cum_done = (S(n) for n in (
            "gate_mm", "gate_y", "gate_negabs", "gate_exp", "gate_ln", "gate_l", "cum_done"))
        eb_done, qs_done, qs_hi, qs_lo = S("eb_done"), S("qs_done"), S("qs_hi"), S("qs_lo")
        ks_arg, ks_exp, ks_done = S("ks_arg"), S("ks_exp"), S("ks_done")
        r_exp, r_one, r_inv, gg_done = S("r_exp"), S("r_one"), S("r_inv"), S("gg_done")
        lev_arg, lev_exp, lev_mul, lev_hi, lev_lo, lev_mm, lev_put = (S(n) for n in (
            "lev_arg", "lev_exp", "lev_mul", "lev_hi", "lev_lo", "lev_mm", "lev_put"))
        att_hi, att_lo = S("att_hi"), S("att_lo")
        v_hi, v_lo, k_turned, k_hi, k_lo = S("v_hi"), S("v_lo"), S("k_turned"), S("k_hi"), S("k_lo")
        kv_mm, st_new, st_hi, st_lo = S("kv_mm"), S("st_new"), S("st_hi"), S("st_lo")
        inter_done, intra_done = S("inter_done"), S("intra_done")
        o_mm, sq_done, n_mm, n_ln, n_exp, o_norm, o_gate = (S(n) for n in (
            "o_mm", "sq_done", "n_mm", "n_ln", "n_exp", "o_norm", "o_gate"))
        on_st = s.sems("on_st", 2)
        c_in, c_u, c_y, c_out = s.sems("c_in", 3), S("c_u"), S("c_y"), s.sems("c_out", 2)
        cs_out = lasting.conv_states

        def level_blocks(g):
            nt = max(1, GG[g][1] // P)
            found = [(li, list(range(nt))) for li in range(NL)]
            return found + [(NL, list(range(x, min(nt, x + 2)))) for x in range(0, nt, 2)]

        order = [("group", 0)] + [("level", 0, li) for li in range(NL + 1)] + [("split", 0)]
        tiles, chunks = [], []
        for g, (t0, n) in enumerate(GG):
            nt = max(1, n // P)
            lv = [("level", g + 1, li) for li in range(NL + 1)] if g + 1 < NG else []
            if lv:
                order.append(("group", g + 1))
            for i in range(nt):
                m = min(P, n)
                cs = list(range(len(chunks), len(chunks) + m // CHUNK))
                chunks += [(len(tiles), x) for x in range(m // CHUNK)]
                tiles.append((g, i, m, cs))
                order.append(("tile", len(tiles) - 1))
                order += lv[:2]
                lv = lv[2:]
            order += lv
            if g + 1 < NG:
                order.append(("split", g + 1))
        FIRST_STREAM = len(chunks) - 1
        inter_no, k = {}, 0
        for c, (ct, cx) in enumerate(chunks):
            if cx != len(tiles[ct][3]) - 1:
                k += 1
                inter_no[c] = k

        bank_no, put_by_group, n_b = {}, {}, 0
        for it in order:
            if it[0] == "level":
                _, g, li = it
                for b in level_blocks(g):
                    if b[0] == li:
                        bank_no[(g, b[0], b[1][0])] = n_b
                        n_b += 1
                put_by_group[g] = 2 * n_b
        group_tiles = [[n for n, t in enumerate(tiles) if t[0] == g] for g in range(NG)]
        tiles_before = [group_tiles[g][0] for g in range(NG)]
        lev_no = {(it[1], it[2]): n for n, it in enumerate([x for x in order if x[0] == "level"])}
        last_bank = {}
        for (g, li, t), b in bank_no.items():
            last_bank[(g, li)] = max(last_bank.get((g, li), 0), 2 * (b + 1))
        lev_by_no = {n: k for k, n in lev_no.items()}

        def halves(x, g, hs, n):
            y = x[:, :, :n].rearrange("p a (b two h) -> p a b two h", two=2, h=hs)
            return y[:, :, :, 0, :], y[:, :, :, 1, :]

        block = s.stack.enter_context(nc.Block())

        def store_tile(sp, j):
            g, i, m, cs = tiles[j]
            t = GG[g][0] + i * P
            sp.wait_ge(o_gate, j + 1)
            sp.dma_start(mixt_dram[0:512, t:t + m].rearrange("(h p) t -> p h t", p=P), on[:, j % 2, :, :m]).then_inc(on_st[j % 2], 16)

        @block.sync
        def _(sp):
            for dst, src in ((ident[:], a["ident"]), (ones[:], a["ones"]), (masks[:], a["level_masks"]),
                             (starts[:], a["chunk_start"][:, :512]), (wgu[:], a["w_gate_up"][0])):
                sp.dma_start(dst, src).then_inc(consts_in, 16)
            with nc.allow_non_contiguous_dma(reason="a few vectors by partition"):
                sp.dma_start(bg[:], a["b_gate"][0].rearrange("(a p) -> p a", p=P)).then_inc(consts_in, 16)
                sp.dma_start(gn[:], a["gla_norm_g"][0].rearrange("(a p) -> p a", p=P)).then_inc(consts_in, 16)
                for x in range(2):
                    sp.dma_start(cw[:, x, :], a["conv_w"][0][:, P * x:P * x + P].rearrange("w p -> p w")).then_inc(consts_in, 16)
            sp.dma_start(st[:, 1, :, :], a["state_gla"][0, 0].rearrange("(a two) k v -> (two k) a v", two=2)).then_inc(st_in, 16)
            for it in order:
                if it[0] == "group":
                    g = it[1]
                    t0, n = GG[g]
                    sl_ = g % 2
                    if g >= 2:
                        sp.wait_ge(ks_done, g - 1)
                        sp.wait_ge(lev_lo, lev_no[(g - 2, NL)] + 1)
                        sp.wait_ge(qs_done, g - 1)
                        sp.wait_ge(gate_mm, 2 * (g - 1))
                    sp.dma_start(glow[:, sl_, :n], zt_dram[Z_GL:Z_GL + RANK, t0:t0 + n]).then_inc(group_in[sl_], 16)
                    sp.dma_start(gq[:, sl_, :, :n], zt_dram[Z_GQ:Z_GQ + 256, t0:t0 + n].rearrange("(a p) t -> p a t", p=P)).then_inc(group_in[sl_], 16)
                    sp.dma_start(gk[:, sl_, :, :n], zt_dram[Z_GK:Z_GK + 256, t0:t0 + n].rearrange("(a p) t -> p a t", p=P)).then_inc(group_in[sl_], 16)
                    if g >= 1:
                        sp.wait_ge(gg_done, g)
                    sp.dma_start(gr[:, :, :n], zt_dram[Z_GR:Z_GR + 512, t0:t0 + n].rearrange("(a p) t -> p a t", p=P)).then_inc(gr_in, 16)
                elif it[0] == "tile":
                    j = it[1]
                    g, i, m, cs = tiles[j]
                    t = GG[g][0] + i * P
                    if j >= 2:
                        sp.wait_ge(v_lo, j - 1)
                    sp.dma_start(v[:m, j % 2, :], gv_dram[t:t + m, :]).then_inc(v_in[j % 2], 16)
                    if j >= 1:
                        store_tile(sp, j - 1)
            store_tile(sp, len(tiles) - 1)
            sp.wait_ge(st_new, len(chunks))
            sp.dma_start(a["gla_state_p"][0, 0].rearrange("(a two) k v -> (two k) a v", two=2), st[:, 0, :, :]).then_inc(st_out, 16)
            sp.dma_start(a["gla_state_s"][0, 0].rearrange("(a two) k v -> (two k) a v", two=2), st[:, 1, :, :]).then_inc(st_out, 16)
            sp.wait_ge(st_out, 32)
            for q in range(2):
                sp.wait_ge(on_st[q], 16 * len([j for j in range(len(tiles)) if j % 2 == q]))

        @block.scalar
        def _(act):
            act.preload_act_table_set("natural_log_exp_and_others")
            act.wait_ge(consts_set, 2)
            act.activation(sh[:, 0, :, :], st[:, 0, :, :], ACT.Copy).then_inc(st_hi, 1)
            for it in order:
                if it[0] == "group":
                    g = it[1]
                    t0, n = GG[g]
                    q = g % 2
                    act.wait_ge(gate_negabs, g + 1)
                    act.activation(ga[:, :, :n], ga[:, :, :n], ACT.Exp).then_inc(gate_exp, 1)
                    act.wait_ge(gate_exp, g + 1)
                    act.activation(ga[:, :, :n], ga[:, :, :n], ACT.Ln, bias=1.0).then_inc(gate_ln, 1)
                    act.wait_ge(gr_in, 16 * (g + 1))
                    if g >= 2:
                        act.wait_ge(o_gate, tiles_before[g - 1])
                    act.activation(gg[:, q, :, :n], gr[:, :, :n], ACT.Exp, scale=-1.0).then_inc(r_exp, 1)
                    act.wait_ge(cum_done, 2 * (g + 1))
                    if g >= 2:
                        act.wait_ge(st_new, tiles[tiles_before[g - 1]][3][0])
                    act.activation(eb[:, q, :, :n], bc[:, q, :, :n], ACT.Exp, scale=1.0 / TAU).then_inc(eb_done, 1)
                    act.wait_ge(ks_arg, g + 1)
                    act.activation(ksf[:, q, :, :n], ksf[:, q, :, :n], ACT.Exp, scale=1.0 / TAU).then_inc(ks_exp, 1)
                    act.wait_ge(qs_done, g + 1)
                    if g >= 2:
                        act.wait_ge(o_mm, tiles_before[g - 1])
                    act.activation(qsh[:, q, :, :n], qs[:, :, :n], ACT.Copy).then_inc(qs_hi, 1)
                elif it[0] == "level":
                    _, g, li = it
                    n, x = GG[g][1], lev_no[(g, li)]
                    if x >= 2:
                        act.wait_ge(lev_mm, last_bank[lev_by_no[x - 2]])
                    if li < NL:
                        act.wait_ge(lev_arg, 2 * (x + 1))
                        act.activation(ex[:, x % 2, :, :n], ex[:, x % 2, :, :n], ACT.Exp, scale=1.0 / TAU).then_inc(lev_exp, 1)
                        act.wait_ge(lev_mul, 2 * (x + 1))
                        act.activation(xh[:, x % 2, :, :n], ex[:, x % 2, :, :n], ACT.Copy).then_inc(lev_hi, 1)
                    else:
                        act.wait_ge(lev_arg, 2 * (x + 1))
                        act.activation(xh[:, x % 2, :, :n], gq[:, g % 2, :, :n], ACT.Copy).then_inc(lev_exp, 1)
                        if g:
                            act.wait_ge(lev_mm, last_bank[(g - 1, NL)])
                        act.activation(kdh[:, :, :n], gk[:, g % 2, :, :n], ACT.Copy).then_inc(lev_hi, 1)
                elif it[0] == "split":
                    g = it[1]
                    n = GG[g][1]
                    act.wait_ge(lev_put, put_by_group[g])
                    if g:
                        act.wait_ge(o_mm, tiles_before[g])
                    w = min(P, n)
                    nt = max(1, n // P)
                    act.activation(ah[:w, :nt, :, :w], att[:w, :nt, :, :w], ACT.Copy, scale=QSCALE).then_inc(att_hi, 1)
                else:
                    j = it[1]
                    g, i, m, cs = tiles[j]
                    act.wait_ge(v_in[j % 2], 16 * (j // 2 + 1))
                    if j >= 2:
                        act.wait_ge(o_mm, j - 1)
                    act.activation(vh[:m, j % 2, :], v[:m, j % 2, :], ACT.Copy).then_inc(v_hi, 1)
                    act.wait_ge(k_turned, j + 1)
                    act.activation(kth[:m, j % 2, :], ps_k[:m, 0:256], ACT.Copy).then_inc(k_hi, 1)
                    for c in cs:
                        act.wait_ge(st_new, c + 1)
                        if c + 1 < len(chunks):
                            if c >= 1:
                                ct, cx = chunks[c - 1]
                                if cx == len(tiles[ct][3]) - 1:
                                    act.wait_ge(o_mm, ct + 1)
                                else:
                                    act.wait_ge(inter_done, inter_no[c - 1])
                            src = st[:, 1 if c + 1 == FIRST_STREAM else 0, :, :]
                            if c + 1 == FIRST_STREAM:
                                act.wait_ge(st_in, 16)
                            act.activation(sh[:, (c + 1) % 2, :, :], src, ACT.Copy).then_inc(st_hi, 1)
                    act.wait_ge(o_mm, j + 1)
                    if j:
                        act.wait_ge(n_mm, j)
                    act.activation(sq[:, :4 * m].rearrange("p (e x) -> p e x", e=2), ps_o[:, :, :2 * m], ACT.Square).then_inc(sq_done, 1)
                    act.wait_ge(n_mm, j + 1)
                    if j:
                        act.wait_ge(o_norm, 2 * j)
                    act.activation(rn[:, :4 * m], ps_g[:, :4 * m], ACT.Ln, scale=1.0 / DV, bias=eps[:, :]).then_inc(n_ln, 1)
                    act.wait_ge(n_ln, j + 1)
                    act.activation(rn[:, :4 * m], rn[:, :4 * m], ACT.Exp, scale=-0.5).then_inc(n_exp, 1)

        @block.vector
        def _(dve):
            dve.memset(eps[:], LN_EPS).then_inc(consts_set, 1)
            dve.memset(st[:, 0, :, :], 0.0).then_inc(consts_set, 1)
            dve.memset(att[:], 0.0).then_inc(consts_set, 1)
            dve.wait_ge(consts_set, 3)
            dve.wait_ge(consts_in, 144)
            dve.wait_ge(st_hi, 1)
            dve.tensor_tensor(sl[:, 0, :, :], st[:, 0, :, :], sh[:, 0, :, :].bitcast(F32), ALU.subtract).then_inc(st_lo, 1)
            for it in order:
                if it[0] == "group":
                    g = it[1]
                    t0, n = GG[g]
                    q = g % 2
                    for p in range(2):
                        dve.wait_ge(gate_mm, 2 * g + p + 1)
                        dve.tensor_scalar(gy[:, p, :n], ps_g[:, :n], bg[:, p:p + 1], None, ALU.add).then_inc(gate_y, 1)
                    dve.wait_ge(gate_y, 2 * g + 2)
                    dve.scalar_tensor_tensor(out=ga[:, :, :n], in0=gy[:, :, :n], scalar=-1.0, in1=gy[:, :, :n], op0=ALU.mult, op1=ALU.min)\
                       .then_inc(gate_negabs, 1)
                    dve.wait_ge(gate_ln, g + 1)
                    dve.scalar_tensor_tensor(out=gy[:, :, :n], in0=gy[:, :, :n], scalar=0.0, in1=ga[:, :, :n], op0=ALU.min, op1=ALU.subtract)\
                       .then_inc(gate_l, 1)
                    dve.wait_ge(gate_l, g + 1)
                    for p in range(2):
                        dve.tensor_tensor_scan(bc[:, q, p, :n], starts[:, :n], gy[:, p, :n], 0.0, ALU.mult, ALU.add).then_inc(cum_done, 1)
                    dve.wait_ge(cum_done, 2 * g + 2)
                    b4 = bc[:, q, :, :n].rearrange("p a (c t) -> p a c t", t=CHUNK)
                    k4 = ksf[:, q, :, :n].rearrange("p a (c t) -> p a c t", t=CHUNK)
                    if g >= 2:
                        dve.wait_ge(k_turned, tiles_before[g - 1])
                    dve.tensor_tensor(k4, b4[:, :, :, CHUNK - 1:CHUNK].to_broadcast([P, 2, n // CHUNK, CHUNK]), b4, ALU.subtract).then_inc(ks_arg, 1)
                    dve.wait_ge(r_exp, g + 1)
                    dve.tensor_scalar(gg[:, q, :, :n], gg[:, q, :, :n], 1.0, None, ALU.add).then_inc(r_one, 1)
                    dve.wait_ge(r_one, g + 1)
                    dve.reciprocal(gg[:, q, :, :n], gg[:, q, :, :n]).then_inc(r_inv, 1)
                    dve.wait_ge(eb_done, g + 1)
                    if g:
                        dve.wait_ge(qs_lo, g)
                    dve.wait_ge(group_in[q], 48 * (g // 2 + 1))
                    dve.scalar_tensor_tensor(out=qs[:, :, :n], in0=eb[:, q, :, :n], scalar=QSCALE, in1=gq[:, q, :, :n], op0=ALU.mult, op1=ALU.mult)\
                       .then_inc(qs_done, 1)
                    dve.wait_ge(ks_exp, g + 1)
                    dve.tensor_tensor(ksf[:, q, :, :n], ksf[:, q, :, :n], gk[:, q, :, :n], ALU.mult).then_inc(ks_done, 1)
                    dve.wait_ge(r_inv, g + 1)
                    for h in range(HEADS):
                        last = dve.scalar_tensor_tensor(out=gg[:, q, h, :n], in0=gr[:, h, :n], scalar=gn[:, h:h + 1], in1=gg[:, q, h, :n],
                                                        op0=ALU.mult, op1=ALU.mult)
                    last.then_inc(gg_done, 1)
                    dve.wait_ge(qs_hi, g + 1)
                    dve.tensor_tensor(qsl[:, q, :, :n], qs[:, :, :n], qsh[:, q, :, :n].bitcast(F32), ALU.subtract).then_inc(qs_lo, 1)
                elif it[0] == "level":
                    _, g, li = it
                    n, x, q = GG[g][1], lev_no[(g, li)], g % 2
                    if li < NL:
                        hs = LEVELS[li]
                        nb = n // (2 * hs)
                        b1, b2 = halves(bc[:, q], g, hs, n)
                        e1, e2 = halves(ex[:, x % 2], g, hs, n)
                        cut = b1[:, :, :, hs - 1:hs].to_broadcast([P, 2, nb, hs])
                        dve.wait_ge(lev_lo, x) if x else None
                        dve.tensor_tensor(e1, cut, b1, ALU.subtract).then_inc(lev_arg, 1)
                        dve.tensor_tensor(e2, b2, cut, ALU.subtract).then_inc(lev_arg, 1)
                        dve.wait_ge(lev_exp, x + 1)
                        k1, _k2 = halves(gk[:, q], g, hs, n)
                        _q1, q2 = halves(gq[:, q], g, hs, n)
                        dve.tensor_tensor(e1, e1, k1, ALU.mult).then_inc(lev_mul, 1)
                        dve.tensor_tensor(e2, e2, q2, ALU.mult).then_inc(lev_mul, 1)
                        dve.wait_ge(lev_hi, x + 1)
                        dve.tensor_tensor(xl[:, x % 2, :, :n], ex[:, x % 2, :, :n], xh[:, x % 2, :, :n].bitcast(F32), ALU.subtract).then_inc(lev_lo, 1)
                    else:
                        dve.engine_nop().then_inc(lev_arg, 1)
                        dve.engine_nop().then_inc(lev_arg, 1)
                        dve.engine_nop().then_inc(lev_mul, 1)
                        dve.wait_ge(lev_exp, x + 1)
                        dve.tensor_tensor(xl[:, x % 2, :, :n], gq[:, q, :, :n], xh[:, x % 2, :, :n].bitcast(F32), ALU.subtract).then_inc(lev_mul, 1)
                        dve.wait_ge(lev_hi, x + 1)
                        dve.tensor_tensor(kdl[:, :, :n], gk[:, q, :, :n], kdh[:, :, :n].bitcast(F32), ALU.subtract).then_inc(lev_lo, 1)
                    if g and li == 0:
                        dve.wait_ge(att_lo, g)
                    for (lj, ts) in level_blocks(g):
                        if lj != li:
                            continue
                        b, w, nt = bank_no[(g, li, ts[0])], min(P, n), len(ts)
                        for e in range(2):
                            dve.wait_ge(lev_mm, 2 * b + e + 1)
                            dst = att[:w, ts[0]:ts[0] + nt, e::2, :w].rearrange("p a h t -> p (a h) t")
                            if li < NL:
                                hs, wo = LEVELS[li], w // 2
                                nb = w // (2 * hs)
                                for_pairs = dst.rearrange("p x (b two h) -> p x b two h", two=2, h=hs)[:, :, :, 1, :]
                                data = ps_l[:w, e, :2 * nt * wo].rearrange("p (x b h) -> p x b h", x=2 * nt, h=hs)
                                mk = masks[:w, 64 * li:64 * li + wo].bitcast(I32).rearrange("p (b h) -> p b h", h=hs).unsqueeze(1).to_broadcast([w, 2 * nt, nb, hs])
                            else:
                                for_pairs = dst
                                data = ps_l[:w, e, :2 * nt * w].rearrange("p (x t) -> p x t", x=2 * nt)
                                mk = masks[:w, 64 * NL:64 * NL + w].bitcast(I32).unsqueeze(1).to_broadcast([w, 2 * nt, w])
                            dve.copy_predicated(for_pairs, mk, data).then_inc(lev_put, 1)
                elif it[0] == "split":
                    g = it[1]
                    n = GG[g][1]
                    w, nt = min(P, n), max(1, n // P)
                    dve.wait_ge(att_hi, g + 1)
                    dve.wait_ge(lev_put, put_by_group[g])
                    for i in range(nt):
                        ins = dve.scalar_tensor_tensor(out=al[:w, i, :, :w], in0=att[:w, i, :, :w], scalar=QSCALE, in1=ah[:w, i, :, :w].bitcast(F32),
                                                       op0=ALU.mult, op1=ALU.subtract)
                    ins.then_inc(att_lo, 1)
                else:
                    j = it[1]
                    g, i, m, cs = tiles[j]
                    q = g % 2
                    dve.wait_ge(v_hi, j + 1)
                    dve.tensor_tensor(vl[:m, j % 2, :], v[:m, j % 2, :], vh[:m, j % 2, :].bitcast(F32), ALU.subtract).then_inc(v_lo, 1)
                    dve.wait_ge(k_hi, j + 1)
                    dve.tensor_tensor(ktl[:m, j % 2, :], ps_k[:m, 0:256], kth[:m, j % 2, :].bitcast(F32), ALU.subtract).then_inc(k_lo, 1)
                    for x, c in enumerate(cs):
                        end = i * P + x * CHUNK + CHUNK - 1
                        which = 1 if c == FIRST_STREAM else 0
                        dve.wait_ge(kv_mm, c + 1)
                        if c == FIRST_STREAM:
                            dve.wait_ge(st_in, 16)
                        dve.wait_ge(st_hi, c + 1)
                        dve.wait_ge(st_lo, c + 1)
                        for p in range(2):
                            for e in range(2):
                                r = slice(64 * e, 64 * e + 64)
                                ins = dve.scalar_tensor_tensor(out=st[r, which, p, :], in0=st[r, which, p, :], scalar=eb[r, q, p, end:end + 1],
                                                               in1=ps_s[r, c % 2, 256 * p + P * e:256 * p + P * e + P], op0=ALU.mult, op1=ALU.add)
                        ins.then_inc(st_new, 1)
                        if c + 1 < len(chunks):
                            dve.wait_ge(st_hi, c + 2)
                            src = st[:, 1 if c + 1 == FIRST_STREAM else 0, :, :]
                            dve.tensor_tensor(sl[:, (c + 1) % 2, :, :], src, sh[:, (c + 1) % 2, :, :].bitcast(F32), ALU.subtract).then_inc(st_lo, 1)
                    dve.wait_ge(n_exp, j + 1)
                    if j >= 2:
                        dve.wait_ge(on_st[j % 2], 16 * (j // 2))
                    for e in range(2):
                        dve.tensor_tensor(on[:, j % 2, e::2, :m], ps_o[:, e, :2 * m].rearrange("p (a t) -> p a t", a=2),
                                          rn[:, 2 * m * e:2 * m * e + 2 * m].rearrange("p (a t) -> p a t", a=2), ALU.mult).then_inc(o_norm, 1)
                    dve.wait_ge(o_norm, 2 * j + 2)
                    dve.tensor_tensor(on[:, j % 2, :, :m], on[:, j % 2, :, :m], gg[:, q, :, i * P:i * P + m], ALU.mult).then_inc(o_gate, 1)

        @block.tensor
        def _(pe):
            pe.wait_ge(consts_in, 144)
            tiles_seen = 0
            for it in order:
                if it[0] == "group":
                    g = it[1]
                    t0, n = GG[g]
                    pe.wait_ge(group_in[g % 2], 48 * (g // 2 + 1))
                    for p in range(2):
                        if 2 * g + p:
                            pe.wait_ge(gate_y, 2 * g + p)
                        if tiles_seen:
                            pe.wait_ge(n_ln, tiles_seen)
                        pe.matmul(ps_g[:, :n], wgu[:, P * p:P * p + P], glow[:, g % 2, :n], start=True, stop=True).then_inc(gate_mm, 1)
                elif it[0] == "level":
                    _, g, li = it
                    x = lev_no[(g, li)]
                    w = min(P, GG[g][1])
                    pe.wait_ge(lev_lo, x + 1)
                    if li == NL:
                        pe.wait_ge(lev_mul, 2 * (x + 1))
                    for (lj, ts) in level_blocks(g):
                        if lj != li:
                            continue
                        b = bank_no[(g, li, ts[0])]
                        for e in range(2):
                            if b:
                                pe.wait_ge(lev_put, 2 * b - 1 + e)
                            n = 0
                            r = slice(64 * e, 64 * e + 64)
                            for t in ts:
                                cols = slice(t * P, t * P + w)
                                for pr in range(2):
                                    if li < NL:
                                        hs, wo = LEVELS[li], w // 2

                                        def second(y):
                                            return y[r, x % 2, pr, cols].rearrange("p (b two h) -> p b two h", two=2, h=hs)[:, :, 1, :]
                                        args = (xh[r, x % 2, pr, cols], xl[r, x % 2, pr, cols], second(xh), second(xl))
                                    else:
                                        wo = w
                                        args = (kdh[r, pr, cols], kdl[r, pr, cols], xh[r, x % 2, pr, cols], xl[r, x % 2, pr, cols])
                                    mm = split_product(pe, ps_l[:w, e, n * wo:n * wo + wo], *args, n == 0, n == 2 * len(ts) - 1, skip=True)
                                    n += 1
                            mm.then_inc(lev_mm, 1)
                elif it[0] == "tile":
                    j = it[1]
                    g, i, m, cs = tiles[j]
                    q = g % 2
                    pe.wait_ge(ks_done, g + 1)
                    if j:
                        pe.wait_ge(k_lo, j)
                    for p in range(2):
                        mm = pe.transpose(ps_k[:m, P * p:P * p + P], ksf[:, q, p, i * P:i * P + m], ident[:, :])
                    mm.then_inc(k_turned, 1)
                    pe.wait_ge(v_lo, j + 1)
                    pe.wait_ge(att_lo, g + 1)
                    pe.wait_ge(qs_lo, g + 1)
                    if j:
                        pe.wait_ge(o_norm, 2 * j)
                    for h in range(HEADS):
                        hc = slice(P * h, P * h + P)
                        mm = split_product(pe, ps_o[:, h % 2, (h // 2) * m:(h // 2) * m + m], vh[:m, j % 2, hc], vl[:m, j % 2, hc], ah[:m, i, h, :m], al[:m, i, h, :m],
                                      h < 2, False, skip=True)
                    if m == 64:
                        mm.then_inc(intra_done, 1)
                        pe.wait_ge(intra_done, 1)
                    pe.wait_ge(k_lo, j + 1)
                    for x, c in enumerate(cs):
                        r = slice(64 * x, 64 * x + 64)
                        if c >= 2:
                            pe.wait_ge(st_new, c - 1)
                        for p in range(2):
                            mm = split_product(pe, ps_s[:, c % 2, 256 * p:256 * p + 256], kth[r, j % 2, P * p:P * p + P], ktl[r, j % 2, P * p:P * p + P],
                                               vh[r, j % 2, 256 * p:256 * p + 256], vl[r, j % 2, 256 * p:256 * p + 256], p == 0, p == 1, skip=True)
                        mm.then_inc(kv_mm, 1)
                    for x, c in enumerate(cs):
                        pe.wait_ge(st_lo, c + 1)
                        cols = slice(i * P + x * CHUNK, i * P + x * CHUNK + CHUNK)
                        for h in (0, 2, 1, 3):
                            hr, pr = slice(64 * (h % 2), 64 * (h % 2) + 64), h // 2
                            last = x == len(cs) - 1 and h == HEADS - 1
                            mm = split_product(pe, ps_o[:, h % 2, pr * m + x * CHUNK:pr * m + x * CHUNK + CHUNK], sh[hr, c % 2, pr, :], sl[hr, c % 2, pr, :],
                                               qsh[hr, q, pr, cols], qsl[hr, q, pr, cols], False, x == len(cs) - 1 and pr == 1, skip=True)
                        mm.then_inc(o_mm if last else inter_done, 1)
                    tiles_seen = j + 1
                    pe.wait_ge(sq_done, j + 1)
                    pe.wait_ge(gate_y, 2 * min(g + 2, NG))
                    if j:
                        pe.wait_ge(n_ln, j)
                    pe.matmul(ps_g[:, :4 * m], ones[:, :], sq[:, :4 * m], start=True, stop=True).then_inc(n_mm, 1)

        pieces = [(x, t, n) for x in range(2) for t, n in GG]

        @block.gpsimd
        def _(pool):
            pool.wait_ge(consts_in, 144)
            for k, (x, t, n) in enumerate(pieces):
                first, sl_, cp = t in (0, SEQ), k % 2, P * x
                with nc.allow_non_contiguous_dma(reason="two columns of state"):
                    pool.dma_start(cc[:, sl_, :n], zt_dram[Z_CC + cp:Z_CC + cp + P, t:t + n]).then_inc(c_in[0], 16)
                    pool.dma_start(ch[:, :n], zt_dram[Z_CH + cp:Z_CH + cp + P, t:t + n]).then_inc(c_in[0], 16)
                    pool.dma_start(cb[:, :n], zt_dram[Z_CB + cp:Z_CB + cp + P, t:t + n]).then_inc(c_in[0], 16)
                    if t == SEQ:
                        pool.dma_start(cu[:, sl_, 0:2], a["state_conv"][0, 0][:, cp:cp + P].rearrange("w p -> p w")).then_inc(c_in[1], 16)
                        pool.wait_ge(c_in[1], 16 * (x + 1))
                pool.wait_ge(c_in[0], 48 * (k + 1))
                u = cu[:, sl_, :]
                if t == 0:
                    pool.memset(u[:, 0:2], 0.0).then_inc(c_u, 1)
                elif t != SEQ:
                    pool.tensor_copy(u[:, 0:2], cu[:, 1 - sl_, 512:514]).then_inc(c_u, 1)
                else:
                    pool.engine_nop().then_inc(c_u, 1)
                pool.tensor_tensor(u[:, 2:2 + n], cc[:, sl_, :n], ch[:, :n], ALU.mult).then_inc(c_u, 1)
                pool.wait_ge(c_u, 2 * (k + 1))
                y = cy[:, sl_, :n]
                if k >= 2:
                    pool.wait_ge(c_out[sl_], 16 * (k // 2))
                tmp = ctmp[:, :n]
                steps = [
                    lambda: pool.tensor_scalar(y, u[:, 2:2 + n], cw[:, x, 2:3], None, ALU.mult),
                    lambda: pool.tensor_scalar(tmp, u[:, 0:n], cw[:, x, 0:1], None, ALU.mult),
                    lambda: pool.tensor_tensor(y, y, tmp, ALU.add),
                    lambda: pool.tensor_scalar(tmp, u[:, 1:1 + n], cw[:, x, 1:2], None, ALU.mult),
                    lambda: pool.tensor_tensor(y, y, tmp, ALU.add),
                    lambda: pool.tensor_tensor(y, y, cb[:, :n], ALU.mult),
                ]
                for m, step in enumerate(steps):
                    step().then_inc(c_y, 1)
                    pool.wait_ge(c_y, 6 * k + m + 1)
                pool.dma_start(mixt_dram[768 + cp:768 + cp + P, t:t + n], y).then_inc(c_out[sl_], 16)
                if t + n in (SEQ, T):
                    dst = a["conv_state_p" if t + n == SEQ else "conv_state_s"][0, 0]
                    with nc.allow_non_contiguous_dma(reason="two columns of state"):
                        pool.dma_start(dst[:, cp:cp + P].rearrange("w p -> p w"), u[:, n:n + 2]).then_inc(cs_out, 16)
                    pool.wait_ge(cs_out, 16 * (2 * x + (1 if t + n == SEQ else 2)))
            for q in range(2):
                pool.wait_ge(c_out[q], 16 * len([k for k in range(len(pieces)) if k % 2 == q]))


def phase_sb(nc, a, zt_dram, mixt_dram, k_p, v_p, k_s, v_s):
    QG = 512
    NG = SEQ // QG
    SCALE = SBD ** -0.5
    ZB, AB = 3, 3
    KS = PAST + DEC
    s = Scope(nc, "p3")
    with s:
        ident = s.sb("ident", [P, P])
        identb = s.sb("identb", [P, P], mybir.dt.bfloat16)
        causal = s.sb("causal", [P, P])
        causalb = s.sb("causalb", [P, P], mybir.dt.bfloat16)
        raw = s.sb("raw", [P, 3, 512])
        qh, ql = s.sb("qh", [P, 2, T], F32R), s.sb("ql", [P, 2, T], F32R)
        kh, kl = s.sb("kh", [P, 2, SEQ], F32R), s.sb("kl", [P, 2, SEQ], F32R)
        vh, vl = s.sb("vh", [P, SEQ // P, 256], F32R), s.sb("vl", [P, SEQ // P, 256], F32R)
        zero = s.sb("zero", [P, 512])
        keep = s.sb("keep", [P, 4, SEQ + 1])
        sg, tg = s.sb("sg", [P, 2, 512]), s.sb("tg", [P, 2, 512])
        aw = s.sb("aw", [P, 2, 4, 512])
        ath, atl = s.sb("ath", [P, 2, 512], F32R), s.sb("atl", [P, 2, 512], F32R)
        ob = s.sb("ob", [64, 2, 512])
        ps_z = s.ps("ps_z", [P, ZB, 512])
        ps_a = s.ps("ps_a", [P, AB, 512])
        ps_o = s.ps("ps_o", [64, 2, 512])

        consts_in, consts_done, keep_set = s.sem("consts_in"), s.sem("consts_done"), s.sem("keep_set")
        raw_in = s.sems("raw_in", 3)
        kturned = s.sem("kturned")
        prep_hi, prep_lo = s.sem("prep_hi"), s.sem("prep_lo")
        z_done, sig_done, scan_done = s.sem("z_done"), s.sem("sig_done"), s.sem("scan_done")
        a_dve, a_pool = s.sem("a_dve"), s.sem("a_pool")
        a_turned, a_hi, a_lo, av_done = s.sem("a_turned"), s.sem("a_hi"), s.sem("a_lo"), s.sem("av_done")
        o_out = s.sem("o_out")
        o_st = s.sems("o_st", 2)

        def prep_prompt(g):
            items = [("q", p, g * QG, QG, None) for p in range(2)]
            items += [("k", t, P, k_p[t * P:(t + 1) * P, :], v_p[t * P:(t + 1) * P, :]) for t in range(4 * g, 4 * g + 4)]
            return items

        ck = a["cache_sb_k"][0, 0].rearrange("t h d -> t (h d)")
        cv = a["cache_sb_v"][0, 0].rearrange("t h d -> t (h d)")
        prep_stream = [("q", p, SEQ, DEC, None) for p in range(2)]
        prep_stream += [("k", t, P, ck[t * P:(t + 1) * P, :], cv[t * P:(t + 1) * P, :]) for t in range(4)]
        prep_stream += [("k", 4, DEC, k_s[:, :], v_s[:, :])]

        order, units = [], []

        def add_units(q0, tiles, chunks, tag):
            for h in range(SBH):
                for n, c in enumerate(chunks):
                    diag = n == 0
                    if tag == "prompt":
                        widths = [P * (i + 1) if diag else 512 for i in range(4)]
                        kbs = [(c * 512 + P * b, P, 4 * c + b, b if diag else 0) for b in range(4)]
                        masked = [P * i for i in range(4)]
                    else:
                        widths = [DEC if diag else 512]
                        kbs = [(PAST, DEC, 4, 0)] if diag else [(P * b, P, b, 0) for b in range(4)]
                        masked = [0]
                    units.append(dict(h=h, q0=q0, tiles=tiles, k0=c * 512, widths=widths, kbs=kbs, diag=diag, masked=masked,
                                      first=diag, last=n == len(chunks) - 1, width=sum(m for _, m in tiles)))
                    order.append(("unit", len(units) - 1))

        for g in range(NG):
            order += [("prep", it) for it in prep_prompt(g)]
            add_units(g * QG, [(P * i, P) for i in range(4)], list(range(g, -1, -1)), "prompt")
        order.append(("drain",))
        order += [("prep", it) for it in prep_stream]
        add_units(SEQ, [(0, DEC)], [1, 0], "stream")
        order.append(("drain",))

        n_prep = n_k = n_z = n_a = n_o = 0
        plan, last_unit = [], None
        for it in order:
            if it[0] == "prep":
                plan.append(("prep", it[1], n_prep, n_k))
                n_prep += 1
                n_k += it[1][0] == "k"
            elif it[0] == "unit":
                u = units[it[1]]
                u["z0"], u["a0"], u["o"], u["prep"] = n_z, n_a, n_o, n_prep
                n_z += len(u["tiles"])
                n_a += len(u["kbs"])
                n_o += u["last"]
                plan.append(("unit", it[1], last_unit))
                last_unit = it[1]
            else:
                plan.append(("unit", None, last_unit))
                last_unit = None
        for n, u in enumerate(units):
            u["turned_before"] = units[n - 1]["a0"] if n >= 2 else 0
        nk_free = {}
        a_seen = 0
        for it in plan:
            if it[0] == "prep" and it[1][0] == "k":
                nk_free[it[3]] = a_seen
            elif it[0] == "unit" and it[2] is not None:
                a_seen = units[it[2]]["a0"] + len(units[it[2]]["kbs"])
        on_pool = [z % 2 == 1 for z in range(n_z)]
        pool_before = [sum(on_pool[:z]) for z in range(n_z + 1)]

        def wait_weights(eng, z):
            if z - pool_before[z + 1] + 1 > 0:
                eng.wait_ge(a_dve, z + 1 - pool_before[z + 1])
            if pool_before[z + 1]:
                eng.wait_ge(a_pool, pool_before[z + 1])

        block = s.stack.enter_context(nc.Block())

        @block.sync
        def _(sp):
            sp.dma_start(ident[:], a["ident"]).then_inc(consts_in, 16)
            sp.dma_start(causal[:], a["causal"]).then_inc(consts_in, 16)
            for it in plan:
                if it[0] == "prep":
                    _, (kind, *w), n, _nk = it
                    if n >= 3:
                        sp.wait_ge(prep_lo, 2 * (n - 2))
                    if kind == "q":
                        p, t0, cnt, _x = w
                        for x in (0, cnt // 2):
                            sp.dma_start(raw[:, n % 3, x:x + cnt // 2],
                                         zt_dram[Z_SQ + P * p:Z_SQ + P * (p + 1), t0 + x:t0 + x + cnt // 2]).then_inc(raw_in[n % 3], 16)
                    else:
                        t, m, ks, vs = w
                        sp.dma_start(raw[:m, n % 3, 0:256], ks).then_inc(raw_in[n % 3], 16)
                        sp.dma_start(raw[:m, n % 3, 256:512], vs).then_inc(raw_in[n % 3], 16)
                elif it[2] is not None and units[it[2]]["last"]:
                    u = units[it[2]]
                    sp.wait_ge(o_out, u["o"] + 1)
                    sp.dma_start(mixt_dram[512 + 64 * u["h"]:576 + 64 * u["h"], u["q0"]:u["q0"] + u["width"]],
                                 ob[:, u["o"] % 2, :u["width"]]).then_inc(o_st[u["o"] % 2], 16)
            for q in range(2):
                sp.wait_ge(o_st[q], 16 * len([o for o in range(n_o) if o % 2 == q]))

        def prep_dests(kind, w, nk):
            if kind == "q":
                p, t0, cnt, _x = w
                half = cnt // 2
                return [(qh[:, p, t0 + x:t0 + x + half], ql[:, p, t0 + x:t0 + x + half], ("raw", P, x, half)) for x in (0, half)]
            t, m, ks, vs = w
            return [
                (kh[:, :, t * P:t * P + m], kl[:, :, t * P:t * P + m], ("psum", m)),
                (vh[:m, t, :], vl[:m, t, :], ("raw", m, 256, 256)),
            ]

        def prep_source(src, n, nk):
            if src[0] == "psum":
                return ps_a[:, nk % AB, 0:256].rearrange("p (a t) -> p a t", a=2)[:, :, :src[1]]
            return raw[:src[1], n % 3, src[2]:src[2] + src[3]]

        @block.scalar
        def _(act):
            act.wait_ge(consts_in, 32)
            act.activation(identb[:], ident[:], ACT.Copy).then_inc(consts_done, 1)
            act.activation(causalb[:], causal[:], ACT.Copy).then_inc(consts_done, 1)
            for it in plan:
                if it[0] == "prep":
                    _, (kind, *w), n, nk = it
                    act.wait_ge(raw_in[n % 3], 32 * (n // 3 + 1))
                    for hi, lo, src in prep_dests(kind, w, nk):
                        if src[0] == "psum":
                            act.wait_ge(kturned, nk + 1)
                        act.activation(hi, prep_source(src, n, nk), ACT.Copy).then_inc(prep_hi, 1)
                    continue
                _, cur, before = it
                for i in range(4):
                    if cur is not None and i < len(units[cur]["tiles"]):
                        u = units[cur]
                        z, m, w = u["z0"] + i, u["tiles"][i][1], u["widths"][i]
                        act.wait_ge(z_done, z + 1)
                        if z >= 2:
                            wait_weights(act, z - 2)
                        act.activation(tg[:m, z % 2, :w], ps_z[:m, z % ZB, :w], ACT.Sigmoid, scale=-SCALE).then_inc(sig_done, 1)
                        act.activation(sg[:m, z % 2, :w], ps_z[:m, z % ZB, :w], ACT.Sigmoid, scale=SCALE).then_inc(sig_done, 1)
                    if before is not None and i < len(units[before]["kbs"]):
                        u = units[before]
                        ai = u["a0"] + i
                        k0, kn, vt, i0 = u["kbs"][i]
                        c0, c1 = P * i0, u["width"]
                        act.wait_ge(a_turned, ai + 1)
                        if ai >= 2:
                            act.wait_ge(av_done, ai - 1)
                        act.activation(ath[:kn, ai % 2, c0:c1], ps_a[:kn, ai % AB, c0:c1], ACT.Copy).then_inc(a_hi, 1)
                if before is not None and units[before]["last"]:
                    u = units[before]
                    act.wait_ge(av_done, u["a0"] + len(u["kbs"]))
                    if u["o"] >= 2:
                        act.wait_ge(o_st[u["o"] % 2], 16 * (u["o"] // 2))
                    act.activation(ob[:, u["o"] % 2, :u["width"]], ps_o[:, u["o"] % 2, :u["width"]], ACT.Copy).then_inc(o_out, 1)

        @block.vector
        def _(dve):
            dve.memset(keep[:], 1.0).then_inc(keep_set, 1)
            dve.memset(zero[:], 0.0).then_inc(keep_set, 1)
            dve.wait_ge(keep_set, 2)
            hn = 0
            for it in plan:
                if it[0] == "prep":
                    _, (kind, *w), n, nk = it
                    for hi, lo, src in prep_dests(kind, w, nk):
                        hn += 1
                        dve.wait_ge(prep_hi, hn)
                        dve.tensor_tensor(lo, prep_source(src, n, nk), hi.bitcast(F32), ALU.subtract).then_inc(prep_lo, 1)
                    continue
                _, cur, before = it
                for i in range(4):
                    if cur is not None and i < len(units[cur]["tiles"]):
                        u = units[cur]
                        z, m, w, k0 = u["z0"] + i, u["tiles"][i][1], u["widths"][i], u["k0"]
                        dve.wait_ge(sig_done, 2 * z + 1)
                        if z >= 1:
                            dve.wait_ge(scan_done, z)
                        if pool_before[z]:
                            dve.wait_ge(a_pool, pool_before[z])
                        dve.tensor_tensor_scan(keep[:m, i, k0:k0 + w][:, ::-1], tg[:m, z % 2, :w][:, ::-1], zero[:m, :w],
                                               1.0 if u["first"] else keep[:m, i, k0 + w:k0 + w + 1], ALU.mult, ALU.add).then_inc(scan_done, 1)
                        if not on_pool[z]:
                            dve.wait_ge(scan_done, z + 1)
                            dve.wait_ge(sig_done, 2 * z + 2)
                            if u["turned_before"]:
                                dve.wait_ge(a_turned, u["turned_before"])
                            dve.tensor_tensor(aw[:m, cur % 2, i, :w], sg[:m, z % 2, :w], keep[:m, i, k0 + 1:k0 + w + 1], ALU.mult).then_inc(a_dve, 1)
                    if before is not None and i < len(units[before]["kbs"]):
                        u = units[before]
                        ai = u["a0"] + i
                        k0, kn, vt, i0 = u["kbs"][i]
                        c0, c1 = P * i0, u["width"]
                        dve.wait_ge(a_hi, ai + 1)
                        dve.tensor_tensor(atl[:kn, ai % 2, c0:c1], ps_a[:kn, ai % AB, c0:c1], ath[:kn, ai % 2, c0:c1].bitcast(F32),
                                          ALU.subtract).then_inc(a_lo, 1)

        @block.gpsimd
        def _(pool):
            for it in plan:
                if it[0] != "unit" or it[1] is None:
                    continue
                cur = it[1]
                u = units[cur]
                for i, (o, m) in enumerate(u["tiles"]):
                    z, w, k0 = u["z0"] + i, u["widths"][i], u["k0"]
                    if not on_pool[z]:
                        continue
                    pool.wait_ge(scan_done, z + 1)
                    pool.wait_ge(sig_done, 2 * z + 2)
                    if u["turned_before"]:
                        pool.wait_ge(a_turned, u["turned_before"])
                    pool.tensor_tensor(aw[:m, cur % 2, i, :w], sg[:m, z % 2, :w], keep[:m, i, k0 + 1:k0 + w + 1], ALU.mult).then_inc(a_pool, 1)

        def weigh(pe, u, i):
            ai = u["a0"] + i
            k0, kn, vt, i0 = u["kbs"][i]
            c0, c1 = P * i0, u["width"]
            pe.wait_ge(a_lo, ai + 1)
            start = u["first"] and i == 0
            if start and u["o"] >= 2:
                pe.wait_ge(o_out, u["o"] - 1)
            hc = slice(64 * u["h"], 64 * u["h"] + 64)
            mm = split_product(pe, ps_o[:, u["o"] % 2, c0:c1], vh[:kn, vt, hc], vl[:kn, vt, hc], ath[:kn, ai % 2, c0:c1], atl[:kn, ai % 2, c0:c1],
                               start, u["last"] and i == len(u["kbs"]) - 1, skip=True)
            mm.then_inc(av_done, 1)

        @block.tensor
        def _(pe):
            pe.wait_ge(consts_in, 32)
            pe.wait_ge(consts_done, 2)
            np_ = 0
            for it in plan:
                if it[0] == "prep":
                    _, (kind, *w), n, nk = it
                    np_ = n + 1
                    if kind == "k":
                        t, m, ks, vs = w
                        pe.wait_ge(raw_in[n % 3], 32 * (n // 3 + 1))
                        if nk_free[nk]:
                            pe.wait_ge(a_lo, nk_free[nk])
                        if nk >= AB:
                            pe.wait_ge(prep_lo, 2 * n - 2)
                        for p in range(2):
                            mm = pe.transpose(ps_a[:, nk % AB, P * p:P * p + m], raw[:m, n % 3, P * p:P * p + P], ident[:m, :m])
                        mm.then_inc(kturned, 1)
                    continue
                _, cur, before = it
                for i in range(4):
                    if cur is not None and i < len(units[cur]["tiles"]):
                        u = units[cur]
                        z, (o, m), w = u["z0"] + i, u["tiles"][i], u["widths"][i]
                        if i == 0:
                            pe.wait_ge(prep_lo, 2 * u["prep"])
                        if z >= ZB:
                            pe.wait_ge(sig_done, 2 * (z - ZB + 1))
                        pb, pr = 64 * (u["h"] % 2), u["h"] // 2
                        q = slice(u["q0"] + o, u["q0"] + o + m)
                        ks_ = slice(u["k0"], u["k0"] + w)
                        out = ps_z[:m, z % ZB, :w]
                        if u["diag"]:
                            c = u["masked"][i]
                            pe.matmul(out[:, c:c + m], identb[:m, :m], causalb[:m, :m], start=True, stop=False, skip_group_check=True)
                            mm = split_product(pe, out, qh[pb:pb + 64, pr, q], ql[pb:pb + 64, pr, q], kh[pb:pb + 64, pr, ks_], kl[pb:pb + 64, pr, ks_],
                                               False, True, skip=True)
                        else:
                            mm = split_product(pe, out, qh[pb:pb + 64, pr, q], ql[pb:pb + 64, pr, q], kh[pb:pb + 64, pr, ks_], kl[pb:pb + 64, pr, ks_], True, True)
                        mm.then_inc(z_done, 1)
                    if before is not None and i < len(units[before]["kbs"]):
                        u = units[before]
                        ai = u["a0"] + i
                        k0, kn, vt, i0 = u["kbs"][i]
                        if i == 0:
                            wait_weights(pe, u["z0"] + len(u["tiles"]) - 1)
                        if ai >= AB:
                            pe.wait_ge(a_lo, ai - AB + 1)
                        pe.wait_ge(prep_lo, 2 * np_)
                        for qi in range(i0, len(u["tiles"])):
                            o, m = u["tiles"][qi]
                            mm = pe.transpose(ps_a[:kn, ai % AB, o:o + m], aw[:m, before % 2, qi, k0 - u["k0"]:k0 - u["k0"] + kn], ident[:m, :m])
                        mm.then_inc(a_turned, 1)
                        if i >= 1:
                            weigh(pe, u, i - 1)
                if before is not None:
                    weigh(pe, units[before], len(units[before]["kbs"]) - 1)


def phase_out(nc, mixt_dram, w_out, ln_g, ln_b, xn_dram, x1_dram):
    RAW, BANKS = 4, 6
    s = Scope(nc, "p4")
    with s:
        g_b = s.sb("g_b", [P, D])
        b_b = s.sb("b_b", [P, D])
        eps = s.sb("eps", [P, 1])
        wst = s.sb("wst", [P, 2, D])
        wh = s.sb("wh", [P, KT, D], F32R)
        wl = s.sb("wl", [P, KT, D], F32R)
        raw = s.sb("raw", [P, RAW, NMAX])
        mh = s.sb("mh", [P, 2, KT, NMAX], F32R)
        ml = s.sb("ml", [P, 2, KT, NMAX], F32R)
        res = s.sb("res", [P, 2, D])
        y = s.sb("y", [P, 2, D])
        stats = s.sb("stats", [P, 2, 12])
        mv = s.sb("mv", [P, 2, 2])
        rstd = s.sb("rstd", [P, 2, 1])
        ps = s.ps("ps", [P, BANKS, 512])

        consts_in = s.sem("consts_in")
        eps_set = s.sem("eps_set")
        w_in_ = s.sems("w_in", 2)
        whi_done, wlo_done = s.sem("whi_done"), s.sem("wlo_done")
        mix_in = s.sems("mix_in", RAW)
        mhi_done, mlo_done = s.sem("mhi_done"), s.sem("mlo_done")
        res_in = s.sems("res_in", 2)
        product_done = s.sem("product_done")
        added = s.sem("added")
        stats_done, var_done, std_done = s.sem("stats_done"), s.sem("var_done"), s.sem("std_done")
        rstd_done, centred, scaled, normed = s.sem("rstd_done"), s.sem("centred"), s.sem("scaled"), s.sem("normed")
        y_out = s.sems("y_out", 2)

        gtiles, n = [], 0
        for (t0, cnt) in GROUPS:
            gtiles.append([(n + i, o, c) for i, (o, c) in enumerate(subtiles(t0, cnt, P))])
            n += len(gtiles[-1])
        last_tile = [gt[-1][0] for gt in gtiles]
        order = [("w",), ("mix", 0)]
        for g in range(len(GROUPS)):
            for i, t in enumerate(gtiles[g]):
                order.append(("tile", g, t))
                if i == 0 and g + 1 < len(GROUPS):
                    order.append(("mix", g + 1))

        block = s.stack.enter_context(nc.Block())

        @block.sync
        def _(sp):
            load_row_broadcast(sp, g_b[:], ln_g, consts_in)
            load_row_broadcast(sp, b_b[:], ln_b, consts_in)
            for what, *a in order:
                if what == "w":
                    for k in range(KT):
                        if k >= 2:
                            sp.wait_ge(wlo_done, k - 1)
                        sp.dma_start(wst[:, k % 2, :], w_out[k * P:(k + 1) * P, :]).then_inc(w_in_[k % 2], 16)
                elif what == "mix":
                    g = a[0]
                    t0, cnt = GROUPS[g]
                    for k in range(KT):
                        u = g * KT + k
                        if u >= RAW:
                            sp.wait_ge(mlo_done, u - RAW + 1)
                        sp.dma_start(raw[:, u % RAW, :cnt], mixt_dram[k * P:(k + 1) * P, t0:t0 + cnt]).then_inc(mix_in[u % RAW], 16)
                else:
                    g, (j, o, c) = a
                    t = GROUPS[g][0] + o
                    if j >= 2:
                        sp.wait_ge(added, 2 * (j - 1))
                    sp.dma_start(res[:c, j % 2, :], xn_dram[t:t + c, :]).then_inc(res_in[j % 2], 16)

        @block.scalar
        def _(act):
            for what, *a in order:
                if what == "w":
                    for k in range(KT):
                        act.wait_ge(w_in_[k % 2], 16 * (k // 2 + 1))
                        act.activation(wh[:, k, :], wst[:, k % 2, :], ACT.Copy).then_inc(whi_done, 1)
                elif what == "mix":
                    g = a[0]
                    cnt = GROUPS[g][1]
                    for k in range(KT):
                        u = g * KT + k
                        act.wait_ge(mix_in[u % RAW], 16 * (u // RAW + 1))
                        if g >= 2 and k == 0:
                            act.wait_ge(product_done, 2 * (last_tile[g - 2] + 1))
                        act.activation(mh[:, g % 2, k, :cnt], raw[:, u % RAW, :cnt], ACT.Copy).then_inc(mhi_done, 1)
                else:
                    g, (j, o, c) = a
                    act.wait_ge(eps_set, 1)
                    act.wait_ge(var_done, j + 1)
                    if j >= 2:
                        act.wait_ge(centred, j - 1)
                    act.activation(rstd[:c, j % 2, :], mv[:c, j % 2, 1:2], ACT.Sqrt, bias=eps[:c, :]).then_inc(std_done, 1)

        @block.vector
        def _(dve):
            dve.memset(eps[:], LN_EPS).then_inc(eps_set, 1)
            for what, *a in order:
                if what == "w":
                    for k in range(KT):
                        dve.wait_ge(whi_done, k + 1)
                        dve.tensor_tensor(wl[:, k, :], wst[:, k % 2, :], wh[:, k, :].bitcast(F32), ALU.subtract).then_inc(wlo_done, 1)
                elif what == "mix":
                    g = a[0]
                    cnt = GROUPS[g][1]
                    for k in range(KT):
                        u = g * KT + k
                        dve.wait_ge(mhi_done, u + 1)
                        dve.tensor_tensor(ml[:, g % 2, k, :cnt], raw[:, u % RAW, :cnt], mh[:, g % 2, k, :cnt].bitcast(F32),
                                          ALU.subtract).then_inc(mlo_done, 1)
                else:
                    g, (j, o, c) = a
                    sl = j % 2
                    dve.wait_ge(res_in[sl], 16 * (j // 2 + 1))
                    if j >= 2:
                        dve.wait_ge(y_out[sl], 16 * (j // 2))
                    for h in range(2):
                        dve.wait_ge(product_done, 2 * j + h + 1)
                        dve.scalar_tensor_tensor(out=y[:c, sl, 512 * h:512 * h + 512], in0=res[:c, sl, 512 * h:512 * h + 512], scalar=ALPHA,
                                                 in1=ps[:c, (2 * j + h) % BANKS, :], op0=ALU.mult, op1=ALU.add).then_inc(added, 1)
                    dve.wait_ge(added, 2 * j + 2)
                    dve.bn_stats(stats[:c, sl, 0:6], y[:c, sl, 0:512]).then_inc(stats_done, 1)
                    dve.bn_stats(stats[:c, sl, 6:12], y[:c, sl, 512:1024]).then_inc(stats_done, 1)
                    dve.wait_ge(stats_done, 2 * j + 2)
                    if j >= 2:
                        dve.wait_ge(std_done, j - 1)
                    dve.bn_aggr(mv[:c, sl, :], stats[:c, sl, :]).then_inc(var_done, 1)
                    dve.wait_ge(std_done, j + 1)
                    dve.reciprocal(rstd[:c, sl, :], rstd[:c, sl, :]).then_inc(rstd_done, 1)
                    dve.wait_ge(rstd_done, j + 1)
                    dve.tensor_scalar(y[:c, sl, :], y[:c, sl, :], mv[:c, sl, 0:1], rstd[:c, sl, :], ALU.subtract, ALU.mult).then_inc(centred, 1)
                    dve.wait_ge(centred, j + 1)
                    dve.wait_ge(consts_in, 32)
                    dve.tensor_tensor(y[:c, sl, :], y[:c, sl, :], g_b[:c, :], ALU.mult).then_inc(scaled, 1)

        @block.gpsimd
        def _(pool):
            pool.wait_ge(consts_in, 32)
            for what, *a in order:
                if what == "tile":
                    g, (j, o, c) = a
                    t = GROUPS[g][0] + o
                    pool.wait_ge(scaled, j + 1)
                    pool.tensor_tensor(y[:c, j % 2, :], y[:c, j % 2, :], b_b[:c, :], ALU.add).then_inc(normed, 1)
                    pool.wait_ge(normed, j + 1)
                    pool.dma_start(x1_dram[t:t + c, :], y[:c, j % 2, :]).then_inc(y_out[j % 2], 16)
            for q in range(2):
                pool.wait_ge(y_out[q], 16 * len([j for j in range(n) if j % 2 == q]))

        @block.tensor
        def _(pe):
            pe.wait_ge(wlo_done, KT)
            for what, *a in order:
                if what == "tile":
                    g, (j, o, c) = a
                    pe.wait_ge(mlo_done, KT * (g + 1))
                    for h in range(2):
                        i = 2 * j + h
                        if i >= BANKS:
                            pe.wait_ge(added, i - BANKS + 1)
                        for k in range(KT):
                            mm = split_product(pe, ps[:c, i % BANKS, :], mh[:, g % 2, k, o:o + c], ml[:, g % 2, k, o:o + c],
                                               wh[:, k, 512 * h:512 * h + 512], wl[:, k, 512 * h:512 * h + 512], k == 0, k == KT - 1)
                        mm.then_inc(product_done, 1)


def phase_ffn(nc, x1_dram, w_up, w_down, ln_g, ln_b, ident_in, y_tile, lasting):
    NF = 8
    NC = D_FF // P // NF
    WRING, WSTG = 3, 2
    MT = 5
    s = Scope(nc, "p5")
    with s:
        ident = s.sb("ident", [P, P])
        g_b = s.sb("g_b", [P, D])
        b_b = s.sb("b_b", [P, D])
        eps = s.sb("eps", [P, 1])
        xh = s.sb("xh", [P, KT, NMAX], F32R)
        xl = s.sb("xl", [P, KT, NMAX], F32R)
        res = s.sb("res", [P, 2, MT, D])
        hh = s.sb("hh", [P, NF + 2, NMAX], F32R)
        hl = s.sb("hl", [P, NF + 2, NMAX], F32R)
        r = s.sb("r", [P, 2, 512])
        wst = s.sb("wst", [P, WSTG, 2048])
        wh = s.sb("wh", [P, WRING, 2048], F32R)
        wl = s.sb("wl", [P, WRING, 2048], F32R)
        stats = s.sb("stats", [P, 2, 12])
        mv = s.sb("mv", [P, 2, 2])
        rstd = s.sb("rstd", [P, 2, 1])
        ps_d = s.ps("ps_d", [P, MT, 512])
        ps_u = s.ps("ps_u", [P, 2, 512])
        ps_t = s.ps("ps_t", [P, 512])

        consts_in = s.sem("consts_in")
        eps_set = s.sem("eps_set")
        res_in = s.sems("res_in", MT)
        y_out = lasting.rows
        turned, xhi_done, xlo_done = s.sem("turned"), s.sem("xhi_done"), s.sem("xlo_done")
        w_loaded = s.sems("w_loaded", WSTG)
        whi_done, wlo_done = s.sem("whi_done"), s.sem("wlo_done")
        products = s.sem("products")
        relu_done, sq_done, hfull_done, hlo_done = s.sem("relu_done"), s.sem("sq_done"), s.sem("hfull_done"), s.sem("hlo_done")
        summed = s.sem("summed")
        stats_done, var_done, std_done = s.sem("stats_done"), s.sem("var_done"), s.sem("std_done")
        rstd_done, centred, scaled, normed = s.sem("rstd_done"), s.sem("centred"), s.sem("scaled"), s.sem("normed")

        gtiles, n = [], 0
        for (t0, cnt) in GROUPS:
            gtiles.append([(n + i, o, c) for i, (o, c) in enumerate(subtiles(t0, cnt, P))])
            n += len(gtiles[-1])

        work, nw, wunits = [], 0, []
        for g in range(len(GROUPS)):
            steps = [("up", 0, 0)]
            for c in range(NC):
                steps += [("up", c, p) for p in range(1, NF // 2)]
                if c + 1 < NC:
                    steps.append(("up", c + 1, 0))
                steps += [("down", c, 0), ("down", c, 1)]
            for kind, c, p in steps:
                k = 1 if kind == "up" else 2
                for q in range(k):
                    wunits.append((kind, c, p, q))
                work.append((kind, g, c, p, nw, k))
                nw += k
        order, next_w = [], 0
        order += [("turn", 0, t) for t in gtiles[0]]
        pending_ln = []
        for kind, g, c, p, w0, k in work:
            while next_w < min(nw, w0 + k + 2):
                order.append(("w", next_w))
                next_w += 1
            order.append((kind, g, c, p, w0))
            if kind == "down" and c == NC - 1 and p == 1:
                pending_ln = [("ln", g, t) for t in gtiles[g]]
                if g == len(GROUPS) - 1:
                    order += pending_ln
            elif pending_ln and kind == "up":
                order.append(pending_ln.pop(0))
            if kind == "down" and c == NC - 1 and p == 0 and g + 1 < len(GROUPS):
                order += [("turn", g + 1, t) for t in gtiles[g + 1]]

        mark, up_index, down_index, unit_used = {}, {}, {}, {}
        n_mark = n_up = n_down = n_ln = 0
        last_up, last_down, ln_index = {}, {}, {}
        for what, *a in order:
            if what == "up":
                g, c, p, w0 = a
                for f in (2 * p, 2 * p + 1):
                    for o, cc in subtiles(0, GROUPS[g][1], 512):
                        n_mark += 1
                        mark[("up", n_up)] = n_mark
                        up_index[(g, c, f, o)] = n_up
                        n_up += 1
                unit_used[w0] = n_mark
                last_up[g] = n_mark
                last_up[(g, c)] = n_up
            elif what == "down":
                g, c, h, w0 = a
                n_mark += 1
                unit_used[w0] = n_mark
                for i in range(len(gtiles[g])):
                    n_mark += 1
                    mark[("down", n_down)] = n_mark
                    down_index[(g, c, h, i)] = n_down
                    n_down += 1
                unit_used[w0 + 1] = n_mark
                last_down[(g, c)] = n_mark
                last_down[("n", g, c, h)] = n_down
            elif what == "ln":
                ln_index[(a[0], a[1][0])] = n_ln
                n_ln += 1

        bank_before, in_bank = {}, {}
        for (g, c, h, ti), i in down_index.items():
            bank_before[i] = in_bank.get(ti)
            in_bank[ti] = i

        def slot_of(c, f):
            return (NF + f if c % 2 else f) if f < 2 else f

        def prev_reader(g, c, f):
            gc = g * NC + c - (2 if f < 2 else 1)
            return last_down.get(divmod(gc, NC)) if gc >= 0 else None

        block = s.stack.enter_context(nc.Block())

        @block.sync
        def _(sp):
            sp.dma_start(ident[:], ident_in).then_inc(consts_in, 16)
            load_row_broadcast(sp, g_b[:], ln_g, consts_in)
            load_row_broadcast(sp, b_b[:], ln_b, consts_in)

            def load_res(g):
                for i, (j, o, c) in enumerate(gtiles[g]):
                    t = GROUPS[g][0] + o
                    stored = len([q for q in gtiles[:max(0, g - 1)] if len(q) > i])
                    if stored:
                        sp.wait_ge(y_out[i], 16 * stored)
                    sp.dma_start(res[:c, g % 2, i, :], x1_dram[t:t + c, :]).then_inc(res_in[i], 16)

            load_res(0)
            for what, *a in order:
                if what == "w":
                    u = a[0]
                    if u >= WSTG:
                        sp.wait_ge(wlo_done, u - WSTG + 1)
                    kind, c, p, q = wunits[u]
                    if kind == "up":
                        c0 = (c * NF + 2 * p) * P
                        sp.dma_start(wst[:, u % WSTG, :].rearrange("p (k f) -> p k f", k=KT),
                                     w_up.rearrange("(k p) f -> p k f", p=P)[:, :, c0:c0 + 2 * P]).then_inc(w_loaded[u % WSTG], 16)
                    else:
                        r0 = c * NF + 4 * q
                        sp.dma_start(wst[:, u % WSTG, :].rearrange("p (f n) -> p f n", f=4),
                                     w_down.rearrange("(f p) n -> p f n", p=P)[:, r0:r0 + 4, 512 * p:512 * p + 512]).then_inc(w_loaded[u % WSTG], 16)
                elif what == "down" and a[1] == 1 and a[2] == 1 and a[0] + 1 < len(GROUPS):
                    load_res(a[0] + 1)

        @block.scalar
        def _(act):
            for what, *a in order:
                if what == "w":
                    u = a[0]
                    act.wait_ge(w_loaded[u % WSTG], 16 * (u // WSTG + 1))
                    if u >= WRING:
                        act.wait_ge(products, unit_used[u - WRING])
                    act.activation(wh[:, u % WRING, :], wst[:, u % WSTG, :], ACT.Copy).then_inc(whi_done, 1)
                elif what == "turn":
                    g, (j, o, c) = a
                    for q in range(2):
                        act.wait_ge(turned, 2 * j + q + 1)
                        if g >= 1:
                            act.wait_ge(products, last_up[g - 1])
                        act.activation(xh[:, 4 * q:4 * q + 4, o:o + c], ps_t[:, :].rearrange("p (k t) -> p k t", k=4)[:, :, :c],
                                       ACT.Copy).then_inc(xhi_done, 1)
                elif what == "up":
                    g, c, p, w0 = a
                    for f in (2 * p, 2 * p + 1):
                        for o, cc in subtiles(0, GROUPS[g][1], 512):
                            i = up_index[(g, c, f, o)]
                            act.wait_ge(products, mark[("up", i)])
                            if i >= 2:
                                act.wait_ge(hlo_done, i - 1)
                            act.activation(r[:, i % 2, :cc], ps_u[:, i % 2, :cc], ACT.Relu).then_inc(relu_done, 1)
                            act.wait_ge(hfull_done, i + 1)
                            before = prev_reader(g, c, f)
                            if before:
                                act.wait_ge(products, before)
                            act.activation(hh[:, slot_of(c, f), o:o + cc], r[:, i % 2, :cc], ACT.Copy).then_inc(sq_done, 1)
                elif what == "ln":
                    g, (j, o, c) = a
                    i = ln_index[(g, j)]
                    act.wait_ge(eps_set, 1)
                    act.wait_ge(var_done, i + 1)
                    if i >= 2:
                        act.wait_ge(centred, i - 1)
                    act.activation(rstd[:c, i % 2, :], mv[:c, i % 2, 1:2], ACT.Sqrt, bias=eps[:c, :]).then_inc(std_done, 1)

        @block.vector
        def _(dve):
            dve.memset(eps[:], LN_EPS).then_inc(eps_set, 1)
            for what, *a in order:
                if what == "w":
                    u = a[0]
                    dve.wait_ge(whi_done, u + 1)
                    dve.tensor_tensor(wl[:, u % WRING, :], wst[:, u % WSTG, :], wh[:, u % WRING, :].bitcast(F32), ALU.subtract).then_inc(wlo_done, 1)
                elif what == "turn":
                    g, (j, o, c) = a
                    for q in range(2):
                        dve.wait_ge(xhi_done, 2 * j + q + 1)
                        dve.tensor_tensor(xl[:, 4 * q:4 * q + 4, o:o + c], ps_t[:, :].rearrange("p (k t) -> p k t", k=4)[:, :, :c],
                                          xh[:, 4 * q:4 * q + 4, o:o + c].bitcast(F32), ALU.subtract).then_inc(xlo_done, 1)
                elif what == "up":
                    g, c, p, w0 = a
                    for f in (2 * p, 2 * p + 1):
                        for o, cc in subtiles(0, GROUPS[g][1], 512):
                            i = up_index[(g, c, f, o)]
                            dve.wait_ge(relu_done, i + 1)
                            dve.scalar_tensor_tensor(out=r[:, i % 2, :cc], in0=ps_u[:, i % 2, :cc], scalar=0.0, in1=r[:, i % 2, :cc],
                                                     op0=ALU.max, op1=ALU.mult).then_inc(hfull_done, 1)
                            dve.wait_ge(sq_done, i + 1)
                            dve.tensor_tensor(hl[:, slot_of(c, f), o:o + cc], r[:, i % 2, :cc], hh[:, slot_of(c, f), o:o + cc].bitcast(F32),
                                              ALU.subtract).then_inc(hlo_done, 1)
                elif what == "down":
                    g, c, h, w0 = a
                    for ti, (j, o, cc) in enumerate(gtiles[g]):
                        i = down_index[(g, c, h, ti)]
                        dve.wait_ge(products, mark[("down", i)])
                        if i >= 1:
                            dve.wait_ge(summed, i)
                        acc = res[:cc, g % 2, ti, 512 * h:512 * h + 512]
                        dve.scalar_tensor_tensor(out=acc, in0=acc, scalar=ALPHA if c == 0 else 1.0, in1=ps_d[:cc, ti, :],
                                                 op0=ALU.mult, op1=ALU.add).then_inc(summed, 1)
                elif what == "ln":
                    g, (j, o, c) = a
                    i = ln_index[(g, j)]
                    sl, ti = i % 2, gtiles[g].index((j, o, c))
                    acc = res[:c, g % 2, ti, :]
                    dve.wait_ge(summed, last_down[("n", g, NC - 1, 1)])
                    dve.bn_stats(stats[:c, sl, 0:6], acc[:, 0:512]).then_inc(stats_done, 1)
                    dve.bn_stats(stats[:c, sl, 6:12], acc[:, 512:1024]).then_inc(stats_done, 1)
                    dve.wait_ge(stats_done, 2 * i + 2)
                    if i >= 2:
                        dve.wait_ge(std_done, i - 1)
                    dve.bn_aggr(mv[:c, sl, :], stats[:c, sl, :]).then_inc(var_done, 1)
                    dve.wait_ge(std_done, i + 1)
                    dve.reciprocal(rstd[:c, sl, :], rstd[:c, sl, :]).then_inc(rstd_done, 1)
                    dve.wait_ge(rstd_done, i + 1)
                    dve.tensor_scalar(acc, acc, mv[:c, sl, 0:1], rstd[:c, sl, :], ALU.subtract, ALU.mult).then_inc(centred, 1)
                    dve.wait_ge(centred, i + 1)
                    dve.wait_ge(consts_in, 48)
                    dve.tensor_tensor(acc, acc, g_b[:c, :], ALU.mult).then_inc(scaled, 1)

        @block.gpsimd
        def _(pool):
            pool.wait_ge(consts_in, 48)
            for what, *a in order:
                if what == "ln":
                    g, (j, o, c) = a
                    i, ti = ln_index[(g, j)], gtiles[g].index((j, o, c))
                    pool.wait_ge(scaled, i + 1)
                    pool.tensor_tensor(res[:c, g % 2, ti, :], res[:c, g % 2, ti, :], b_b[:c, :], ALU.add).then_inc(normed, 1)
                    pool.wait_ge(normed, i + 1)
                    pool.dma_start(y_tile(j), res[:c, g % 2, ti, :]).then_inc(y_out[ti], 16)
            for ti in range(MT):
                pool.wait_ge(y_out[ti], 16 * len([g for g in gtiles if len(g) > ti]))

        @block.tensor
        def _(pe):
            pe.wait_ge(consts_in, 48)
            for what, *a in order:
                if what == "turn":
                    g, (j, o, c) = a
                    ti = gtiles[g].index((j, o, c))
                    pe.wait_ge(res_in[ti], 16 * len([q for q in gtiles[:g + 1] if len(q) > ti]))
                    for q in range(2):
                        if 2 * j + q >= 1:
                            pe.wait_ge(xlo_done, 2 * j + q)
                        for k in range(4):
                            mm = pe.transpose(ps_t[:, k * P:k * P + c], res[:c, g % 2, ti, (4 * q + k) * P:(4 * q + k + 1) * P], ident[:c, :c])
                        mm.then_inc(turned, 1)
                elif what == "up":
                    g, c, p, w0 = a
                    pe.wait_ge(xlo_done, 2 * (gtiles[g][-1][0] + 1))
                    pe.wait_ge(wlo_done, w0 + 1)
                    for f in (2 * p, 2 * p + 1):
                        for o, cc in subtiles(0, GROUPS[g][1], 512):
                            i = up_index[(g, c, f, o)]
                            if i >= 2:
                                pe.wait_ge(hfull_done, i - 1)
                            for k in range(KT):
                                col = slice(256 * k + P * (f - 2 * p), 256 * k + P * (f - 2 * p) + P)
                                mm = split_product(pe, ps_u[:, i % 2, :cc], wh[:, w0 % WRING, col], wl[:, w0 % WRING, col],
                                                   xh[:, k, o:o + cc], xl[:, k, o:o + cc], k == 0, k == KT - 1)
                            mm.then_inc(products, 1)
                elif what == "down":
                    g, c, h, w0 = a
                    pe.wait_ge(hlo_done, last_up[(g, c)])
                    for f in range(NF):
                        w = w0 + f // 4
                        pe.wait_ge(wlo_done, w + 1)
                        row = slice(512 * (f % 4), 512 * (f % 4) + 512)
                        for ti, (j, o, cc) in enumerate(gtiles[g]):
                            i = down_index[(g, c, h, ti)]
                            if f == 0 and bank_before[i] is not None:
                                pe.wait_ge(summed, bank_before[i] + 1)
                            sl = slot_of(c, f)
                            mm = split_product(pe, ps_d[:cc, ti, :], hh[:, sl, o:o + cc], hl[:, sl, o:o + cc],
                                               wh[:, w % WRING, row], wl[:, w % WRING, row], f == 0, f == NF - 1)
                            if f == NF - 1:
                                mm.then_inc(products, 1)
                        if f == 3:
                            mm.then_inc(products, 1)


def build_program(nc, a):
    def dram(name, shape):
        return nc.dram_tensor(name, shape, F32, kind="Internal").ap()

    xn_dram = dram("xn_scratch", (T, D))
    zt_dram = dram("zt_scratch", (Z_ROWS, T))
    gv_dram = dram("gv_scratch", (T, 512))
    mixt_dram = dram("mixt_scratch", (D, T))
    x1_dram = dram("x1_scratch", (T, D))
    x_p, x_s = a["x_prompt"][0], a["x_sample"][0]
    k_p = a["new_sb_k_p"][0, 0].rearrange("t h d -> t (h d)")
    v_p = a["new_sb_v_p"][0, 0].rearrange("t h d -> t (h d)")
    k_s = a["new_sb_k_s"][0, 0].rearrange("t h d -> t (h d)")
    v_s = a["new_sb_v_s"][0, 0].rearrange("t h d -> t (h d)")

    def x_tile(j):
        t, c = TILES[j]
        return x_p[t:t + c, :] if t < SEQ else x_s[t - SEQ:t - SEQ + c, :]

    def y_tile(j):
        t, c = TILES[j]
        return a["y_prompt"][0][t:t + c, :] if t < SEQ else a["y_sample"][0][t - SEQ:t - SEQ + c, :]

    def token_stores(what, t, n):
        if what == "gv":
            return [(gv_dram[t:t + n, :], 0, 512)]
        if t < SEQ:
            return [(k_p[t:t + n, :], 0, 256), (v_p[t:t + n, :], 256, 512)]
        return [(k_s[t - SEQ:t - SEQ + n, :], 0, 256), (v_s[t - SEQ:t - SEQ + n, :], 256, 512)]

    lasting = OutputStores(nc)
    with lasting.scope.stack:
        phase_in(nc, x_tile, a["ln_in_g"], a["ln_in_b"], a["w_in"][0], a["ident"], xn_dram, zt_dram, token_stores, lasting)
        phase_gla(nc, a, zt_dram, gv_dram, mixt_dram, lasting)
        phase_sb(nc, a, zt_dram, mixt_dram, k_p, v_p, k_s, v_s)
        phase_out(nc, mixt_dram, a["w_out"][0], a["ln1_g"][0], a["ln1_b"][0], xn_dram, x1_dram)
        phase_ffn(nc, x1_dram, a["w_up"][0], a["w_down"][0], a["ln2_g"][0], a["ln2_b"][0], a["ident"], y_tile, lasting)


OUTPUTS = {
    "y_prompt": (1, SEQ, D),
    "y_sample": (1, DEC, D),
    "new_sb_k_p": (1, 1, SEQ, SBH, SBD),
    "new_sb_v_p": (1, 1, SEQ, SBH, SBD),
    "gla_state_p": (1, 1, HEADS, DK, DV),
    "conv_state_p": (1, 1, 2, CONV_CH),
    "new_sb_k_s": (1, 1, DEC, SBH, SBD),
    "new_sb_v_s": (1, 1, DEC, SBH, SBD),
    "gla_state_s": (1, 1, HEADS, DK, DV),
    "conv_state_s": (1, 1, 2, CONV_CH),
}


def shape_constants():
    ident = np.eye(P, dtype=np.float32)
    s_, t_ = np.arange(P)[:, None], np.arange(P)[None, :]
    level_masks = []
    for hs in LEVELS:
        second = np.array([t for t in range(P) if (t // hs) % 2 == 1])[None, :]
        level_masks.append(((s_ // (2 * hs) == second // (2 * hs)) & ((s_ // hs) % 2 == 0)).astype(np.float32))
    level_masks.append((s_ == t_).astype(np.float32))
    chunk_start = np.ones((P, T), np.float32)
    chunk_start[:, ::CHUNK] = 0.0
    causal = np.where(t_ < s_, 0.0, MASKED).astype(np.float32)
    return {
        "ident": ident,
        "level_masks": np.concatenate(level_masks, axis=1),
        "chunk_start": chunk_start,
        "causal": causal,
        "ones": np.ones((P, P), np.float32),
    }


LEVELS = (32, 16, 8, 4, 2, 1)


def kernel(**inputs):
    import concourse.bacc as bacc
    from concourse.bass_utils import run_bass_kernel_spmd

    nc = bacc.Bacc("TRN2", target_bir_lowering=False, num_devices=1)
    arrays, aps = {}, {}
    for name, value in {**inputs, **shape_constants()}.items():
        value = np.ascontiguousarray(value)
        arrays[f"in_{name}"] = value
        aps[name] = nc.dram_tensor(f"in_{name}", value.shape, mybir.dt.from_np(value.dtype), kind="ExternalInput").ap()
    for name, shape in OUTPUTS.items():
        aps[name] = nc.dram_tensor(f"out_{name}", shape, F32, kind="ExternalOutput").ap()
    build_program(nc, aps)
    r = run_bass_kernel_spmd(nc, [arrays], core_ids=[0])
    return tuple(r.results[0][f"out_{name}"] for name in OUTPUTS)
```

```python
from contextlib import ExitStack

import numpy as np
import concourse.bass as bass
import concourse.mybir as mybir

F32 = mybir.dt.float32
F32R = mybir.dt.float32r
I32 = mybir.dt.int32
ALU = mybir.AluOpType
ACT = mybir.ActivationFunctionType

P = 128
D = 1024
KT = D // P
SEQ, DEC, PAST = 2048, 64, 512
T = SEQ + DEC
D_FF = 4 * D
HEADS, DK, DV = 4, 64, 128
CHUNK = 64
RANK = 16
TAU = 16.0
SBH, SBD = 4, 64
CONV_CH = 256
LN_EPS = 1e-5
ALPHA = 2.0 ** 0.25
MASKED = -1e30

C_GQ, C_GK, C_GV, C_GR, C_GL = 0, 256, 512, 1024, 1536
C_SQ, C_SK, C_SV, C_CB, C_CC, C_CH = 1552, 1808, 2064, 2320, 2576, 2832
Z_GQ, Z_GK, Z_GR, Z_GL, Z_SQ, Z_CB, Z_CC, Z_CH, Z_ROWS = 0, 256, 512, 1024, 1040, 1296, 1552, 1808, 2064

GROUPS = [(0, 512), (512, 512), (1024, 512), (1536, 576)]
NMAX = 576


def subtiles(start, n, width):
    return [(o, min(width, n - o)) for o in range(0, n, width)]


def moving(n):
    parts = -(-n // 512)
    return [(i * (n // parts), n // parts) for i in range(parts)]


TILES = [(t, min(P, T - t)) for t in range(0, T, P)]


class Scope:

    def __init__(self, nc, tag):
        self.nc, self.tag, self.stack, self.semaphores = nc, tag, ExitStack(), []

    def __enter__(self):
        self.stack.__enter__()
        return self

    def __exit__(self, *e):
        self.stack.__exit__(*e)
        if self.semaphores:
            self.nc.clear_and_free_semaphores(self.semaphores)
            self.nc.all_engine_barrier()

    def sb(self, name, shape, dt=F32):
        return self.stack.enter_context(self.nc.sbuf_tensor(f"{self.tag}_{name}", shape, dt))

    def ps(self, name, shape):
        return self.stack.enter_context(self.nc.psum_tensor(f"{self.tag}_{name}", shape, F32))

    def sem(self, name):
        self.semaphores.append(self.nc.alloc_semaphore(f"{self.tag}_{name}"))
        return self.semaphores[-1]

    def sems(self, name, n):
        return [self.sem(f"{name}{i}") for i in range(n)]


class OutputStores:

    def __init__(self, nc):
        self.scope = Scope(nc, "stores")
        self.results = self.scope.sems("results", 4)
        self.states = self.scope.sem("states")
        self.conv_states = self.scope.sem("conv_states")
        self.rows = self.scope.sems("rows", 5)


def load_row_broadcast(eng, dst, row, sem):
    eng.dma_start(dst, row.rearrange("(o d) -> o d", o=1).to_broadcast([P, D])).then_inc(sem, 16)


def split_product(pe, out, lhs_hi, lhs_lo, rhs_hi, rhs_lo, first, last, skip=False):
    pe.matmul(out, lhs_hi, rhs_hi, start=first, stop=False, skip_group_check=skip)
    pe.matmul(out, lhs_lo, rhs_hi, start=False, stop=False, skip_group_check=skip)
    return pe.matmul(out, lhs_hi, rhs_lo, start=False, stop=last, skip_group_check=skip)


def phase_in(nc, x_tile, ln_g, ln_b, w_in, ident_in, xn_dram, zt_dram, token_stores, lasting):
    WW = 528
    chunks = [
        ([(C_GQ, 512)], "F", Z_GQ),
        ([(C_GR, 528)], "F", Z_GR),
        ([(C_GV, 512)], "T", "gv"),
        ([(C_SQ, 256), (C_CB, 256)], "F", Z_SQ),
        ([(C_SK, 512)], "T", "kv"),
        ([(C_CC, 512)], "F", Z_CC),
    ]
    NCH = len(chunks)
    WSTAGE, OUTS, BANKS = 4, 4, 6
    s = Scope(nc, "p1")
    with s:
        ident = s.sb("ident", [P, P])
        g_b = s.sb("g_b", [P, D])
        b_b = s.sb("b_b", [P, D])
        xs = s.sb("xs", [P, 2, D])
        xn = s.sb("xn", [P, 2, D])
        stats = s.sb("stats", [P, 2, 12])
        mv = s.sb("mv", [P, 2, 2])
        rstd = s.sb("rstd", [P, 2, 1])
        eps = s.sb("eps", [P, 1])
        xh = s.sb("xh", [P, 2, KT, NMAX], F32R)
        xl = s.sb("xl", [P, 2, KT, NMAX], F32R)
        wst = s.sb("wst", [P, WSTAGE, WW])
        wh = s.sb("wh", [P, 2, KT, WW], F32R)
        wl = s.sb("wl", [P, 2, KT, WW], F32R)
        outb = s.sb("outb", [P, OUTS, 512])
        ps_t = s.ps("ps_t", [P, 2, 512])
        ps_m = s.ps("ps_m", [P, BANKS, 512])

        ident_loaded, rows_in = s.sem("ident_loaded"), s.sem("rows_in")
        eps_set = s.sem("eps_set")
        x_in = s.sems("x_in", 2)
        stats_done = s.sem("stats_done")
        var_done = s.sem("var_done")
        std_done = s.sem("std_done")
        rstd_done = s.sem("rstd_done")
        centred = s.sem("centred")
        scaled = s.sem("scaled")
        normed = s.sem("normed")
        xn_out = s.sems("xn_out", 2)
        turned = s.sem("turned")
        xhi_done = s.sem("xhi_done")
        xlo_done = s.sem("xlo_done")
        w_loaded = s.sems("w_in", WSTAGE)
        whi_done = s.sem("whi_done")
        wlo_done = s.sem("wlo_done")
        unit_done = s.sem("unit_done")
        evacuated = s.sem("evacuated")
        out_st = lasting.results

        gtiles, n = [], 0
        for (t0, cnt) in GROUPS:
            gtiles.append([(n + i, o, c) for i, (o, c) in enumerate(subtiles(t0, cnt, P))])
            n += len(gtiles[-1])
        units = []
        for g, (t0, cnt) in enumerate(GROUPS):
            for c, (pieces, kind, where) in enumerate(chunks):
                gc = g * NCH + c
                width = sum(w for _, w in pieces)
                if kind == "F":
                    for m0 in range(0, width, P):
                        mw = min(P, width - m0)
                        for o, cc in moving(cnt):
                            units.append(dict(g=g, gc=gc, kind="F", m0=m0, mw=mw, o=o, n=cc, t0=t0, row=where + m0))
                else:
                    for o, cc in subtiles(t0, cnt, P):
                        units.append(dict(g=g, gc=gc, kind="T", o=o, n=cc, t0=t0, what=where))
        by_chunk = {}
        for i, u in enumerate(units):
            by_chunk.setdefault(u["gc"], []).append((i, u))
        chunk_end = {gc: us[-1][0] + 1 for gc, us in by_chunk.items()}
        order = [("norm", 0, gtiles[0][0]), ("weights", 0)]
        for i, t in enumerate(gtiles[0]):
            order += [("norm", 0, x) for x in gtiles[0][i + 1:i + 2]] + [("turn", 0, t)]
        for g in range(len(GROUPS)):
            for c in range(NCH):
                gc = g * NCH + c
                if gc + 1 < NCH * len(GROUPS):
                    order.append(("weights", gc + 1))
                ahead = [(g + 1, t) for t in gtiles[g + 1][c:c + 1]] if g + 1 < len(GROUPS) else []
                order += [("norm", *x) for x in ahead] + [("product", gc)] + [("turn", *x) for x in ahead]

        block = s.stack.enter_context(nc.Block())

        @block.sync
        def _(sp):
            for what, *a in order:
                if what == "norm":
                    j, o, c = a[1]
                    if j >= 2:
                        sp.wait_ge(centred, j - 1)
                    sp.dma_start(xs[:c, j % 2, :], x_tile(j)).then_inc(x_in[j % 2], 16)
                    if j == 0:
                        load_row_broadcast(sp, g_b[:], ln_g, rows_in)
                        load_row_broadcast(sp, b_b[:], ln_b, rows_in)
                        sp.dma_start(ident[:], ident_in).then_inc(ident_loaded, 16)
                elif what == "weights":
                    gc = a[0]
                    for k in range(KT):
                        u = gc * KT + k
                        if u >= WSTAGE:
                            sp.wait_ge(wlo_done, u - WSTAGE + 1)
                        slot, at = u % WSTAGE, 0
                        pieces = chunks[gc % NCH][0]
                        for c0, w in pieces:
                            sp.dma_start(wst[:, slot, at:at + w], w_in[k * P:(k + 1) * P, c0:c0 + w]).then_inc(w_loaded[slot], 16)
                            at += w

        def n_stores(i):
            return sum(1 if units[j]["kind"] == "F" or units[j]["what"] == "gv" else 2 for j in range(i % OUTS, i + 1, OUTS))

        slot_loads = [0] * WSTAGE
        loads_by_unit = []
        for u in range(NCH * len(GROUPS) * KT):
            slot_loads[u % WSTAGE] += len(chunks[(u // KT) % NCH][0])
            loads_by_unit.append(slot_loads[u % WSTAGE])

        @block.scalar
        def _(act):
            for what, *a in order:
                if what == "norm":
                    g, (j, o, c) = a
                    act.wait_ge(eps_set, 1)
                    act.wait_ge(var_done, j + 1)
                    if j >= 2:
                        act.wait_ge(centred, j - 1)
                    act.activation(rstd[:c, j % 2, :], mv[:c, j % 2, 1:2], ACT.Sqrt, bias=eps[:c, :]).then_inc(std_done, 1)
                elif what == "turn":
                    g, (j, o, c) = a
                    for q in range(2):
                        act.wait_ge(turned, 2 * j + q + 1)
                        if g >= 2 and q == 0:
                            act.wait_ge(unit_done, chunk_end[(g - 1) * NCH - 1])
                        act.activation(xh[:, g % 2, 4 * q:4 * q + 4, o:o + c],
                                       ps_t[:, q, :].rearrange("p (k t) -> p k t", k=4)[:, :, :c],
                                       ACT.Copy).then_inc(xhi_done, 1)
                elif what == "weights":
                    gc = a[0]
                    width = sum(w for _, w in chunks[gc % NCH][0])
                    for k in range(KT):
                        u = gc * KT + k
                        act.wait_ge(w_loaded[u % WSTAGE], 16 * loads_by_unit[u])
                        if gc >= 2 and k == 0:
                            act.wait_ge(unit_done, chunk_end[gc - 2])
                        act.activation(wh[:, gc % 2, k, :width], wst[:, u % WSTAGE, :width], ACT.Copy).then_inc(whi_done, 1)
                else:
                    for i, u in by_chunk[a[0]]:
                        act.wait_ge(unit_done, i + 1)
                        if i >= OUTS:
                            act.wait_ge(out_st[i % OUTS], 16 * n_stores(i - OUTS))
                        rows, cols = (u["mw"], u["n"]) if u["kind"] == "F" else (u["n"], 512)
                        act.activation(outb[:rows, i % OUTS, :cols], ps_m[:rows, i % BANKS, :cols], ACT.Copy).then_inc(evacuated, 1)
                        act.wait_ge(evacuated, i + 1)
                        src = outb[:, i % OUTS, :]
                        t = u["t0"] + u["o"]
                        if u["kind"] == "F":
                            act.dma_start(zt_dram[u["row"]:u["row"] + u["mw"], t:t + u["n"]], src[:u["mw"], :u["n"]]).then_inc(out_st[i % OUTS], 16)
                        else:
                            for dst, c0, c1 in token_stores(u["what"], t, u["n"]):
                                act.dma_start(dst, src[:u["n"], c0:c1]).then_inc(out_st[i % OUTS], 16)
            for q in range(OUTS):
                last = max(i for i in range(len(units)) if i % OUTS == q)
                act.wait_ge(out_st[q], 16 * n_stores(last))

        @block.vector
        def _(dve):
            dve.memset(eps[:], LN_EPS).then_inc(eps_set, 1)
            for what, *a in order:
                if what == "norm":
                    g, (j, o, c) = a
                    sl = j % 2
                    dve.wait_ge(x_in[sl], 16 * (j // 2 + 1))
                    dve.bn_stats(stats[:c, sl, 0:6], xs[:c, sl, 0:512]).then_inc(stats_done, 1)
                    dve.bn_stats(stats[:c, sl, 6:12], xs[:c, sl, 512:1024]).then_inc(stats_done, 1)
                    dve.wait_ge(stats_done, 2 * j + 2)
                    if j >= 2:
                        dve.wait_ge(std_done, j - 1)
                    dve.bn_aggr(mv[:c, sl, :], stats[:c, sl, :]).then_inc(var_done, 1)
                    dve.wait_ge(std_done, j + 1)
                    dve.reciprocal(rstd[:c, sl, :], rstd[:c, sl, :]).then_inc(rstd_done, 1)
                    dve.wait_ge(rstd_done, j + 1)
                    if j >= 2:
                        dve.wait_ge(xn_out[sl], 16 * (j // 2))
                        dve.wait_ge(turned, 2 * (j - 1))
                    dve.tensor_scalar(xn[:c, sl, :], xs[:c, sl, :], mv[:c, sl, 0:1], rstd[:c, sl, :], ALU.subtract, ALU.mult).then_inc(centred, 1)
                    dve.wait_ge(centred, j + 1)
                    dve.wait_ge(rows_in, 32)
                    dve.tensor_tensor(xn[:c, sl, :], xn[:c, sl, :], g_b[:c, :], ALU.mult).then_inc(scaled, 1)
                elif what == "turn":
                    g, (j, o, c) = a
                    for q in range(2):
                        dve.wait_ge(xhi_done, 2 * j + q + 1)
                        dve.tensor_tensor(xl[:, g % 2, 4 * q:4 * q + 4, o:o + c],
                                          ps_t[:, q, :].rearrange("p (k t) -> p k t", k=4)[:, :, :c],
                                          xh[:, g % 2, 4 * q:4 * q + 4, o:o + c].bitcast(F32), ALU.subtract).then_inc(xlo_done, 1)
                elif what == "weights":
                    gc = a[0]
                    width = sum(w for _, w in chunks[gc % NCH][0])
                    for k in range(KT):
                        u = gc * KT + k
                        dve.wait_ge(whi_done, u + 1)
                        dve.tensor_tensor(wl[:, gc % 2, k, :width], wst[:, u % WSTAGE, :width],
                                          wh[:, gc % 2, k, :width].bitcast(F32), ALU.subtract).then_inc(wlo_done, 1)

        @block.gpsimd
        def _(pool):
            pool.wait_ge(rows_in, 32)
            for what, *a in order:
                if what == "norm":
                    g, (j, o, c) = a
                    pool.wait_ge(scaled, j + 1)
                    pool.tensor_tensor(xn[:c, j % 2, :], xn[:c, j % 2, :], b_b[:c, :], ALU.add).then_inc(normed, 1)
                    pool.wait_ge(normed, j + 1)
                    t = GROUPS[g][0] + o
                    pool.dma_start(xn_dram[t:t + c, :], xn[:c, j % 2, :]).then_inc(xn_out[j % 2], 16)
            for q in range(2):
                pool.wait_ge(xn_out[q], 16 * len([j for j in range(n) if j % 2 == q]))

        @block.tensor
        def _(pe):
            pe.wait_ge(ident_loaded, 16)
            for what, *a in order:
                if what == "turn":
                    g, (j, o, c) = a
                    pe.wait_ge(normed, j + 1)
                    for q in range(2):
                        if j >= 1:
                            pe.wait_ge(xlo_done, 2 * (j - 1) + q + 1)
                        for k in range(4):
                            mm = pe.transpose(ps_t[:, q, k * P:k * P + c], xn[:c, j % 2, (4 * q + k) * P:(4 * q + k + 1) * P], ident[:c, :c])
                        mm.then_inc(turned, 1)
                elif what == "product":
                    gc = a[0]
                    g = gc // NCH
                    tiles_by = gtiles[g][-1][0] + 1
                    pe.wait_ge(xlo_done, 2 * tiles_by)
                    pe.wait_ge(wlo_done, KT * (gc + 1))
                    for i, u in by_chunk[gc]:
                        if i >= BANKS:
                            pe.wait_ge(evacuated, i - BANKS + 1)
                        for k in range(KT):
                            tok = slice(u["o"], u["o"] + u["n"])
                            hx, lx = xh[:, g % 2, k, tok], xl[:, g % 2, k, tok]
                            if u["kind"] == "F":
                                col = slice(u["m0"], u["m0"] + u["mw"])
                                mm = split_product(pe, ps_m[:u["mw"], i % BANKS, :u["n"]], wh[:, gc % 2, k, col], wl[:, gc % 2, k, col],
                                                   hx, lx, k == 0, k == KT - 1)
                            else:
                                mm = split_product(pe, ps_m[:u["n"], i % BANKS, :512], hx, lx, wh[:, gc % 2, k, :512], wl[:, gc % 2, k, :512],
                                                   k == 0, k == KT - 1)
                        mm.then_inc(unit_done, 1)


def phase_gla(nc, a, zt_dram, gv_dram, mixt_dram, lasting):
    GG = [(g * 512, 512) for g in range(SEQ // 512)] + [(SEQ, DEC)]
    NG = len(GG)
    NL = len(LEVELS)
    QSCALE = DK ** -0.5
    EX, VS = 3, 3
    s = Scope(nc, "p2")
    with s:
        ident, ones = s.sb("ident", [P, P]), s.sb("ones", [P, P])
        masks = s.sb("masks", [P, NL * 64 + P])
        starts = s.sb("starts", [P, 512])
        eps = s.sb("eps", [P, 1])
        wgu = s.sb("wgu", [RANK, 256])
        bg = s.sb("bg", [P, 2])
        gn = s.sb("gn", [P, HEADS])
        cw = s.sb("cw", [P, 2, 3])
        glow = s.sb("glow", [RANK, 2, 512])
        gq, gk = s.sb("gq", [P, 2, 2, 512]), s.sb("gk", [P, 2, 2, 512])
        gr = s.sb("gr", [P, 4, 512])
        gy, ga = s.sb("gy", [P, 2, 512]), s.sb("ga", [P, 2, 512])
        bc = s.sb("bc", [P, 2, 2, 512])
        ex = s.sb("ex", [P, EX, 2, 512])
        att = s.sb("att", [P, 2, 2, 4, 2, P])
        eb = s.sb("eb", [P, 2, 2, 512])
        qb = s.sb("qb", [P, EX, 2, 2, 256])
        qs = s.sb("qs", [P, 2, 2, 2, 512])
        ksf = s.sb("ksf", [P, 2, 2, 512])
        gg = s.sb("gg", [P, 2, 4, 512])
        v = s.sb("v", [P, VS, 512])
        kt = s.sb("kt", [P, 2, 256])
        st = s.sb("st", [P, 3, 2, P])
        sq, rn = s.sb("sq", [P, 512]), s.sb("rn", [P, 512])
        on = s.sb("on", [P, 2, 4, P])
        cb, cc, ch = s.sb("cb", [P, 512]), s.sb("cc", [P, 2, 512]), s.sb("ch", [P, 512])
        cu, ctmp = s.sb("cu", [P, 2, 514]), s.sb("ctmp", [P, 512])
        cy = s.sb("cy", [P, 2, 512])
        ps_g = s.ps("ps_g", [P, 512])
        ps_l = s.ps("ps_l", [P, 2, 512])
        ps_k = s.ps("ps_k", [P, 512])
        ps_s = s.ps("ps_s", [P, 2, 512])
        ps_o = s.ps("ps_o", [P, 2, 512])

        S = s.sem
        consts_in, consts_set = S("consts_in"), S("consts_set")
        group_in, gr_in = s.sems("group_in", 2), S("gr_in")
        v_in = s.sems("v_in", VS)
        st_in, st_out = S("st_in"), lasting.states
        gate_mm, gate_y, gate_abs, gate_exp, gate_ln, gate_l, cum_done = (S(n) for n in (
            "gate_mm", "gate_y", "gate_abs", "gate_exp", "gate_ln", "gate_l", "cum_done"))
        eb_done, qs_done, gn_scaled = S("eb_done"), S("qs_done"), S("gn_scaled")
        ks_arg, ks_exp, ks_done = S("ks_arg"), S("ks_exp"), S("ks_done")
        r_exp, r_one, r_inv, gg_done = S("r_exp"), S("r_one"), S("r_inv"), S("gg_done")
        lev_arg, lev_exp, lev_mul, lev_mm, lev_put = (S(n) for n in ("lev_arg", "lev_exp", "lev_mul", "lev_mm", "lev_put"))
        k_turned, k_out, kv_mm, st_new = S("k_turned"), S("k_out"), S("kv_mm"), S("st_new")
        inter_done, intra_done = S("inter_done"), S("intra_done")
        o_mm, sq_done, n_mm, n_ln, n_exp, o_norm, o_gate = (S(n) for n in (
            "o_mm", "sq_done", "n_mm", "n_ln", "n_exp", "o_norm", "o_gate"))
        on_st = s.sems("on_st", 2)
        c_in, c_u, c_y, c_out = s.sems("c_in", 3), S("c_u"), S("c_y"), s.sems("c_out", 2)
        cs_out = lasting.conv_states

        def level_blocks(g):
            nt = max(1, GG[g][1] // P)
            found = [(li, list(range(nt))) for li in range(NL)]
            return found + [(NL, list(range(x, min(nt, x + 2)))) for x in range(0, nt, 2)]

        tiles, chunks, group_tiles = [], [], []
        for g, (t0, n) in enumerate(GG):
            m = min(P, n)
            group_tiles.append([])
            for i in range(max(1, n // P)):
                cs = list(range(len(chunks), len(chunks) + m // CHUNK))
                chunks += [(len(tiles), x) for x in range(m // CHUNK)]
                group_tiles[g].append(len(tiles))
                tiles.append((g, i, m, cs))

        def ahead(g):
            todo = [(("gate_sum", g), 5), (("decay", g), 2.5),
                    (("level_arg", g, 0), 1.2)]
            for li in range(NL + 1):
                if li < NL:
                    todo.append((("level_arg", g, li + 1), 1.2))
                todo.append((("level_mul", g, li), 1.2))
                if li:
                    todo.append((("level_put", g, li - 1), 2.4))
                todo.append((("level_product", g, li), 1.2))
                if li == 0:
                    todo.append((("silu_exp", g), 0))
                elif li == 2:
                    todo.append((("silu", g), 3))
            todo.append((("level_put", g, NL), 4.5))
            if g + 1 < NG:
                todo += [(("gate", g + 1), 0), (("gate_log", g + 1), 0)]
            return todo

        first = [it for it, _ in ahead(0)]
        order = [("load", 0), ("load", 1), ("gate", 0), ("gate_log", 0)] + first[:-2] + [("v_in", 0), ("turn", 0), ("kv", 0)] + first[-2:]
        for g in range(NG):
            todo = ahead(g + 1) if g + 1 < NG else []
            places = 4 * len(group_tiles[g])
            share = sum(w for _, w in todo) / places
            spent, place = 0.0, 0

            def fill():
                nonlocal spent, place
                place += 1
                while todo and (spent < share * place or place == places):
                    it, w = todo.pop(0)
                    order.append(it)
                    spent += w
            for j in group_tiles[g]:
                cs, more = tiles[j][3], j + 1 < len(tiles)
                if more:
                    order.append(("v_in", j + 1))
                if j == group_tiles[g][-2:][0] and g + 2 < NG:
                    order.append(("load", g + 2))
                order += [("intra", j), ("inter", cs[0]), ("state", cs[0])]
                fill()
                if len(cs) > 1:
                    order += [("inter", cs[1]), ("state", cs[1])]
                fill()
                order.append(("squares", j))
                if more:
                    order.append(("turn", j + 1))
                fill()
                order.append(("root", j))
                if more:
                    order.append(("kv", j + 1))
                fill()
                order.append(("norm", j))
        FIRST_STREAM = len(chunks) - 1

        def before(c):
            return 2 if c == FIRST_STREAM else c % 2
        inter_no, k = {}, 0
        for c, (ct, cx) in enumerate(chunks):
            if cx != len(tiles[ct][3]) - 1:
                k += 1
                inter_no[c] = k

        bank_no, put_by_group, n_b = {}, {}, 0
        for it in order:
            if it[0] == "level_product":
                _, g, li = it
                for b in level_blocks(g):
                    if b[0] == li:
                        bank_no[(g, b[0], b[1][0])] = n_b
                        n_b += 1
                put_by_group[g] = 2 * n_b
        tiles_before = [group_tiles[g][0] for g in range(NG)]
        lev_no = {(it[1], it[2]): n for n, it in enumerate([x for x in order if x[0] == "level_product"])}
        last_bank = {}
        for (g, li, t), b in bank_no.items():
            last_bank[(g, li)] = max(last_bank.get((g, li), 0), 2 * (b + 1))
        lev_by_no = {n: k for k, n in lev_no.items()}

        def halves(x, g, hs, n):
            y = x[:, :, :n].rearrange("p a (b two h) -> p a b two h", two=2, h=hs)
            return y[:, :, :, 0, :], y[:, :, :, 1, :]

        block = s.stack.enter_context(nc.Block())

        def store_tile(sp, j):
            g, i, m, cs = tiles[j]
            t = GG[g][0] + i * P
            sp.wait_ge(o_gate, j + 1)
            sp.dma_start(mixt_dram[0:512, t:t + m].rearrange("(h p) t -> p h t", p=P), on[:, j % 2, :, :m]).then_inc(on_st[j % 2], 16)

        @block.sync
        def _(sp):
            for dst, src in ((ident[:], a["ident"]), (ones[:], a["ones"]), (masks[:], a["level_masks"]),
                             (starts[:], a["chunk_start"][:, :512]), (wgu[:], a["w_gate_up"][0])):
                sp.dma_start(dst, src).then_inc(consts_in, 16)
            with nc.allow_non_contiguous_dma(reason="a few vectors by partition"):
                sp.dma_start(bg[:], a["b_gate"][0].rearrange("(a p) -> p a", p=P)).then_inc(consts_in, 16)
                sp.dma_start(gn[:], a["gla_norm_g"][0].rearrange("(a p) -> p a", p=P)).then_inc(consts_in, 16)
                for x in range(2):
                    sp.dma_start(cw[:, x, :], a["conv_w"][0][:, P * x:P * x + P].rearrange("w p -> p w")).then_inc(consts_in, 16)
            sp.dma_start(st[:, 2, :, :], a["state_gla"][0, 0].rearrange("(a two) k v -> (two k) a v", two=2)).then_inc(st_in, 16)
            for it in order:
                if it[0] == "load":
                    g = it[1]
                    t0, n = GG[g]
                    sl_ = g % 2
                    if g >= 2:
                        sp.wait_ge(ks_done, g - 1)
                        sp.wait_ge(lev_mm, last_bank[(g - 2, NL)])
                        sp.wait_ge(qs_done, 2 * (g - 1))
                        sp.wait_ge(gate_mm, 2 * (g - 1))
                    sp.dma_start(glow[:, sl_, :n], zt_dram[Z_GL:Z_GL + RANK, t0:t0 + n]).then_inc(group_in[sl_], 16)
                    sp.dma_start(gq[:, sl_, :, :n], zt_dram[Z_GQ:Z_GQ + 256, t0:t0 + n].rearrange("(a p) t -> p a t", p=P)).then_inc(group_in[sl_], 16)
                    sp.dma_start(gk[:, sl_, :, :n], zt_dram[Z_GK:Z_GK + 256, t0:t0 + n].rearrange("(a p) t -> p a t", p=P)).then_inc(group_in[sl_], 16)
                    if g >= 1:
                        sp.wait_ge(gg_done, g)
                    sp.dma_start(gr[:, :, :n], zt_dram[Z_GR:Z_GR + 512, t0:t0 + n].rearrange("(a p) t -> p a t", p=P)).then_inc(gr_in, 16)
                elif it[0] == "v_in":
                    j = it[1]
                    g, i, m, cs = tiles[j]
                    t = GG[g][0] + i * P
                    if j >= VS:
                        sp.wait_ge(o_mm, j - VS + 1)
                    sp.dma_start(v[:m, j % VS, :], gv_dram[t:t + m, :]).then_inc(v_in[j % VS], 16)
                elif it[0] == "norm":
                    store_tile(sp, it[1])
            sp.wait_ge(st_new, len(chunks))
            sp.dma_start(a["gla_state_p"][0, 0].rearrange("(a two) k v -> (two k) a v", two=2), st[:, FIRST_STREAM % 2, :, :]).then_inc(st_out, 16)
            sp.dma_start(a["gla_state_s"][0, 0].rearrange("(a two) k v -> (two k) a v", two=2), st[:, (FIRST_STREAM + 1) % 2, :, :]).then_inc(st_out, 16)
            sp.wait_ge(st_out, 32)
            for q in range(2):
                sp.wait_ge(on_st[q], 16 * len([j for j in range(len(tiles)) if j % 2 == q]))

        @block.scalar
        def _(act):
            act.preload_act_table_set("natural_log_exp_and_others")
            act.wait_ge(consts_set, 5)
            act.wait_ge(consts_in, 144)
            for step, *at in order:
                if step == "gate":
                    g = at[0]
                    n = GG[g][1]
                    if g:
                        act.wait_ge(cum_done, 2 * g)
                    for p in range(2):
                        act.wait_ge(gate_mm, 2 * g + p + 1)
                        act.activation(gy[:, p, :n], ps_g[:, :n], ACT.Identity, bias=bg[:, p:p + 1]).then_inc(gate_y, 1)
                    act.wait_ge(gate_y, 2 * g + 2)
                    if g:
                        act.wait_ge(gate_l, g)
                    act.activation(ga[:, :, :n], gy[:, :, :n], ACT.Abs).then_inc(gate_abs, 1)
                elif step == "gate_log":
                    g = at[0]
                    n = GG[g][1]
                    act.wait_ge(gate_abs, g + 1)
                    act.activation(ga[:, :, :n], ga[:, :, :n], ACT.Exp, scale=-1.0).then_inc(gate_exp, 1)
                    act.wait_ge(gate_exp, g + 1)
                    act.activation(ga[:, :, :n], ga[:, :, :n], ACT.Ln, bias=1.0).then_inc(gate_ln, 1)
                elif step == "gate_sum":
                    g = at[0]
                    n, q = GG[g][1], g % 2
                    act.wait_ge(cum_done, 2 * (g + 1))
                    if g >= 2:
                        act.wait_ge(st_new, tiles[tiles_before[g - 1]][3][0])
                    act.activation(eb[:, q, :, :n], bc[:, q, :, :n], ACT.Exp, scale=1.0 / TAU).then_inc(eb_done, 1)
                    act.wait_ge(ks_arg, g + 1)
                    act.activation(ksf[:, q, :, :n], ksf[:, q, :, :n], ACT.Exp, scale=1.0 / TAU).then_inc(ks_exp, 1)
                elif step == "silu_exp":
                    g = at[0]
                    n, q = GG[g][1], g % 2
                    act.wait_ge(gr_in, 16 * (g + 1))
                    if g >= 2:
                        act.wait_ge(o_gate, tiles_before[g - 1])
                    act.activation(gg[:, q, :, :n], gr[:, :, :n], ACT.Exp, scale=-1.0).then_inc(r_exp, 1)
                    act.wait_ge(r_exp, g + 1)
                    act.activation(gg[:, q, :, :n], gg[:, q, :, :n], ACT.Ln, bias=1.0).then_inc(r_one, 1)
                    act.wait_ge(r_one, g + 1)
                    act.activation(gg[:, q, :, :n], gg[:, q, :, :n], ACT.Exp, scale=-1.0).then_inc(r_inv, 1)
                elif step == "level_arg" and at[1] < NL:
                    g, li = at
                    n, x = GG[g][1], lev_no[(g, li)]
                    act.wait_ge(lev_arg, 2 * (x - g + 1))
                    act.activation(ex[:, x % EX, :, :n], ex[:, x % EX, :, :n], ACT.Exp, scale=1.0 / TAU).then_inc(lev_exp, 1)
                elif step == "turn":
                    j = at[0]
                    m = tiles[j][2]
                    act.wait_ge(k_turned, j + 1)
                    if j >= 2:
                        act.wait_ge(kv_mm, tiles[j - 2][3][-1] + 1)
                    act.activation(kt[:m, j % 2, :], ps_k[:m, 0:256], ACT.Copy).then_inc(k_out, 1)
                elif step == "squares":
                    j = at[0]
                    m = tiles[j][2]
                    act.wait_ge(o_mm, j + 1)
                    if j:
                        act.wait_ge(n_mm, j)
                    act.activation(sq[:, :4 * m].rearrange("p (e x) -> p e x", e=2), ps_o[:, :, :2 * m], ACT.Square).then_inc(sq_done, 1)
                elif step == "root":
                    j = at[0]
                    m = tiles[j][2]
                    act.wait_ge(n_mm, j + 1)
                    if j:
                        act.wait_ge(o_norm, 2 * j)
                    act.activation(rn[:, :4 * m], ps_g[:, :4 * m], ACT.Ln, scale=QSCALE * QSCALE / DV, bias=eps[:, :]).then_inc(n_ln, 1)
                    act.wait_ge(n_ln, j + 1)
                    act.activation(rn[:, :4 * m], rn[:, :4 * m], ACT.Exp, scale=-0.5).then_inc(n_exp, 1)

        @block.vector
        def _(dve):
            dve.memset(eps[:], LN_EPS).then_inc(consts_set, 1)
            dve.memset(st[:, 0, :, :], 0.0).then_inc(consts_set, 1)
            dve.memset(att[:], 0.0).then_inc(consts_set, 1)
            dve.wait_ge(consts_in, 144)
            dve.tensor_scalar(gn[:], gn[:], QSCALE, None, ALU.mult).then_inc(gn_scaled, 1)
            for step, *at in order:
                if step == "gate_sum":
                    g = at[0]
                    n, q = GG[g][1], g % 2
                    dve.wait_ge(gate_ln, g + 1)
                    dve.scalar_tensor_tensor(out=gy[:, :, :n], in0=gy[:, :, :n], scalar=0.0, in1=ga[:, :, :n], op0=ALU.min, op1=ALU.subtract)\
                       .then_inc(gate_l, 1)
                    dve.wait_ge(gate_l, g + 1)
                    for p in range(2):
                        dve.tensor_tensor_scan(bc[:, q, p, :n], starts[:, :n], gy[:, p, :n], 0.0, ALU.mult, ALU.add).then_inc(cum_done, 1)
                    dve.wait_ge(cum_done, 2 * g + 2)
                    b4 = bc[:, q, :, :n].rearrange("p a (c t) -> p a c t", t=CHUNK)
                    k4 = ksf[:, q, :, :n].rearrange("p a (c t) -> p a c t", t=CHUNK)
                    if g >= 2:
                        dve.wait_ge(k_turned, tiles_before[g - 1])
                    dve.tensor_tensor(k4, b4[:, :, :, CHUNK - 1:CHUNK].to_broadcast([P, 2, n // CHUNK, CHUNK]), b4, ALU.subtract).then_inc(ks_arg, 1)
                elif step == "decay":
                    g = at[0]
                    n, q = GG[g][1], g % 2
                    dve.wait_ge(eb_done, g + 1)
                    if g >= 2:
                        dve.wait_ge(o_mm, tiles_before[g - 1])
                    dve.wait_ge(group_in[q], 48 * (g // 2 + 1))
                    dve.wait_ge(consts_set, 5)
                    for e in range(2):
                        r = slice(64 * e, 64 * e + 64)
                        dve.tensor_tensor(qs[r, q, :, e, :n], eb[r, q, :, :n], gq[r, q, :, :n], ALU.mult).then_inc(qs_done, 1)
                    dve.wait_ge(ks_exp, g + 1)
                    dve.tensor_tensor(ksf[:, q, :, :n], ksf[:, q, :, :n], gk[:, q, :, :n], ALU.mult).then_inc(ks_done, 1)
                elif step == "silu":
                    g = at[0]
                    n, q = GG[g][1], g % 2
                    dve.wait_ge(r_inv, g + 1)
                    dve.wait_ge(gn_scaled, 1)
                    for h in range(HEADS):
                        last = dve.scalar_tensor_tensor(out=gg[:, q, h, :n], in0=gr[:, h, :n], scalar=gn[:, h:h + 1], in1=gg[:, q, h, :n],
                                                        op0=ALU.mult, op1=ALU.mult)
                    last.then_inc(gg_done, 1)
                elif step == "level_arg" and at[1] < NL:
                    g, li = at
                    n, x, q = GG[g][1], lev_no[(g, li)], g % 2
                    hs = LEVELS[li]
                    b1, b2 = halves(bc[:, q], g, hs, n)
                    e1, e2 = halves(ex[:, x % EX], g, hs, n)
                    cut = b1[:, :, :, hs - 1:hs].to_broadcast([P, 2, n // (2 * hs), hs])
                    if x >= EX:
                        dve.wait_ge(lev_mm, last_bank[lev_by_no[x - EX]])
                    dve.tensor_tensor(e1, cut, b1, ALU.subtract).then_inc(lev_arg, 1)
                    dve.tensor_tensor(e2, b2, cut, ALU.subtract).then_inc(lev_arg, 1)
                elif step == "level_mul" and at[1] < NL:
                    g, li = at
                    n, x, q = GG[g][1], lev_no[(g, li)], g % 2
                    hs = LEVELS[li]
                    dve.wait_ge(lev_exp, x - g + 1)
                    e1, e2 = halves(ex[:, x % EX], g, hs, n)
                    k1, _ = halves(gk[:, q], g, hs, n)
                    _, q2 = halves(gq[:, q], g, hs, n)
                    dve.tensor_tensor(e1, e1, k1, ALU.mult).then_inc(lev_mul, 1)
                    dve.wait_ge(consts_set, 5)
                    if x >= EX:
                        dve.wait_ge(lev_mm, last_bank[lev_by_no[x - EX]])
                    for e in range(2):
                        r = slice(64 * e, 64 * e + 64)
                        dve.tensor_tensor(qb[r, x % EX, :, e, :n // 2].rearrange("p a (b h) -> p a b h", h=hs), e2[r], q2[r], ALU.mult).then_inc(lev_mul, 1)
                elif step == "level_put":
                    g, li = at
                    n = GG[g][1]
                    if li == 0:
                        dve.wait_ge(consts_set, 5)
                    if g >= 2 and li == 0:
                        dve.wait_ge(o_mm, tiles_before[g - 1])
                    for (lj, ts) in level_blocks(g):
                        if lj != li:
                            continue
                        b, w, nt = bank_no[(g, li, ts[0])], min(P, n), len(ts)
                        for e in range(2):
                            dve.wait_ge(lev_mm, 2 * b + e + 1)
                            if li == NL and e == 0:
                                dve.wait_ge(lev_put, 2 * b)
                            if li < NL:
                                dst = att[:w, g % 2, e, ts[0]:ts[0] + nt, :, :w].rearrange("p a h t -> p (a h) t")
                                hs, wo = LEVELS[li], w // 2
                                nb = w // (2 * hs)
                                for_pairs = dst.rearrange("p x (b two h) -> p x b two h", two=2, h=hs)[:, :, :, 1, :]
                                data = ps_l[:w, e, :2 * nt * wo].rearrange("p (x b h) -> p x b h", x=2 * nt, h=hs)
                                mk = masks[:w, 64 * li:64 * li + wo].bitcast(I32).rearrange("p (b h) -> p b h", h=hs).unsqueeze(1).to_broadcast([w, 2 * nt, nb, hs])
                            else:
                                for_pairs = att[:w, g % 2, :, ts[0]:ts[0] + nt, e, :w]
                                data = ps_l[:w, e, :2 * nt * w].rearrange("p (x a t) -> p x a t", x=2, a=nt)
                                mk = masks[:w, 64 * NL:64 * NL + w].bitcast(I32).unsqueeze(1).unsqueeze(1).to_broadcast([w, 2, nt, w])
                            dve.copy_predicated(for_pairs, mk, data).then_inc(lev_put, 1)
                elif step == "state":
                    c = at[0]
                    ct, x = chunks[c]
                    g, i, m, cs = tiles[ct]
                    q, end = g % 2, i * P + x * CHUNK + CHUNK - 1
                    dve.wait_ge(kv_mm, c + 1)
                    dve.wait_ge(consts_set, 5)
                    if c == FIRST_STREAM:
                        dve.wait_ge(st_in, 16)
                    if c:
                        dve.wait_ge(st_new, c)
                        pt, px = chunks[c - 1]
                        if px == len(tiles[pt][3]) - 1:
                            dve.wait_ge(o_mm, pt + 1)
                        else:
                            dve.wait_ge(inter_done, inter_no[c - 1])
                    for p in range(2):
                        ins = dve.scalar_tensor_tensor(out=st[:, (c + 1) % 2, p, :], in0=st[:, before(c), p, :], scalar=eb[:, q, p, end:end + 1],
                                                       in1=ps_s[:, c % 2, P * p:P * p + P], op0=ALU.mult, op1=ALU.add)
                    ins.then_inc(st_new, 1)
                elif step == "norm":
                    j = at[0]
                    g, i, m, cs = tiles[j]
                    q = g % 2
                    dve.wait_ge(n_exp, j + 1)
                    if j >= 2:
                        dve.wait_ge(on_st[j % 2], 16 * (j // 2))
                    for e in range(2):
                        dve.tensor_tensor(on[:, j % 2, 2 * e:2 * e + 2, :m], ps_o[:, e, :2 * m].rearrange("p (a t) -> p a t", a=2),
                                          rn[:, 2 * m * e:2 * m * e + 2 * m].rearrange("p (a t) -> p a t", a=2), ALU.mult).then_inc(o_norm, 1)
                    dve.wait_ge(o_norm, 2 * j + 2)
                    dve.tensor_tensor(on[:, j % 2, :, :m], on[:, j % 2, :, :m], gg[:, q, :, i * P:i * P + m], ALU.mult).then_inc(o_gate, 1)

        @block.tensor
        def _(pe):
            pe.wait_ge(consts_in, 144)
            gates_seen = tiles_seen = 0
            for step, *at in order:
                if step == "gate":
                    g = at[0]
                    n = GG[g][1]
                    pe.wait_ge(group_in[g % 2], 48 * (g // 2 + 1))
                    for p in range(2):
                        if gates_seen:
                            pe.wait_ge(gate_y, gates_seen)
                        if tiles_seen:
                            pe.wait_ge(n_ln, tiles_seen)
                        pe.matmul(ps_g[:, :n], wgu[:, P * p:P * p + P], glow[:, g % 2, :n], start=True, stop=True).then_inc(gate_mm, 1)
                        gates_seen += 1
                elif step == "level_product":
                    g, li = at
                    x = lev_no[(g, li)]
                    w = min(P, GG[g][1])
                    if li < NL:
                        pe.wait_ge(lev_mul, 3 * (x - g + 1))
                    for (lj, ts) in level_blocks(g):
                        if lj != li:
                            continue
                        b = bank_no[(g, li, ts[0])]
                        for e in range(2):
                            if b:
                                pe.wait_ge(lev_put, 2 * b - 1 + e)
                            for n, t in enumerate(ts):
                                cols = slice(t * P, t * P + w)
                                if li < NL:
                                    wo = w // 2
                                    mm = pe.matmul(ps_l[:w, e, n * w:n * w + w], ex[:, x % EX, e, cols], qb[:, x % EX, e, :, t * wo:t * wo + wo],
                                                   start=n == 0, stop=n == len(ts) - 1, skip_group_check=True)
                                    continue
                                r = slice(64 * e, 64 * e + 64)
                                for pr in range(2):
                                    at_ = (pr * len(ts) + n) * w
                                    mm = pe.matmul(ps_l[:w, e, at_:at_ + w], gk[r, g % 2, pr, cols], gq[r, g % 2, pr, cols],
                                                   start=n + pr == 0, stop=n + pr == len(ts), skip_group_check=True)
                            mm.then_inc(lev_mm, 1)
                elif step == "turn":
                    j = at[0]
                    g, i, m, cs = tiles[j]
                    pe.wait_ge(ks_done, g + 1)
                    if j:
                        pe.wait_ge(k_out, j)
                    for p in range(2):
                        mm = pe.transpose(ps_k[:m, P * p:P * p + P], ksf[:, g % 2, p, i * P:i * P + m], ident[:, :])
                    mm.then_inc(k_turned, 1)
                elif step == "kv":
                    j = at[0]
                    g, i, m, cs = tiles[j]
                    pe.wait_ge(v_in[j % VS], 16 * (j // VS + 1))
                    pe.wait_ge(k_out, j + 1)
                    for x, c in enumerate(cs):
                        r = slice(64 * x, 64 * x + 64)
                        if c >= 2:
                            pe.wait_ge(st_new, c - 1)
                        for p in range(2):
                            for e in range(2):
                                h = 2 * p + e
                                mm = pe.matmul(ps_s[64 * e:64 * e + 64, c % 2, P * p:P * p + P], kt[r, j % 2, 64 * h:64 * h + 64],
                                               v[r, j % VS, P * h:P * h + P], start=True, stop=True, skip_group_check=True)
                        mm.then_inc(kv_mm, 1)
                elif step == "intra":
                    j = at[0]
                    g, i, m, cs = tiles[j]
                    pe.wait_ge(v_in[j % VS], 16 * (j // VS + 1))
                    pe.wait_ge(lev_put, put_by_group[g])
                    if j:
                        pe.wait_ge(o_norm, 2 * j)
                    for h in range(HEADS):
                        mm = pe.matmul(ps_o[:, h // 2, (h % 2) * m:(h % 2) * m + m], v[:m, j % VS, P * h:P * h + P], att[:m, g % 2, h // 2, i, h % 2, :m],
                                       start=h % 2 == 0, stop=False, skip_group_check=True)
                    if m == 64:
                        mm.then_inc(intra_done, 1)
                        pe.wait_ge(intra_done, 1)
                elif step == "inter":
                    c = at[0]
                    j, x = chunks[c]
                    g, i, m, cs = tiles[j]
                    q = g % 2
                    pe.wait_ge(qs_done, 2 * (g + 1))
                    if c == FIRST_STREAM:
                        pe.wait_ge(st_in, 16)
                    elif c:
                        pe.wait_ge(st_new, c)
                    else:
                        pe.wait_ge(consts_set, 5)
                    cols = slice(i * P + x * CHUNK, i * P + x * CHUNK + CHUNK)
                    for pr in range(2):
                        mm = pe.matmul(ps_o[:, pr, :2 * m].rearrange("p (e t) -> p e t", e=2)[:, :, x * CHUNK:x * CHUNK + CHUNK], st[:, before(c), pr, :],
                                       qs[:, q, pr, :, cols], start=False, stop=x == len(cs) - 1, skip_group_check=True)
                    mm.then_inc(o_mm if x == len(cs) - 1 else inter_done, 1)
                elif step == "squares":
                    j = at[0]
                    m = tiles[j][2]
                    pe.wait_ge(sq_done, j + 1)
                    pe.wait_ge(gate_y, gates_seen)
                    if j:
                        pe.wait_ge(n_ln, j)
                    pe.matmul(ps_g[:, :4 * m], ones[:, :], sq[:, :4 * m], start=True, stop=True).then_inc(n_mm, 1)
                    tiles_seen = j + 1

        pieces = [(x, t, n) for x in range(2) for t, n in GG]

        @block.gpsimd
        def _(pool):
            pool.memset(qs[:], 0.0).then_inc(consts_set, 1)
            pool.memset(qb[:], 0.0).then_inc(consts_set, 1)
            pool.wait_ge(consts_in, 144)
            for k, (x, t, n) in enumerate(pieces):
                first, sl_, cp = t in (0, SEQ), k % 2, P * x
                with nc.allow_non_contiguous_dma(reason="two columns of state"):
                    pool.dma_start(cc[:, sl_, :n], zt_dram[Z_CC + cp:Z_CC + cp + P, t:t + n]).then_inc(c_in[0], 16)
                    pool.dma_start(ch[:, :n], zt_dram[Z_CH + cp:Z_CH + cp + P, t:t + n]).then_inc(c_in[0], 16)
                    pool.dma_start(cb[:, :n], zt_dram[Z_CB + cp:Z_CB + cp + P, t:t + n]).then_inc(c_in[0], 16)
                    if t == SEQ:
                        pool.dma_start(cu[:, sl_, 0:2], a["state_conv"][0, 0][:, cp:cp + P].rearrange("w p -> p w")).then_inc(c_in[1], 16)
                        pool.wait_ge(c_in[1], 16 * (x + 1))
                pool.wait_ge(c_in[0], 48 * (k + 1))
                u = cu[:, sl_, :]
                if t == 0:
                    pool.memset(u[:, 0:2], 0.0).then_inc(c_u, 1)
                elif t != SEQ:
                    pool.tensor_copy(u[:, 0:2], cu[:, 1 - sl_, 512:514]).then_inc(c_u, 1)
                else:
                    pool.engine_nop().then_inc(c_u, 1)
                pool.tensor_tensor(u[:, 2:2 + n], cc[:, sl_, :n], ch[:, :n], ALU.mult).then_inc(c_u, 1)
                pool.wait_ge(c_u, 2 * (k + 1))
                y = cy[:, sl_, :n]
                if k >= 2:
                    pool.wait_ge(c_out[sl_], 16 * (k // 2))
                tmp = ctmp[:, :n]
                steps = [
                    lambda: pool.tensor_scalar(y, u[:, 2:2 + n], cw[:, x, 2:3], None, ALU.mult),
                    lambda: pool.tensor_scalar(tmp, u[:, 0:n], cw[:, x, 0:1], None, ALU.mult),
                    lambda: pool.tensor_tensor(y, y, tmp, ALU.add),
                    lambda: pool.tensor_scalar(tmp, u[:, 1:1 + n], cw[:, x, 1:2], None, ALU.mult),
                    lambda: pool.tensor_tensor(y, y, tmp, ALU.add),
                    lambda: pool.tensor_tensor(y, y, cb[:, :n], ALU.mult),
                ]
                for m, step in enumerate(steps):
                    step().then_inc(c_y, 1)
                    pool.wait_ge(c_y, 6 * k + m + 1)
                pool.dma_start(mixt_dram[768 + cp:768 + cp + P, t:t + n], y).then_inc(c_out[sl_], 16)
                if t + n in (SEQ, T):
                    dst = a["conv_state_p" if t + n == SEQ else "conv_state_s"][0, 0]
                    with nc.allow_non_contiguous_dma(reason="two columns of state"):
                        pool.dma_start(dst[:, cp:cp + P].rearrange("w p -> p w"), u[:, n:n + 2]).then_inc(cs_out, 16)
                    pool.wait_ge(cs_out, 16 * (2 * x + (1 if t + n == SEQ else 2)))
            for q in range(2):
                pool.wait_ge(c_out[q], 16 * len([k for k in range(len(pieces)) if k % 2 == q]))


def phase_sb(nc, a, zt_dram, mixt_dram, k_p, v_p, k_s, v_s):
    QG = 512
    NG = SEQ // QG
    SCALE = SBD ** -0.5
    ZB, AB = 3, 3
    SIG, AW, AT = 4, 3, 3
    RAW = 5
    TURN_LAG, WEIGH_LAG = 6, 8
    s = Scope(nc, "p3")
    with s:
        ident = s.sb("ident", [P, P])
        identb = s.sb("identb", [P, P], mybir.dt.bfloat16)
        causal = s.sb("causal", [P, P])
        causalb = s.sb("causalb", [P, P], mybir.dt.bfloat16)
        raw = s.sb("raw", [P, RAW, 512])
        qh, ql = s.sb("qh", [P, 2, T], F32R), s.sb("ql", [P, 2, T], F32R)
        kh, kl = s.sb("kh", [P, 2, SEQ], F32R), s.sb("kl", [P, 2, SEQ], F32R)
        vh, vl = s.sb("vh", [P, SEQ // P, 256], F32R), s.sb("vl", [P, SEQ // P, 256], F32R)
        zero = s.sb("zero", [P, 512])
        keep = s.sb("keep", [P, 4, SEQ + 1])
        sg, tg = s.sb("sg", [P, SIG, 512]), s.sb("tg", [P, SIG, 512])
        aw = s.sb("aw", [P, AW, 4, 512])
        ath, atl = s.sb("ath", [P, AT, 512], F32R), s.sb("atl", [P, AT, 512], F32R)
        ob = s.sb("ob", [64, 2, 512])
        ps_z = s.ps("ps_z", [P, ZB, 512])
        ps_a = s.ps("ps_a", [P, AB, 512])
        ps_o = s.ps("ps_o", [64, 2, 512])

        consts_in, consts_done, keep_set = s.sem("consts_in"), s.sem("consts_done"), s.sem("keep_set")
        raw_in = s.sems("raw_in", RAW)
        kturned = s.sem("kturned")
        prep_hi, prep_lo = s.sem("prep_hi"), s.sem("prep_lo")
        z_done, sig_done, scan_done = s.sem("z_done"), s.sem("sig_done"), s.sem("scan_done")
        a_dve, a_pool = s.sem("a_dve"), s.sem("a_pool")
        a_turned, a_hi, a_lo, av_done = s.sem("a_turned"), s.sem("a_hi"), s.sem("a_lo"), s.sem("av_done")
        o_out = s.sem("o_out")
        o_st = s.sems("o_st", 2)

        def prep_prompt(g):
            items = [("q", p, g * QG, QG, None) for p in range(2)]
            items += [("k", t, P, k_p[t * P:(t + 1) * P, :], v_p[t * P:(t + 1) * P, :]) for t in range(4 * g, 4 * g + 4)]
            return items

        ck = a["cache_sb_k"][0, 0].rearrange("t h d -> t (h d)")
        cv = a["cache_sb_v"][0, 0].rearrange("t h d -> t (h d)")
        prep_stream = [("q", p, SEQ, DEC, None) for p in range(2)]
        prep_stream += [("k", t, P, ck[t * P:(t + 1) * P, :], cv[t * P:(t + 1) * P, :]) for t in range(4)]
        prep_stream += [("k", 4, DEC, k_s[:, :], v_s[:, :])]

        units = []

        def add_units(q0, tiles, chunks, tag, prepared):
            first = len(units)
            for h in range(SBH):
                for n, c in enumerate(chunks):
                    diag = n == 0
                    if tag == "prompt":
                        widths = [P * (i + 1) if diag else 512 for i in range(4)]
                        kbs = [(c * 512 + P * b, P, 4 * c + b, b if diag else 0) for b in range(4)]
                        masked = [P * i for i in range(4)]
                    else:
                        widths = [DEC if diag else 512]
                        kbs = [(PAST, DEC, 4, 0)] if diag else [(P * b, P, b, 0) for b in range(4)]
                        masked = [0]
                    units.append(dict(h=h, q0=q0, tiles=tiles, k0=c * 512, widths=widths, kbs=kbs, diag=diag, masked=masked,
                                      first=diag, last=n == len(chunks) - 1, width=sum(m for _, m in tiles), prep=prepared))
            return range(first, len(units))

        plan = []
        n_prep = n_k = 0

        def add_prep(item):
            nonlocal n_prep, n_k
            plan.append(("prep", item, n_prep, n_k))
            n_prep += 1
            n_k += item[0] == "k"

        def add_slots(slots, ahead):
            n = 0
            while n < len(slots) + WEIGH_LAG + 1:
                def lagged(lag, what):
                    x = slots[n - lag] if 0 <= n - lag < len(slots) else None
                    return x if x is not None and x[1] < len(units[x[0]][what]) else None
                score, turn, weigh_ = lagged(0, "tiles"), lagged(TURN_LAG, "kbs"), lagged(WEIGH_LAG, "kbs")
                done = lagged(WEIGH_LAG + 1, "kbs")
                out = done[0] if done and units[done[0]]["last"] and done[1] == len(units[done[0]]["kbs"]) - 1 else None
                plan.append(("slot", score, turn, weigh_, out))
                if n in ahead:
                    add_prep(ahead[n])
                n += 1

        for it in prep_prompt(0):
            add_prep(it)
        slots, ahead, prepared = [], {}, n_prep
        for g in range(NG):
            us = add_units(g * QG, [(P * i, P) for i in range(4)], list(range(g, -1, -1)), "prompt", prepared)
            if g + 1 < NG:
                items = prep_prompt(g + 1)
                ahead.update({len(slots) + 2 * i: it for i, it in enumerate(items)})
                prepared += len(items)
            slots += [(u, i) for u in us for i in range(4)]
        add_slots(slots, ahead)
        for it in prep_stream:
            add_prep(it)
        add_slots([(u, i) for u in add_units(SEQ, [(0, DEC)], [1, 0], "stream", n_prep) for i in range(max(1, len(units[u]["kbs"])))], {})

        n_z = n_a = n_o = 0
        for u in units:
            u["z0"], u["a0"], u["o"] = n_z, n_a, n_o
            n_z += len(u["tiles"])
            n_a += len(u["kbs"])
            n_o += u["last"]
        for n, u in enumerate(units):
            u["turned_before"] = units[n - AW + 1]["a0"] if n >= AW else 0
        key_bank, block_bank, users = {}, {}, []
        for it in plan:
            if it[0] == "prep" and it[1][0] == "k":
                key_bank[it[3]] = len(users)
                users.append(("key", it[2]))
            elif it[0] == "slot" and it[2]:
                ai = units[it[2][0]]["a0"] + it[2][1]
                block_bank[ai] = len(users)
                users.append(("block", ai))

        def wait_bank(eng, b):
            if b >= AB:
                kind, n = users[b - AB]
                if kind == "key":
                    eng.wait_ge(prep_lo, 2 * n + 1)
                else:
                    eng.wait_ge(a_lo, n + 1)

        on_pool = [z % 2 == 1 for z in range(n_z)]
        pool_before = [sum(on_pool[:z]) for z in range(n_z + 1)]
        keep_reader, readers = {}, []
        for u in units:
            for i in range(len(u["tiles"])):
                z, k0, w = u["z0"] + i, u["k0"], u["widths"][i]
                hits = [r[0] for r in readers if r[1] == i and r[2] < k0 + w and k0 < r[3]]
                keep_reader[z] = max(hits) if hits else None
                readers.append((z, i, k0 + 1, k0 + w + 1))

        def wait_weights(eng, z):
            if z - pool_before[z + 1] + 1 > 0:
                eng.wait_ge(a_dve, z + 1 - pool_before[z + 1])
            if pool_before[z + 1]:
                eng.wait_ge(a_pool, pool_before[z + 1])

        block = s.stack.enter_context(nc.Block())

        @block.sync
        def _(sp):
            sp.dma_start(ident[:], a["ident"]).then_inc(consts_in, 16)
            sp.dma_start(causal[:], a["causal"]).then_inc(consts_in, 16)
            items = [it[1] for it in plan if it[0] == "prep"]

            def load(n):
                kind, *w = items[n]
                if kind == "q":
                    p, t0, cnt, _x = w
                    for x in (0, cnt // 2):
                        sp.dma_start(raw[:, n % RAW, x:x + cnt // 2],
                                     zt_dram[Z_SQ + P * p:Z_SQ + P * (p + 1), t0 + x:t0 + x + cnt // 2]).then_inc(raw_in[n % RAW], 16)
                else:
                    t, m, ks, vs = w
                    sp.dma_start(raw[:m, n % RAW, 0:256], ks).then_inc(raw_in[n % RAW], 16)
                    sp.dma_start(raw[:m, n % RAW, 256:512], vs).then_inc(raw_in[n % RAW], 16)

            for n in range(RAW):
                load(n)
            for it in plan:
                if it[0] == "prep":
                    n = it[2]
                    if n + RAW < len(items):
                        sp.wait_ge(prep_lo, 2 * (n + 1))
                        load(n + RAW)
                elif it[4] is not None:
                    u = units[it[4]]
                    sp.wait_ge(o_out, u["o"] + 1)
                    sp.dma_start(mixt_dram[512 + 64 * u["h"]:576 + 64 * u["h"], u["q0"]:u["q0"] + u["width"]],
                                 ob[:, u["o"] % 2, :u["width"]]).then_inc(o_st[u["o"] % 2], 16)
            for q in range(2):
                sp.wait_ge(o_st[q], 16 * len([o for o in range(n_o) if o % 2 == q]))

        def prep_dests(kind, w, nk):
            if kind == "q":
                p, t0, cnt, _x = w
                half = cnt // 2
                return [(qh[:, p, t0 + x:t0 + x + half], ql[:, p, t0 + x:t0 + x + half], ("raw", P, x, half)) for x in (0, half)]
            t, m, ks, vs = w
            return [
                (kh[:, :, t * P:t * P + m], kl[:, :, t * P:t * P + m], ("psum", m)),
                (vh[:m, t, :], vl[:m, t, :], ("raw", m, 256, 256)),
            ]

        def prep_source(src, n, nk):
            if src[0] == "psum":
                return ps_a[:, key_bank[nk] % AB, 0:256].rearrange("p (a t) -> p a t", a=2)[:, :, :src[1]]
            return raw[:src[1], n % RAW, src[2]:src[2] + src[3]]

        @block.scalar
        def _(act):
            act.wait_ge(consts_in, 32)
            act.activation(identb[:], ident[:], ACT.Copy).then_inc(consts_done, 1)
            act.activation(causalb[:], causal[:], ACT.Copy).then_inc(consts_done, 1)
            for it in plan:
                if it[0] == "prep":
                    _, (kind, *w), n, nk = it
                    act.wait_ge(raw_in[n % RAW], 32 * (n // RAW + 1))
                    for hi, lo, src in prep_dests(kind, w, nk):
                        if src[0] == "psum":
                            act.wait_ge(kturned, nk + 1)
                        act.activation(hi, prep_source(src, n, nk), ACT.Copy).then_inc(prep_hi, 1)
                    continue
                _, score, turn, _, out = it
                if score:
                    u, i = units[score[0]], score[1]
                    z, m, w = u["z0"] + i, u["tiles"][i][1], u["widths"][i]
                    act.wait_ge(z_done, z + 1)
                    if z >= SIG:
                        wait_weights(act, z - SIG)
                    act.activation(tg[:m, z % SIG, :w], ps_z[:m, z % ZB, :w], ACT.Sigmoid, scale=-SCALE).then_inc(sig_done, 1)
                    act.activation(sg[:m, z % SIG, :w], ps_z[:m, z % ZB, :w], ACT.Sigmoid, scale=SCALE).then_inc(sig_done, 1)
                if turn:
                    u, i = units[turn[0]], turn[1]
                    ai = u["a0"] + i
                    k0, kn, vt, i0 = u["kbs"][i]
                    c0, c1 = P * i0, u["width"]
                    act.wait_ge(a_turned, ai + 1)
                    if ai >= AT:
                        act.wait_ge(av_done, ai - AT + 1)
                    act.activation(ath[:kn, ai % AT, c0:c1], ps_a[:kn, block_bank[ai] % AB, c0:c1], ACT.Copy).then_inc(a_hi, 1)
                if out is not None:
                    u = units[out]
                    act.wait_ge(av_done, u["a0"] + len(u["kbs"]))
                    if u["o"] >= 2:
                        act.wait_ge(o_st[u["o"] % 2], 16 * (u["o"] // 2))
                    act.activation(ob[:, u["o"] % 2, :u["width"]], ps_o[:, u["o"] % 2, :u["width"]], ACT.Copy).then_inc(o_out, 1)

        @block.vector
        def _(dve):
            dve.memset(keep[:], 1.0).then_inc(keep_set, 1)
            dve.memset(zero[:], 0.0).then_inc(keep_set, 1)
            dve.wait_ge(keep_set, 2)
            hn = 0
            for it in plan:
                if it[0] == "prep":
                    _, (kind, *w), n, nk = it
                    for hi, lo, src in prep_dests(kind, w, nk):
                        hn += 1
                        dve.wait_ge(prep_hi, hn)
                        dve.tensor_tensor(lo, prep_source(src, n, nk), hi.bitcast(F32), ALU.subtract).then_inc(prep_lo, 1)
                    continue
                _, score, turn, _, _ = it
                if score:
                    cur, i = score
                    u = units[cur]
                    z, m, w, k0 = u["z0"] + i, u["tiles"][i][1], u["widths"][i], u["k0"]
                    dve.wait_ge(sig_done, 2 * z + 1)
                    if z >= 1:
                        dve.wait_ge(scan_done, z)
                    read = keep_reader[z]
                    if read is not None and pool_before[read + 1]:
                        dve.wait_ge(a_pool, pool_before[read + 1])
                    dve.tensor_tensor_scan(keep[:m, i, k0:k0 + w][:, ::-1], tg[:m, z % SIG, :w][:, ::-1], zero[:m, :w],
                                           1.0 if u["first"] else keep[:m, i, k0 + w:k0 + w + 1], ALU.mult, ALU.add).then_inc(scan_done, 1)
                    if not on_pool[z]:
                        dve.wait_ge(scan_done, z + 1)
                        dve.wait_ge(sig_done, 2 * z + 2)
                        if u["turned_before"]:
                            dve.wait_ge(a_turned, u["turned_before"])
                        dve.tensor_tensor(aw[:m, cur % AW, i, :w], sg[:m, z % SIG, :w], keep[:m, i, k0 + 1:k0 + w + 1], ALU.mult).then_inc(a_dve, 1)
                if turn:
                    u, i = units[turn[0]], turn[1]
                    ai = u["a0"] + i
                    k0, kn, vt, i0 = u["kbs"][i]
                    c0, c1 = P * i0, u["width"]
                    dve.wait_ge(a_hi, ai + 1)
                    dve.tensor_tensor(atl[:kn, ai % AT, c0:c1], ps_a[:kn, block_bank[ai] % AB, c0:c1], ath[:kn, ai % AT, c0:c1].bitcast(F32),
                                      ALU.subtract).then_inc(a_lo, 1)

        @block.gpsimd
        def _(pool):
            for it in plan:
                if it[0] != "slot" or not it[1]:
                    continue
                cur, i = it[1]
                u = units[cur]
                z, m, w, k0 = u["z0"] + i, u["tiles"][i][1], u["widths"][i], u["k0"]
                if not on_pool[z]:
                    continue
                pool.wait_ge(scan_done, z + 1)
                pool.wait_ge(sig_done, 2 * z + 2)
                if u["turned_before"]:
                    pool.wait_ge(a_turned, u["turned_before"])
                pool.tensor_tensor(aw[:m, cur % AW, i, :w], sg[:m, z % SIG, :w], keep[:m, i, k0 + 1:k0 + w + 1], ALU.mult).then_inc(a_pool, 1)

        def weigh(pe, u, i):
            ai = u["a0"] + i
            k0, kn, vt, i0 = u["kbs"][i]
            c0, c1 = P * i0, u["width"]
            pe.wait_ge(a_lo, ai + 1)
            start = u["first"] and i == 0
            if start and u["o"] >= 2:
                pe.wait_ge(o_out, u["o"] - 1)
            hc = slice(64 * u["h"], 64 * u["h"] + 64)
            mm = split_product(pe, ps_o[:, u["o"] % 2, c0:c1], vh[:kn, vt, hc], vl[:kn, vt, hc], ath[:kn, ai % AT, c0:c1], atl[:kn, ai % AT, c0:c1],
                               start, u["last"] and i == len(u["kbs"]) - 1, skip=True)
            mm.then_inc(av_done, 1)

        @block.tensor
        def _(pe):
            pe.wait_ge(consts_in, 32)
            pe.wait_ge(consts_done, 2)
            for it in plan:
                if it[0] == "prep":
                    _, (kind, *w), n, nk = it
                    if kind == "k":
                        t, m, ks, vs = w
                        pe.wait_ge(raw_in[n % RAW], 32 * (n // RAW + 1))
                        wait_bank(pe, key_bank[nk])
                        for p in range(2):
                            mm = pe.transpose(ps_a[:, key_bank[nk] % AB, P * p:P * p + m], raw[:m, n % RAW, P * p:P * p + P], ident[:m, :m])
                        mm.then_inc(kturned, 1)
                    continue
                _, score, turn, weigh_, _ = it
                if score:
                    u, i = units[score[0]], score[1]
                    z, (o, m), w = u["z0"] + i, u["tiles"][i], u["widths"][i]
                    if i == 0:
                        pe.wait_ge(prep_lo, 2 * u["prep"])
                    if z >= ZB:
                        pe.wait_ge(sig_done, 2 * (z - ZB + 1))
                    pb, pr = 64 * (u["h"] % 2), u["h"] // 2
                    q = slice(u["q0"] + o, u["q0"] + o + m)
                    ks_ = slice(u["k0"], u["k0"] + w)
                    out = ps_z[:m, z % ZB, :w]
                    if u["diag"]:
                        c = u["masked"][i]
                        pe.matmul(out[:, c:c + m], identb[:m, :m], causalb[:m, :m], start=True, stop=False, skip_group_check=True)
                        mm = split_product(pe, out, qh[pb:pb + 64, pr, q], ql[pb:pb + 64, pr, q], kh[pb:pb + 64, pr, ks_], kl[pb:pb + 64, pr, ks_],
                                           False, True, skip=True)
                    else:
                        mm = split_product(pe, out, qh[pb:pb + 64, pr, q], ql[pb:pb + 64, pr, q], kh[pb:pb + 64, pr, ks_], kl[pb:pb + 64, pr, ks_], True, True)
                    mm.then_inc(z_done, 1)
                if turn:
                    u, i = units[turn[0]], turn[1]
                    ai = u["a0"] + i
                    k0, kn, vt, i0 = u["kbs"][i]
                    if i == 0:
                        wait_weights(pe, u["z0"] + len(u["tiles"]) - 1)
                    wait_bank(pe, block_bank[ai])
                    for qi in range(i0, len(u["tiles"])):
                        o, m = u["tiles"][qi]
                        mm = pe.transpose(ps_a[:kn, block_bank[ai] % AB, o:o + m], aw[:m, turn[0] % AW, qi, k0 - u["k0"]:k0 - u["k0"] + kn], ident[:m, :m])
                    mm.then_inc(a_turned, 1)
                if weigh_:
                    weigh(pe, units[weigh_[0]], weigh_[1])


def phase_out(nc, mixt_dram, w_out, ln_g, ln_b, xn_dram, x1_dram):
    RAW, STAGE, BANKS = 4, 4, 6
    s = Scope(nc, "p4")
    with s:
        g_b = s.sb("g_b", [P, D])
        b_b = s.sb("b_b", [P, D])
        eps = s.sb("eps", [P, 1])
        wst = s.sb("wst", [P, STAGE, D])
        wh = s.sb("wh", [P, KT, D], F32R)
        wl = s.sb("wl", [P, KT, D], F32R)
        raw = s.sb("raw", [P, RAW, NMAX])
        mh = s.sb("mh", [P, 2, KT, NMAX], F32R)
        ml = s.sb("ml", [P, 2, KT, NMAX], F32R)
        res = s.sb("res", [P, 2, D])
        y = s.sb("y", [P, 2, D])
        stats = s.sb("stats", [P, 2, 12])
        mv = s.sb("mv", [P, 2, 2])
        rstd = s.sb("rstd", [P, 2, 1])
        ps = s.ps("ps", [P, BANKS, 512])

        consts_in = s.sem("consts_in")
        eps_set = s.sem("eps_set")
        w_loaded = s.sems("w_loaded", STAGE)
        whi_done, wlo_done = s.sem("whi_done"), s.sem("wlo_done")
        mix_in = s.sems("mix_in", RAW)
        mhi_done, mlo_done = s.sem("mhi_done"), s.sem("mlo_done")
        res_in = s.sems("res_in", 2)
        product_done = s.sem("product_done")
        added = s.sem("added")
        stats_done, var_done, std_done = s.sem("stats_done"), s.sem("var_done"), s.sem("std_done")
        rstd_done, centred, scaled, normed = s.sem("rstd_done"), s.sem("centred"), s.sem("scaled"), s.sem("normed")
        y_out = s.sems("y_out", 2)

        gtiles, n = [], 0
        for (t0, cnt) in GROUPS:
            gtiles.append([(n + i, o, c) for i, (o, c) in enumerate(subtiles(t0, cnt, P))])
            n += len(gtiles[-1])
        last_tile = [gt[-1][0] for gt in gtiles]
        order = [x for k in range(KT) for x in (("w", k), ("mix", 0, k))] + [("first",)]
        for g in range(len(GROUPS)):
            for i, t in enumerate(gtiles[g]):
                order.append(("tile", g, t))
                if i == 0 and g + 1 < len(GROUPS):
                    order += [("mix", g + 1, k) for k in range(KT)]

        block = s.stack.enter_context(nc.Block())

        @block.sync
        def _(sp):
            for what, *a in order:
                if what == "w":
                    k = a[0]
                    if k >= STAGE:
                        sp.wait_ge(wlo_done, k - STAGE + 1)
                    sp.dma_start(wst[:, k % STAGE, :], w_out[k * P:(k + 1) * P, :]).then_inc(w_loaded[k % STAGE], 16)
                elif what == "mix":
                    g, k = a
                    t0, cnt = GROUPS[g]
                    u = g * KT + k
                    if u >= RAW:
                        sp.wait_ge(mlo_done, u - RAW + 1)
                    sp.dma_start(raw[:, u % RAW, :cnt], mixt_dram[k * P:(k + 1) * P, t0:t0 + cnt]).then_inc(mix_in[u % RAW], 16)
                elif what == "first":
                    load_row_broadcast(sp, g_b[:], ln_g, consts_in)
                    load_row_broadcast(sp, b_b[:], ln_b, consts_in)
                else:
                    g, (j, o, c) = a
                    t = GROUPS[g][0] + o
                    if j >= 2:
                        sp.wait_ge(added, 2 * (j - 1))
                    sp.dma_start(res[:c, j % 2, :], xn_dram[t:t + c, :]).then_inc(res_in[j % 2], 16)

        @block.scalar
        def _(act):
            for what, *a in order:
                if what == "w":
                    k = a[0]
                    act.wait_ge(w_loaded[k % STAGE], 16 * (k // STAGE + 1))
                    act.activation(wh[:, k, :], wst[:, k % STAGE, :], ACT.Copy).then_inc(whi_done, 1)
                elif what == "mix":
                    g, k = a
                    cnt, u = GROUPS[g][1], g * KT + k
                    act.wait_ge(mix_in[u % RAW], 16 * (u // RAW + 1))
                    if g >= 2 and k == 0:
                        act.wait_ge(product_done, 2 * (last_tile[g - 2] + 1))
                    act.activation(mh[:, g % 2, k, :cnt], raw[:, u % RAW, :cnt], ACT.Copy).then_inc(mhi_done, 1)
                elif what == "tile":
                    g, (j, o, c) = a
                    act.wait_ge(eps_set, 1)
                    act.wait_ge(var_done, j + 1)
                    if j >= 2:
                        act.wait_ge(centred, j - 1)
                    act.activation(rstd[:c, j % 2, :], mv[:c, j % 2, 1:2], ACT.Sqrt, bias=eps[:c, :]).then_inc(std_done, 1)

        @block.vector
        def _(dve):
            dve.memset(eps[:], LN_EPS).then_inc(eps_set, 1)
            for what, *a in order:
                if what == "w":
                    k = a[0]
                    dve.wait_ge(whi_done, k + 1)
                    dve.tensor_tensor(wl[:, k, :], wst[:, k % STAGE, :], wh[:, k, :].bitcast(F32), ALU.subtract).then_inc(wlo_done, 1)
                elif what == "mix":
                    g, k = a
                    cnt, u = GROUPS[g][1], g * KT + k
                    dve.wait_ge(mhi_done, u + 1)
                    dve.tensor_tensor(ml[:, g % 2, k, :cnt], raw[:, u % RAW, :cnt], mh[:, g % 2, k, :cnt].bitcast(F32),
                                      ALU.subtract).then_inc(mlo_done, 1)
                elif what == "tile":
                    g, (j, o, c) = a
                    sl = j % 2
                    dve.wait_ge(res_in[sl], 16 * (j // 2 + 1))
                    if j >= 2:
                        dve.wait_ge(y_out[sl], 16 * (j // 2))
                    for h in range(2):
                        dve.wait_ge(product_done, 2 * j + h + 1)
                        dve.scalar_tensor_tensor(out=y[:c, sl, 512 * h:512 * h + 512], in0=res[:c, sl, 512 * h:512 * h + 512], scalar=ALPHA,
                                                 in1=ps[:c, (2 * j + h) % BANKS, :], op0=ALU.mult, op1=ALU.add).then_inc(added, 1)
                    dve.wait_ge(added, 2 * j + 2)
                    dve.bn_stats(stats[:c, sl, 0:6], y[:c, sl, 0:512]).then_inc(stats_done, 1)
                    dve.bn_stats(stats[:c, sl, 6:12], y[:c, sl, 512:1024]).then_inc(stats_done, 1)
                    dve.wait_ge(stats_done, 2 * j + 2)
                    if j >= 2:
                        dve.wait_ge(std_done, j - 1)
                    dve.bn_aggr(mv[:c, sl, :], stats[:c, sl, :]).then_inc(var_done, 1)
                    dve.wait_ge(std_done, j + 1)
                    dve.reciprocal(rstd[:c, sl, :], rstd[:c, sl, :]).then_inc(rstd_done, 1)
                    dve.wait_ge(rstd_done, j + 1)
                    dve.tensor_scalar(y[:c, sl, :], y[:c, sl, :], mv[:c, sl, 0:1], rstd[:c, sl, :], ALU.subtract, ALU.mult).then_inc(centred, 1)
                    dve.wait_ge(centred, j + 1)
                    dve.wait_ge(consts_in, 32)
                    dve.tensor_tensor(y[:c, sl, :], y[:c, sl, :], g_b[:c, :], ALU.mult).then_inc(scaled, 1)

        @block.gpsimd
        def _(pool):
            pool.wait_ge(consts_in, 32)
            for what, *a in order:
                if what == "tile":
                    g, (j, o, c) = a
                    t = GROUPS[g][0] + o
                    pool.wait_ge(scaled, j + 1)
                    pool.tensor_tensor(y[:c, j % 2, :], y[:c, j % 2, :], b_b[:c, :], ALU.add).then_inc(normed, 1)
                    pool.wait_ge(normed, j + 1)
                    pool.dma_start(x1_dram[t:t + c, :], y[:c, j % 2, :]).then_inc(y_out[j % 2], 16)
            for q in range(2):
                pool.wait_ge(y_out[q], 16 * len([j for j in range(n) if j % 2 == q]))

        @block.tensor
        def _(pe):
            def product(g, t, h, k):
                j, o, c = t
                return split_product(pe, ps[:c, (2 * j + h) % BANKS, :], mh[:, g % 2, k, o:o + c], ml[:, g % 2, k, o:o + c],
                                     wh[:, k, 512 * h:512 * h + 512], wl[:, k, 512 * h:512 * h + 512], k == 0, k == KT - 1)

            for what, *a in order:
                if what == "first":
                    for k in range(KT):
                        pe.wait_ge(wlo_done, k + 1)
                        pe.wait_ge(mlo_done, k + 1)
                        for t in gtiles[0][:BANKS // 2]:
                            for h in range(2):
                                mm = product(0, t, h, k)
                                if k == KT - 1:
                                    mm.then_inc(product_done, 1)
                elif what == "tile" and 2 * a[1][0] >= BANKS:
                    g, t = a
                    pe.wait_ge(mlo_done, KT * (g + 1))
                    for h in range(2):
                        pe.wait_ge(added, 2 * t[0] + h - BANKS + 1)
                        for k in range(KT):
                            mm = product(g, t, h, k)
                        mm.then_inc(product_done, 1)


def phase_ffn(nc, x1_dram, w_up, w_down, ln_g, ln_b, ident_in, y_tile, lasting):
    NF = 8
    NC = D_FF // P // NF
    WRING, WSTG = 3, 2
    MT = 5
    s = Scope(nc, "p5")
    with s:
        ident = s.sb("ident", [P, P])
        g_b = s.sb("g_b", [P, D])
        b_b = s.sb("b_b", [P, D])
        eps = s.sb("eps", [P, 1])
        xh = s.sb("xh", [P, KT, NMAX], F32R)
        xl = s.sb("xl", [P, KT, NMAX], F32R)
        res = s.sb("res", [P, 2, MT, D])
        hh = s.sb("hh", [P, NF + 2, NMAX], F32R)
        hl = s.sb("hl", [P, NF + 2, NMAX], F32R)
        r = s.sb("r", [P, 2, 512])
        wst = s.sb("wst", [P, WSTG, 2048])
        wh = s.sb("wh", [P, WRING, 2048], F32R)
        wl = s.sb("wl", [P, WRING, 2048], F32R)
        stats = s.sb("stats", [P, 2, 12])
        mv = s.sb("mv", [P, 2, 2])
        rstd = s.sb("rstd", [P, 2, 1])
        ps_d = s.ps("ps_d", [P, MT, 512])
        ps_u = s.ps("ps_u", [P, 2, 512])
        ps_t = s.ps("ps_t", [P, 512])

        ident_loaded, rows_in = s.sem("ident_loaded"), s.sem("rows_in")
        eps_set = s.sem("eps_set")
        res_in = s.sems("res_in", MT)
        y_out = lasting.rows
        turned, xhi_done, xlo_done = s.sem("turned"), s.sem("xhi_done"), s.sem("xlo_done")
        w_loaded = s.sems("w_loaded", WSTG)
        whi_done, wlo_done = s.sem("whi_done"), s.sem("wlo_done")
        products = s.sem("products")
        relu_done, sq_done, hfull_done, hlo_done = s.sem("relu_done"), s.sem("sq_done"), s.sem("hfull_done"), s.sem("hlo_done")
        summed = s.sem("summed")
        stats_done, var_done, std_done = s.sem("stats_done"), s.sem("var_done"), s.sem("std_done")
        rstd_done, centred, scaled, normed = s.sem("rstd_done"), s.sem("centred"), s.sem("scaled"), s.sem("normed")

        gtiles, n = [], 0
        for (t0, cnt) in GROUPS:
            gtiles.append([(n + i, o, c) for i, (o, c) in enumerate(subtiles(t0, cnt, P))])
            n += len(gtiles[-1])

        work, nw, wunits = [], 0, []
        for g in range(len(GROUPS)):
            steps = [("up", 0, 0)]
            for c in range(NC):
                steps += [("up", c, p) for p in range(1, NF // 2)]
                if c + 1 < NC:
                    steps.append(("up", c + 1, 0))
                steps += [("down", c, 0), ("down", c, 1)]
            for kind, c, p in steps:
                k = 1 if kind == "up" else 2
                for q in range(k):
                    wunits.append((kind, c, p, q))
                work.append((kind, g, c, p, nw, k))
                nw += k
        order, next_w = [], 0
        order += [("turn", 0, t) for t in gtiles[0]]
        pending_ln = []
        for kind, g, c, p, w0, k in work:
            while next_w < min(nw, w0 + k + 2):
                order.append(("w", next_w))
                next_w += 1
            order.append((kind, g, c, p, w0))
            if kind == "down" and c == NC - 1 and p == 1:
                pending_ln = [("ln", g, t) for t in gtiles[g]]
                if g == len(GROUPS) - 1:
                    for ln in pending_ln:
                        order += [("sum", *ln[1:]), ln]
            elif pending_ln and kind == "up":
                order.append(pending_ln.pop(0))
            if kind == "down" and c == NC - 1 and p == 0 and g + 1 < len(GROUPS):
                order += [("turn", g + 1, t) for t in gtiles[g + 1]]

        mark, up_index, down_index, unit_used = {}, {}, {}, {}
        n_mark = n_up = n_down = n_ln = 0
        last_up, last_down, ln_index = {}, {}, {}
        for what, *a in order:
            if what == "up":
                g, c, p, w0 = a
                for f in (2 * p, 2 * p + 1):
                    for o, cc in moving(GROUPS[g][1]):
                        n_mark += 1
                        mark[("up", n_up)] = n_mark
                        up_index[(g, c, f, o)] = n_up
                        n_up += 1
                unit_used[w0] = n_mark
                last_up[g] = n_mark
                last_up[(g, c)] = n_up
            elif what == "down":
                g, c, h, w0 = a
                n_mark += 1
                unit_used[w0] = n_mark
                for i in range(len(gtiles[g])):
                    n_mark += 1
                    mark[("down", n_down)] = n_mark
                    down_index[(g, c, h, i)] = n_down
                    n_down += 1
                unit_used[w0 + 1] = n_mark
                last_down[(g, c)] = n_mark
            elif what == "ln":
                ln_index[(a[0], a[1][0])] = n_ln
                n_ln += 1

        bank_before, in_bank = {}, {}
        for (g, c, h, ti), i in down_index.items():
            bank_before[i] = in_bank.get(ti)
            in_bank[ti] = i

        LAST = (len(GROUPS) - 1, NC - 1, 1)

        def slot_of(c, f):
            return (NF + f if c % 2 else f) if f < 2 else f

        def prev_reader(g, c, f):
            gc = g * NC + c - (2 if f < 2 else 1)
            return last_down.get(divmod(gc, NC)) if gc >= 0 else None

        block = s.stack.enter_context(nc.Block())

        @block.sync
        def _(sp):
            sp.dma_start(ident[:], ident_in).then_inc(ident_loaded, 16)

            def load_res(g):
                for i, (j, o, c) in enumerate(gtiles[g]):
                    t = GROUPS[g][0] + o
                    stored = len([q for q in gtiles[:max(0, g - 1)] if len(q) > i])
                    if stored:
                        sp.wait_ge(y_out[i], 16 * stored)
                    sp.dma_start(res[:c, g % 2, i, :], x1_dram[t:t + c, :]).then_inc(res_in[i], 16)

            load_res(0)
            for what, *a in order:
                if what == "w":
                    u = a[0]
                    if u == 3:
                        load_row_broadcast(sp, g_b[:], ln_g, rows_in)
                        load_row_broadcast(sp, b_b[:], ln_b, rows_in)
                    if u >= WSTG:
                        sp.wait_ge(wlo_done, u - WSTG + 1)
                    kind, c, p, q = wunits[u]
                    if kind == "up":
                        c0 = (c * NF + 2 * p) * P
                        sp.dma_start(wst[:, u % WSTG, :].rearrange("p (k f) -> p k f", k=KT),
                                     w_up.rearrange("(k p) f -> p k f", p=P)[:, :, c0:c0 + 2 * P]).then_inc(w_loaded[u % WSTG], 16)
                    else:
                        r0 = c * NF + 4 * q
                        sp.dma_start(wst[:, u % WSTG, :].rearrange("p (f n) -> p f n", f=4),
                                     w_down.rearrange("(f p) n -> p f n", p=P)[:, r0:r0 + 4, 512 * p:512 * p + 512]).then_inc(w_loaded[u % WSTG], 16)
                elif what == "down" and a[1] == 1 and a[2] == 1 and a[0] + 1 < len(GROUPS):
                    load_res(a[0] + 1)

        @block.scalar
        def _(act):
            for what, *a in order:
                if what == "w":
                    u = a[0]
                    act.wait_ge(w_loaded[u % WSTG], 16 * (u // WSTG + 1))
                    if u >= WRING:
                        act.wait_ge(products, unit_used[u - WRING])
                    act.activation(wh[:, u % WRING, :], wst[:, u % WSTG, :], ACT.Copy).then_inc(whi_done, 1)
                elif what == "turn":
                    g, (j, o, c) = a
                    for q in range(2):
                        act.wait_ge(turned, 2 * j + q + 1)
                        if g >= 1:
                            act.wait_ge(products, last_up[g - 1])
                        act.activation(xh[:, 4 * q:4 * q + 4, o:o + c], ps_t[:, :].rearrange("p (k t) -> p k t", k=4)[:, :, :c],
                                       ACT.Copy).then_inc(xhi_done, 1)
                elif what == "up":
                    g, c, p, w0 = a
                    for f in (2 * p, 2 * p + 1):
                        for o, cc in moving(GROUPS[g][1]):
                            i = up_index[(g, c, f, o)]
                            act.wait_ge(products, mark[("up", i)])
                            if i >= 2:
                                act.wait_ge(hlo_done, i - 1)
                            act.activation(r[:, i % 2, :cc], ps_u[:, i % 2, :cc], ACT.Relu).then_inc(relu_done, 1)
                            act.wait_ge(hfull_done, i + 1)
                            before = prev_reader(g, c, f)
                            if before:
                                act.wait_ge(products, before)
                            act.activation(hh[:, slot_of(c, f), o:o + cc], r[:, i % 2, :cc], ACT.Copy).then_inc(sq_done, 1)
                elif what == "ln":
                    g, (j, o, c) = a
                    i = ln_index[(g, j)]
                    act.wait_ge(eps_set, 1)
                    act.wait_ge(var_done, i + 1)
                    if i >= 2:
                        act.wait_ge(centred, i - 1)
                    act.activation(rstd[:c, i % 2, :], mv[:c, i % 2, 1:2], ACT.Sqrt, bias=eps[:c, :]).then_inc(std_done, 1)

        @block.vector
        def _(dve):
            def add_product(g, c, h, ti):
                i, cc = down_index[(g, c, h, ti)], gtiles[g][ti][2]
                dve.wait_ge(products, mark[("down", i)])
                if i >= 1:
                    dve.wait_ge(summed, i)
                acc = res[:cc, g % 2, ti, 512 * h:512 * h + 512]
                dve.scalar_tensor_tensor(out=acc, in0=acc, scalar=ALPHA if c == 0 else 1.0, in1=ps_d[:cc, ti, :],
                                         op0=ALU.mult, op1=ALU.add).then_inc(summed, 1)

            dve.memset(eps[:], LN_EPS).then_inc(eps_set, 1)
            for what, *a in order:
                if what == "w":
                    u = a[0]
                    dve.wait_ge(whi_done, u + 1)
                    dve.tensor_tensor(wl[:, u % WRING, :], wst[:, u % WSTG, :], wh[:, u % WRING, :].bitcast(F32), ALU.subtract).then_inc(wlo_done, 1)
                elif what == "turn":
                    g, (j, o, c) = a
                    for q in range(2):
                        dve.wait_ge(xhi_done, 2 * j + q + 1)
                        dve.tensor_tensor(xl[:, 4 * q:4 * q + 4, o:o + c], ps_t[:, :].rearrange("p (k t) -> p k t", k=4)[:, :, :c],
                                          xh[:, 4 * q:4 * q + 4, o:o + c].bitcast(F32), ALU.subtract).then_inc(xlo_done, 1)
                elif what == "up":
                    g, c, p, w0 = a
                    for f in (2 * p, 2 * p + 1):
                        for o, cc in moving(GROUPS[g][1]):
                            i = up_index[(g, c, f, o)]
                            dve.wait_ge(relu_done, i + 1)
                            dve.scalar_tensor_tensor(out=r[:, i % 2, :cc], in0=ps_u[:, i % 2, :cc], scalar=0.0, in1=r[:, i % 2, :cc],
                                                     op0=ALU.max, op1=ALU.mult).then_inc(hfull_done, 1)
                            dve.wait_ge(sq_done, i + 1)
                            dve.tensor_tensor(hl[:, slot_of(c, f), o:o + cc], r[:, i % 2, :cc], hh[:, slot_of(c, f), o:o + cc].bitcast(F32),
                                              ALU.subtract).then_inc(hlo_done, 1)
                elif what == "down":
                    g, c, h, w0 = a
                    if (g, c, h) != LAST:
                        for ti in range(len(gtiles[g])):
                            add_product(g, c, h, ti)
                elif what == "sum":
                    g, t = a
                    add_product(*LAST, gtiles[g].index(t))
                elif what == "ln":
                    g, (j, o, c) = a
                    i = ln_index[(g, j)]
                    sl, ti = i % 2, gtiles[g].index((j, o, c))
                    acc = res[:c, g % 2, ti, :]
                    dve.wait_ge(summed, down_index[(g, NC - 1, 1, ti)] + 1)
                    dve.bn_stats(stats[:c, sl, 0:6], acc[:, 0:512]).then_inc(stats_done, 1)
                    dve.bn_stats(stats[:c, sl, 6:12], acc[:, 512:1024]).then_inc(stats_done, 1)
                    dve.wait_ge(stats_done, 2 * i + 2)
                    if i >= 2:
                        dve.wait_ge(std_done, i - 1)
                    dve.bn_aggr(mv[:c, sl, :], stats[:c, sl, :]).then_inc(var_done, 1)
                    dve.wait_ge(std_done, i + 1)
                    dve.reciprocal(rstd[:c, sl, :], rstd[:c, sl, :]).then_inc(rstd_done, 1)
                    dve.wait_ge(rstd_done, i + 1)
                    dve.tensor_scalar(acc, acc, mv[:c, sl, 0:1], rstd[:c, sl, :], ALU.subtract, ALU.mult).then_inc(centred, 1)
                    dve.wait_ge(centred, i + 1)
                    dve.wait_ge(rows_in, 32)
                    dve.tensor_tensor(acc, acc, g_b[:c, :], ALU.mult).then_inc(scaled, 1)

        @block.gpsimd
        def _(pool):
            pool.wait_ge(rows_in, 32)
            for what, *a in order:
                if what == "ln":
                    g, (j, o, c) = a
                    i, ti = ln_index[(g, j)], gtiles[g].index((j, o, c))
                    pool.wait_ge(scaled, i + 1)
                    pool.tensor_tensor(res[:c, g % 2, ti, :], res[:c, g % 2, ti, :], b_b[:c, :], ALU.add).then_inc(normed, 1)
                    pool.wait_ge(normed, i + 1)
                    pool.dma_start(y_tile(j), res[:c, g % 2, ti, :]).then_inc(y_out[ti], 16)
            for ti in range(MT):
                pool.wait_ge(y_out[ti], 16 * len([g for g in gtiles if len(g) > ti]))

        @block.tensor
        def _(pe):
            pe.wait_ge(ident_loaded, 16)
            for what, *a in order:
                if what == "turn":
                    g, (j, o, c) = a
                    ti = gtiles[g].index((j, o, c))
                    pe.wait_ge(res_in[ti], 16 * len([q for q in gtiles[:g + 1] if len(q) > ti]))
                    for q in range(2):
                        if 2 * j + q >= 1:
                            pe.wait_ge(xlo_done, 2 * j + q)
                        for k in range(4):
                            mm = pe.transpose(ps_t[:, k * P:k * P + c], res[:c, g % 2, ti, (4 * q + k) * P:(4 * q + k + 1) * P], ident[:c, :c])
                        mm.then_inc(turned, 1)
                elif what == "up":
                    g, c, p, w0 = a
                    pe.wait_ge(xlo_done, 2 * (gtiles[g][-1][0] + 1))
                    pe.wait_ge(wlo_done, w0 + 1)
                    for f in (2 * p, 2 * p + 1):
                        for o, cc in moving(GROUPS[g][1]):
                            i = up_index[(g, c, f, o)]
                            if i >= 2:
                                pe.wait_ge(hfull_done, i - 1)
                            for k in range(KT):
                                col = slice(256 * k + P * (f - 2 * p), 256 * k + P * (f - 2 * p) + P)
                                mm = split_product(pe, ps_u[:, i % 2, :cc], wh[:, w0 % WRING, col], wl[:, w0 % WRING, col],
                                                   xh[:, k, o:o + cc], xl[:, k, o:o + cc], k == 0, k == KT - 1)
                            mm.then_inc(products, 1)
                elif what == "down":
                    g, c, h, w0 = a
                    pe.wait_ge(hlo_done, last_up[(g, c)])
                    tile_nos = range(len(gtiles[g]))
                    if (g, c, h) == LAST:
                        steps = [(f, ti) for ti in tile_nos for f in range(NF)]
                    else:
                        steps = [(f, ti) for f in range(NF) for ti in tile_nos]
                    first_half = [x for x in steps if x[0] == 3][0 if (g, c, h) == LAST else -1]
                    for f, ti in steps:
                        j, o, cc = gtiles[g][ti]
                        w, sl = w0 + f // 4, slot_of(c, f)
                        pe.wait_ge(wlo_done, w + 1)
                        row = slice(512 * (f % 4), 512 * (f % 4) + 512)
                        i = down_index[(g, c, h, ti)]
                        if f == 0 and bank_before[i] is not None:
                            pe.wait_ge(summed, bank_before[i] + 1)
                        mm = split_product(pe, ps_d[:cc, ti, :], hh[:, sl, o:o + cc], hl[:, sl, o:o + cc],
                                           wh[:, w % WRING, row], wl[:, w % WRING, row], f == 0, f == NF - 1)
                        if f == NF - 1 or (f, ti) == first_half:
                            mm.then_inc(products, 1)


def build_program(nc, a):
    def dram(name, shape):
        return nc.dram_tensor(name, shape, F32, kind="Internal").ap()

    xn_dram = dram("xn_scratch", (T, D))
    zt_dram = dram("zt_scratch", (Z_ROWS, T))
    gv_dram = dram("gv_scratch", (T, 512))
    mixt_dram = dram("mixt_scratch", (D, T))
    x1_dram = dram("x1_scratch", (T, D))
    x_p, x_s = a["x_prompt"][0], a["x_sample"][0]
    k_p = a["new_sb_k_p"][0, 0].rearrange("t h d -> t (h d)")
    v_p = a["new_sb_v_p"][0, 0].rearrange("t h d -> t (h d)")
    k_s = a["new_sb_k_s"][0, 0].rearrange("t h d -> t (h d)")
    v_s = a["new_sb_v_s"][0, 0].rearrange("t h d -> t (h d)")

    def x_tile(j):
        t, c = TILES[j]
        return x_p[t:t + c, :] if t < SEQ else x_s[t - SEQ:t - SEQ + c, :]

    def y_tile(j):
        t, c = TILES[j]
        return a["y_prompt"][0][t:t + c, :] if t < SEQ else a["y_sample"][0][t - SEQ:t - SEQ + c, :]

    def token_stores(what, t, n):
        if what == "gv":
            return [(gv_dram[t:t + n, :], 0, 512)]
        if t < SEQ:
            return [(k_p[t:t + n, :], 0, 256), (v_p[t:t + n, :], 256, 512)]
        return [(k_s[t - SEQ:t - SEQ + n, :], 0, 256), (v_s[t - SEQ:t - SEQ + n, :], 256, 512)]

    lasting = OutputStores(nc)
    with lasting.scope.stack:
        phase_in(nc, x_tile, a["ln_in_g"], a["ln_in_b"], a["w_in"][0], a["ident"], xn_dram, zt_dram, token_stores, lasting)
        phase_gla(nc, a, zt_dram, gv_dram, mixt_dram, lasting)
        phase_sb(nc, a, zt_dram, mixt_dram, k_p, v_p, k_s, v_s)
        phase_out(nc, mixt_dram, a["w_out"][0], a["ln1_g"][0], a["ln1_b"][0], xn_dram, x1_dram)
        phase_ffn(nc, x1_dram, a["w_up"][0], a["w_down"][0], a["ln2_g"][0], a["ln2_b"][0], a["ident"], y_tile, lasting)


OUTPUTS = {
    "y_prompt": (1, SEQ, D),
    "y_sample": (1, DEC, D),
    "new_sb_k_p": (1, 1, SEQ, SBH, SBD),
    "new_sb_v_p": (1, 1, SEQ, SBH, SBD),
    "gla_state_p": (1, 1, HEADS, DK, DV),
    "conv_state_p": (1, 1, 2, CONV_CH),
    "new_sb_k_s": (1, 1, DEC, SBH, SBD),
    "new_sb_v_s": (1, 1, DEC, SBH, SBD),
    "gla_state_s": (1, 1, HEADS, DK, DV),
    "conv_state_s": (1, 1, 2, CONV_CH),
}


def shape_constants():
    ident = np.eye(P, dtype=np.float32)
    s_, t_ = np.arange(P)[:, None], np.arange(P)[None, :]
    level_masks = []
    for hs in LEVELS:
        second = np.array([t for t in range(P) if (t // hs) % 2 == 1])[None, :]
        level_masks.append(((s_ // (2 * hs) == second // (2 * hs)) & ((s_ // hs) % 2 == 0)).astype(np.float32))
    level_masks.append((s_ == t_).astype(np.float32))
    chunk_start = np.ones((P, T), np.float32)
    chunk_start[:, ::CHUNK] = 0.0
    causal = np.where(t_ < s_, 0.0, MASKED).astype(np.float32)
    return {
        "ident": ident,
        "level_masks": np.concatenate(level_masks, axis=1),
        "chunk_start": chunk_start,
        "causal": causal,
        "ones": np.ones((P, P), np.float32),
    }


LEVELS = (32, 16, 8, 4, 2, 1)


def kernel(**inputs):
    import concourse.bacc as bacc
    from concourse.bass_utils import run_bass_kernel_spmd

    nc = bacc.Bacc("TRN2", target_bir_lowering=False, num_devices=1)
    arrays, aps = {}, {}
    for name, value in {**inputs, **shape_constants()}.items():
        value = np.ascontiguousarray(value)
        arrays[f"in_{name}"] = value
        aps[name] = nc.dram_tensor(f"in_{name}", value.shape, mybir.dt.from_np(value.dtype), kind="ExternalInput").ap()
    for name, shape in OUTPUTS.items():
        aps[name] = nc.dram_tensor(f"out_{name}", shape, F32, kind="ExternalOutput").ap()
    build_program(nc, aps)
    r = run_bass_kernel_spmd(nc, [arrays], core_ids=[0])
    return tuple(r.results[0][f"out_{name}"] for name in OUTPUTS)
```
